# Optimizing a Trainium2 kernel written in Bass

```python
import math
import jax, jax.numpy as jnp
from jax import lax
import numpy as np

D_MODEL = 2048
BATCH = 1
SEQ = 256
DEPTH = 1
DEC_BATCH = 8
DEC_SEQ = 1
PAST_LEN = 2048
PAGE_SIZE = 128

MIX_WIDTH = D_MODEL
RW_WIDTH = MIX_WIDTH // 2
RW_HEAD = 64
RW_HEADS = RW_WIDTH // RW_HEAD
RW_LORA_W = 64
RW_LORA_A = 64
RW_LORA_G = 160
RW_COLS = 3 * RW_WIDTH + RW_LORA_W + RW_LORA_A + RW_LORA_G
RW_SPLITS = (RW_WIDTH, 2 * RW_WIDTH, 3 * RW_WIDTH, 3 * RW_WIDTH + RW_LORA_W, 3 * RW_WIDTH + RW_LORA_W + RW_LORA_A)
RW_LNX_EPS = 64e-5

NSA_WIDTH = MIX_WIDTH - RW_WIDTH
NSA_DK = 64
NSA_HEADS = NSA_WIDTH // NSA_DK
NSA_KV_HEADS = 4
NSA_GROUP = NSA_HEADS // NSA_KV_HEADS
NSA_KV = NSA_KV_HEADS * NSA_DK
CMP_STRIDE = 16
CMP_BLOCK = 2 * CMP_STRIDE
CMP_HID = 128
SLC_BLOCK = 64
SLC_RATIO = SLC_BLOCK // CMP_STRIDE
N_SEL = 16
WINDOW = 512
NSA_QBLK = 64
NSA_SPLITS = tuple(NSA_WIDTH + i * NSA_KV for i in range(7))
NSA_COLS = NSA_WIDTH + 6 * NSA_KV + 3 * NSA_HEADS
IN_COLS = RW_COLS + NSA_COLS

MEM_TOKENS = 256
X_HEADS = 4
X_HEAD_DIM = 128
X_WIDTH = X_HEADS * X_HEAD_DIM

PEER_HEADS = 8
PEER_KEYS = 128
PEER_EXPERTS = PEER_KEYS * PEER_KEYS
PEER_QDIM = 256
PEER_HALF = PEER_QDIM // 2
PEER_TOPK = 16
PEER_TOKBLK = 64

RMS_EPS = 1e-6
NEG_BIG = -1e30
POS_BIG = 1e30

kernel_name = 'hybrid_rwkv7_nsa_peer_step'

def rmsnorm(x, g):
    xf = x.astype(jnp.float32)
    y = xf * lax.rsqrt(jnp.mean(xf * xf, axis=-1, keepdims=True) + RMS_EPS)
    return (y * g.astype(jnp.float32)).astype(x.dtype)

def masked_softmax(s, mask, axis):
    s = jnp.where(mask, s.astype(jnp.float32), NEG_BIG)
    p = jax.nn.softmax(s, axis=axis)
    return jnp.where(mask, p, 0.0)

def rwkv7_mix(u, prev_row, wkv0, rw_mu, rw_w0, rw_w2, rw_a0, rw_a2, rw_g2, rw_k_k, rw_k_a, rw_r_k, rw_lnx_g, rw_lnx_b):
    B, S = u.shape[0], u.shape[1]
    H, N = RW_HEADS, RW_HEAD
    prev = jnp.concatenate([prev_row[:, None, :].astype(u.dtype), u[:, :-1]], axis=1)
    us = u + (prev - u) * rw_mu
    r, k, v, wd, ad, gd = jnp.split(us, RW_SPLITS, axis=-1)
    w_log = -jax.nn.softplus(-(rw_w0 + jnp.tanh(wd) @ rw_w2)) - 0.5
    decay = jnp.exp(-jnp.exp(w_log.astype(jnp.float32)))
    a = jax.nn.sigmoid(rw_a0 + ad @ rw_a2)
    g = jax.nn.sigmoid(gd) @ rw_g2
    kk = (k * rw_k_k).reshape(B, S, H, N).astype(jnp.float32)
    kk = kk * lax.rsqrt(jnp.maximum(jnp.sum(kk * kk, axis=-1, keepdims=True), 1e-24))
    k = k * (1.0 + (a - 1.0) * rw_k_a)
    heads = lambda z: z.reshape(B, S, H, N).astype(jnp.float32)
    r_h, k_h, v_h, a_h, w_h = heads(r), heads(k), heads(v), heads(a), heads(decay)
    b_h = kk * a_h

    def step(st, inp):
        r_t, w_t, k_t, v_t, kk_t, b_t = inp
        sa = jnp.einsum('bhij,bhj->bhi', st, -kk_t)
        st = st * w_t[:, :, None, :] + sa[..., None] * b_t[:, :, None, :] + v_t[..., None] * k_t[:, :, None, :]
        return st, jnp.einsum('bhij,bhj->bhi', st, r_t)

    seq_first = lambda z: jnp.swapaxes(z, 0, 1)
    wkv_new, y = lax.scan(step, wkv0.astype(jnp.float32),
                          (seq_first(r_h), seq_first(w_h), seq_first(k_h), seq_first(v_h), seq_first(kk), seq_first(b_h)))
    y = seq_first(y)
    mu = jnp.mean(y, axis=-1, keepdims=True)
    var = jnp.mean(jnp.square(y - mu), axis=-1, keepdims=True)
    y = ((y - mu) * lax.rsqrt(var + RW_LNX_EPS)).reshape(B, S, RW_WIDTH) * rw_lnx_g + rw_lnx_b
    bonus = jnp.sum(r_h * k_h * rw_r_k, axis=-1, keepdims=True) * v_h
    out = (y + bonus.reshape(B, S, RW_WIDTH)) * g
    return out.astype(u.dtype), u[:, -1], wkv_new.astype(wkv0.dtype)

def nsa_compress(kraw, w1, b1, w2):
    B, L = kraw.shape[0], kraw.shape[1]
    nch = L // CMP_STRIDE
    ch = kraw[:, :nch * CMP_STRIDE].reshape(B, nch, CMP_STRIDE, NSA_KV_HEADS, NSA_DK)
    h_lo = jnp.einsum('bclkd,ldh->bckh', ch, w1[:CMP_STRIDE])
    h_hi = jnp.einsum('bclkd,ldh->bckh', ch, w1[CMP_STRIDE:])
    h = jax.nn.gelu(h_lo[:, :-1] + h_hi[:, 1:] + b1)
    return jnp.einsum('bckh,hd->bckd', h, w2)

def nsa_attend(q, gates, kc, vc, ks, vs, kw, vw, pos0, cmp_w1, cmp_b1, cmp_w2):
    B, S = q.shape[0], q.shape[1]
    L = kc.shape[1]
    KH, G, DK = NSA_KV_HEADS, NSA_GROUP, NSA_DK
    kcb = nsa_compress(kc, cmp_w1[0], cmp_b1[0], cmp_w2[0])
    vcb = nsa_compress(vc, cmp_w1[1], cmp_b1[1], cmp_w2[1])
    nc = kcb.shape[1]
    cmp_end = jnp.arange(nc) * CMP_STRIDE + (CMP_BLOCK - 1)
    nsb = -(-L // SLC_BLOCK)
    pad_rows = ((0, 0), (0, nsb * SLC_BLOCK - L), (0, 0), (0, 0))
    to_blocks = lambda z: jnp.pad(z, pad_rows).reshape(B, nsb, SLC_BLOCK, KH, DK).transpose(0, 3, 1, 2, 4)
    ksb, vsb = to_blocks(ks), to_blocks(vs)
    n_sel = min(N_SEL, nsb)
    qb = math.gcd(S, NSA_QBLK)
    qg = q.reshape(B, S, KH, G, DK) * (DK ** -0.5)
    gg = gates.reshape(B, S, KH, G, 3)
    blk_j = jnp.arange(nsb)
    b_idx = jnp.arange(B)[:, None, None, None]
    h_idx = jnp.arange(KH)[None, :, None, None]

    def one_block(i):
        qs = i * qb
        qi = lax.dynamic_slice_in_dim(qg, qs, qb, axis=1)
        gi = lax.dynamic_slice_in_dim(gg, qs, qb, axis=1)
        t = pos0 + qs + jnp.arange(qb)
        p_c = masked_softmax(jnp.einsum('bqkgd,bckd->bkgqc', qi, kcb), cmp_end[None, :] <= t[:, None], -1)
        o_c = jnp.einsum('bkgqc,bckd->bqkgd', p_c.astype(vcb.dtype), vcb)
        imp = jnp.pad(p_c.sum(axis=2), ((0, 0), (0, 0), (0, 0), (1, SLC_RATIO * nsb - nc)))
        quad = imp[..., :SLC_RATIO * nsb].reshape(B, KH, qb, nsb, SLC_RATIO)
        imp_s = 0.5 * quad[..., 0] + quad[..., 1:].sum(axis=-1) + 0.5 * imp[..., SLC_RATIO::SLC_RATIO]
        tb = (t // SLC_BLOCK)[:, None]
        forced = (blk_j == 0) | (blk_j == tb) | (blk_j == tb - 1)
        imp_s = jnp.where(forced, POS_BIG, jnp.where(blk_j <= tb, imp_s, NEG_BIG))
        _, sel = lax.top_k(imp_s, n_sel)
        ks_g = ksb[b_idx, h_idx, sel]
        vs_g = vsb[b_idx, h_idx, sel]
        kpos = sel[..., None] * SLC_BLOCK + jnp.arange(SLC_BLOCK)
        m_s = (kpos <= t[:, None, None])[:, :, None]
        p_s = masked_softmax(jnp.einsum('bqkgd,bkqnld->bkgqnl', qi, ks_g), m_s, (-2, -1))
        o_s = jnp.einsum('bkgqnl,bkqnld->bqkgd', p_s.astype(vs_g.dtype), vs_g)
        kwi = lax.dynamic_slice_in_dim(kw, qs, WINDOW + qb, axis=1)
        vwi = lax.dynamic_slice_in_dim(vw, qs, WINDOW + qb, axis=1)
        wpos = pos0 - WINDOW + qs + jnp.arange(WINDOW + qb)
        dlt = t[:, None] - wpos[None, :]
        m_w = (wpos[None, :] >= 0) & (dlt >= 0) & (dlt < WINDOW)
        p_w = masked_softmax(jnp.einsum('bqkgd,bwkd->bkgqw', qi, kwi), m_w, -1)
        o_w = jnp.einsum('bkgqw,bwkd->bqkgd', p_w.astype(vwi.dtype), vwi)
        return gi[..., 0:1] * o_c + gi[..., 1:2] * o_s + gi[..., 2:3] * o_w

    out = lax.map(one_block, jnp.arange(S // qb))
    return jnp.swapaxes(out, 0, 1).reshape(B, S, NSA_WIDTH)

def peer_ffn(h, peer_wq, peer_sub_keys, peer_u, peer_v):
    B, S, D = h.shape
    n = B * S
    hf = h.reshape(n, D)
    q = (hf @ peer_wq).reshape(n, PEER_HEADS, 2, PEER_HALF)
    s = jnp.einsum('nhcd,hckd->nhck', q, peer_sub_keys).astype(jnp.float32)
    sv, si = lax.top_k(s, PEER_TOPK)
    cand = (sv[:, :, 0, :, None] + sv[:, :, 1, None, :]).reshape(n, PEER_HEADS, PEER_TOPK * PEER_TOPK)
    cv, ci = lax.top_k(cand, PEER_TOPK)
    e_idx = (jnp.take_along_axis(si[:, :, 0], ci // PEER_TOPK, axis=-1) * PEER_KEYS
             + jnp.take_along_axis(si[:, :, 1], ci % PEER_TOPK, axis=-1))
    gate = jax.nn.softmax(cv, axis=-1).astype(h.dtype)
    tb = math.gcd(n, PEER_TOKBLK)

    def one_block(i):
        xs = lax.dynamic_slice_in_dim(hf, i * tb, tb, axis=0)
        ei = lax.dynamic_slice_in_dim(e_idx, i * tb, tb, axis=0)
        gi = lax.dynamic_slice_in_dim(gate, i * tb, tb, axis=0)
        act = jax.nn.gelu(jnp.einsum('td,thkd->thk', xs, peer_u[ei]))
        return jnp.einsum('thk,thkd->td', gi * act, peer_v[ei])

    return lax.map(one_block, jnp.arange(n // tb)).reshape(B, S, D)

def hybrid_layer(x, mem_k, mem_v, rw_prev, wkv0, kc_past, vc_past, ks_past, vs_past, kw_past, vw_past, pos0, p):
    B, S = x.shape[0], x.shape[1]
    h = rmsnorm(x, p['norm_mix_g'])
    u = h @ p['w_in']
    o_rw, shift_new, wkv_new = rwkv7_mix(u[..., :RW_COLS], rw_prev, wkv0, p['rw_mu'], p['rw_w0'], p['rw_w2'],
                                         p['rw_a0'], p['rw_a2'], p['rw_g2'], p['rw_k_k'], p['rw_k_a'],
                                         p['rw_r_k'], p['rw_lnx_g'], p['rw_lnx_b'])
    q, kc, vc, ks, vs, kw, vw, gl = jnp.split(u[..., RW_COLS:], NSA_SPLITS, axis=-1)
    kvh = lambda z: z.reshape(B, S, NSA_KV_HEADS, NSA_DK)
    kc, vc, ks, vs, kw, vw = kvh(kc), kvh(vc), kvh(ks), kvh(vs), kvh(kw), kvh(vw)
    gates = jax.nn.sigmoid(gl).reshape(B, S, NSA_HEADS, 3)
    o_nsa = nsa_attend(q.reshape(B, S, NSA_HEADS, NSA_DK), gates,
                       jnp.concatenate([kc_past, kc], axis=1), jnp.concatenate([vc_past, vc], axis=1),
                       jnp.concatenate([ks_past, ks], axis=1), jnp.concatenate([vs_past, vs], axis=1),
                       jnp.concatenate([kw_past, kw], axis=1), jnp.concatenate([vw_past, vw], axis=1),
                       pos0, p['cmp_w1'], p['cmp_b1'], p['cmp_w2'])
    o_nsa = rmsnorm(o_nsa, p['nsa_norm_g'])
    x = x + jnp.concatenate([o_rw, o_nsa.astype(o_rw.dtype)], axis=-1) @ p['w_out']
    hx = rmsnorm(x, p['norm_x_g'])
    qx = (hx @ p['xq']).reshape(B, S, X_HEADS, X_HEAD_DIM) * (X_HEAD_DIM ** -0.5)
    pa = jax.nn.softmax(jnp.einsum('bshd,bmhd->bhsm', qx, mem_k).astype(jnp.float32), axis=-1)
    ox = jnp.einsum('bhsm,bmhd->bshd', pa.astype(mem_v.dtype), mem_v).reshape(B, S, X_WIDTH)
    x = x + ox @ p['xo']
    x = x + peer_ffn(rmsnorm(x, p['norm_ffn_g']), p['peer_wq'], p['peer_sub_keys'], p['peer_u'], p['peer_v'])
    return (x, shift_new, wkv_new, kc, vc, ks, vs, kw, vw)

def setup_inputs(seed: int = 0) -> dict:
    key = jax.random.key(seed)
    keys = list(jax.random.split(key, 64))

    def nrm(shape, scale):
        return jax.random.normal(keys.pop(), shape, jnp.float32) * scale

    def gain(n):
        return 1.0 + nrm((n,), 0.05)

    n_pages = PAST_LEN // PAGE_SIZE
    n_phys = (DEC_BATCH * n_pages * 5) // 4
    win_buf = min(WINDOW, PAST_LEN)
    page_table = jax.random.permutation(keys.pop(), n_phys)[:DEC_BATCH * n_pages].reshape(DEC_BATCH, n_pages).astype(jnp.int32)
    pool = (n_phys, PAGE_SIZE, NSA_KV_HEADS, NSA_DK)
    return {
        'x_prompt': nrm((BATCH, SEQ, D_MODEL), 1.0),
        'x_sample': nrm((DEC_BATCH, DEC_SEQ, D_MODEL), 1.0),
        'mem_prompt': nrm((BATCH, MEM_TOKENS, D_MODEL), 1.0),
        'state_rwkv_shift': nrm((DEC_BATCH, RW_COLS), 1.0),
        'state_rwkv_wkv': nrm((DEC_BATCH, RW_HEADS, RW_HEAD, RW_HEAD), 0.3),
        'cache_cmp_k': nrm(pool, 1.0),
        'cache_cmp_v': nrm(pool, 1.0),
        'cache_slc_k': nrm(pool, 1.0),
        'cache_slc_v': nrm(pool, 1.0),
        'cache_win_k': nrm((DEC_BATCH, win_buf, NSA_KV_HEADS, NSA_DK), 1.0),
        'cache_win_v': nrm((DEC_BATCH, win_buf, NSA_KV_HEADS, NSA_DK), 1.0),
        'cache_mem_k': nrm((DEC_BATCH, MEM_TOKENS, X_HEADS, X_HEAD_DIM), 1.0),
        'cache_mem_v': nrm((DEC_BATCH, MEM_TOKENS, X_HEADS, X_HEAD_DIM), 1.0),
        'page_table': page_table,
        'norm_mix_g': gain(D_MODEL),
        'w_in': nrm((D_MODEL, IN_COLS), D_MODEL ** -0.5),
        'rw_mu': jax.random.uniform(keys.pop(), (RW_COLS,), jnp.float32),
        'rw_w0': jax.random.uniform(keys.pop(), (RW_WIDTH,), jnp.float32, -4.0, 1.0),
        'rw_w2': nrm((RW_LORA_W, RW_WIDTH), 0.1),
        'rw_a0': nrm((RW_WIDTH,), 0.5),
        'rw_a2': nrm((RW_LORA_A, RW_WIDTH), 0.1),
        'rw_g2': nrm((RW_LORA_G, RW_WIDTH), RW_LORA_G ** -0.5),
        'rw_k_k': 0.85 + nrm((RW_WIDTH,), 0.05),
        'rw_k_a': gain(RW_WIDTH),
        'rw_r_k': nrm((RW_HEADS, RW_HEAD), 0.1),
        'rw_lnx_g': gain(RW_WIDTH),
        'rw_lnx_b': nrm((RW_WIDTH,), 0.01),
        'cmp_w1': nrm((2, CMP_BLOCK, NSA_DK, CMP_HID), (CMP_BLOCK * NSA_DK) ** -0.5),
        'cmp_b1': nrm((2, CMP_HID), 0.01),
        'cmp_w2': nrm((2, CMP_HID, NSA_DK), CMP_HID ** -0.5),
        'nsa_norm_g': gain(NSA_WIDTH),
        'w_out': nrm((MIX_WIDTH, D_MODEL), MIX_WIDTH ** -0.5),
        'norm_x_g': gain(D_MODEL),
        'mem_norm_g': gain(D_MODEL),
        'xq': nrm((D_MODEL, X_WIDTH), D_MODEL ** -0.5),
        'xk': nrm((D_MODEL, X_WIDTH), D_MODEL ** -0.5),
        'xv': nrm((D_MODEL, X_WIDTH), D_MODEL ** -0.5),
        'xo': nrm((X_WIDTH, D_MODEL), X_WIDTH ** -0.5),
        'norm_ffn_g': gain(D_MODEL),
        'peer_wq': nrm((D_MODEL, PEER_HEADS * PEER_QDIM), D_MODEL ** -0.5),
        'peer_sub_keys': nrm((PEER_HEADS, 2, PEER_KEYS, PEER_HALF), PEER_HALF ** -0.5),
        'peer_u': nrm((PEER_EXPERTS, D_MODEL), D_MODEL ** -0.5),
        'peer_v': nrm((PEER_EXPERTS, D_MODEL), 0.1),
        'norm_f_g': gain(D_MODEL),
    }

def reference(x_prompt, x_sample, mem_prompt, state_rwkv_shift, state_rwkv_wkv, cache_cmp_k, cache_cmp_v,
              cache_slc_k, cache_slc_v, cache_win_k, cache_win_v, cache_mem_k, cache_mem_v, page_table,
              norm_mix_g, w_in, rw_mu, rw_w0, rw_w2, rw_a0, rw_a2, rw_g2, rw_k_k, rw_k_a, rw_r_k,
              rw_lnx_g, rw_lnx_b, cmp_w1, cmp_b1, cmp_w2, nsa_norm_g, w_out, norm_x_g, mem_norm_g,
              xq, xk, xv, xo, norm_ffn_g, peer_wq, peer_sub_keys, peer_u, peer_v, norm_f_g):
    p = {'norm_mix_g': norm_mix_g, 'w_in': w_in, 'rw_mu': rw_mu, 'rw_w0': rw_w0, 'rw_w2': rw_w2,
         'rw_a0': rw_a0, 'rw_a2': rw_a2, 'rw_g2': rw_g2, 'rw_k_k': rw_k_k, 'rw_k_a': rw_k_a,
         'rw_r_k': rw_r_k, 'rw_lnx_g': rw_lnx_g, 'rw_lnx_b': rw_lnx_b, 'cmp_w1': cmp_w1,
         'cmp_b1': cmp_b1, 'cmp_w2': cmp_w2, 'nsa_norm_g': nsa_norm_g, 'w_out': w_out,
         'norm_x_g': norm_x_g, 'xq': xq, 'xo': xo, 'norm_ffn_g': norm_ffn_g, 'peer_wq': peer_wq,
         'peer_sub_keys': peer_sub_keys, 'peer_u': peer_u, 'peer_v': peer_v}
    B, S = x_prompt.shape[0], x_prompt.shape[1]
    DB, DS = x_sample.shape[0], x_sample.shape[1]
    past_len = page_table.shape[1] * PAGE_SIZE
    dt = x_prompt.dtype
    kv_shape = lambda b, l: (b, l, NSA_KV_HEADS, NSA_DK)

    n_mem = mem_prompt.shape[1]
    mem_h = rmsnorm(mem_prompt, mem_norm_g)
    p_mem_k = (mem_h @ xk).reshape(B, n_mem, X_HEADS, X_HEAD_DIM)
    p_mem_v = (mem_h @ xv).reshape(B, n_mem, X_HEADS, X_HEAD_DIM)
    empty = jnp.zeros(kv_shape(B, 0), dt)
    wpad = jnp.zeros(kv_shape(B, WINDOW), dt)
    hp = x_prompt
    for _ in range(DEPTH):
        hp, p_rwkv_shift, p_rwkv_wkv, p_cmp_k, p_cmp_v, p_slc_k, p_slc_v, p_wnew_k, p_wnew_v = hybrid_layer(
            hp, p_mem_k, p_mem_v, jnp.zeros((B, RW_COLS), dt),
            jnp.zeros((B, RW_HEADS, RW_HEAD, RW_HEAD), jnp.float32),
            empty, empty, empty, empty, wpad, wpad, 0, p)
    y_prompt = rmsnorm(hp, norm_f_g)
    keep_p = min(WINDOW, S)
    p_win_k = p_wnew_k[:, S - keep_p:]
    p_win_v = p_wnew_v[:, S - keep_p:]

    paged = lambda c: c[page_table].reshape(kv_shape(DB, past_len))
    win_buf = cache_win_k.shape[1]
    spad = jnp.zeros(kv_shape(DB, WINDOW - win_buf), cache_win_k.dtype)
    hs = x_sample
    for _ in range(DEPTH):
        hs, s_rwkv_shift, s_rwkv_wkv, s_cmp_k, s_cmp_v, s_slc_k, s_slc_v, s_wnew_k, s_wnew_v = hybrid_layer(
            hs, cache_mem_k, cache_mem_v, state_rwkv_shift, state_rwkv_wkv,
            paged(cache_cmp_k), paged(cache_cmp_v), paged(cache_slc_k), paged(cache_slc_v),
            jnp.concatenate([spad, cache_win_k], axis=1), jnp.concatenate([spad, cache_win_v], axis=1),
            past_len, p)
    y_sample = rmsnorm(hs, norm_f_g)
    keep_s = min(WINDOW, past_len + DS)
    s_win_k = jnp.concatenate([cache_win_k, s_wnew_k], axis=1)[:, win_buf + DS - keep_s:]
    s_win_v = jnp.concatenate([cache_win_v, s_wnew_v], axis=1)[:, win_buf + DS - keep_s:]

    return (y_prompt, y_sample,
            p_rwkv_shift, p_rwkv_wkv, p_cmp_k, p_cmp_v, p_slc_k, p_slc_v, p_win_k, p_win_v, p_mem_k, p_mem_v,
            s_rwkv_shift, s_rwkv_wkv, s_cmp_k, s_cmp_v, s_slc_k, s_slc_v, s_win_k, s_win_v)


_drawn_inputs = setup_inputs


def setup_inputs(seed=0):
    import zlib

    import numpy as np

    out = dict(_drawn_inputs(seed))
    spreads = {}
    factors = {'rw_lnx_g': 3.741, 'rw_lnx_b': 8.0, 'cmp_b1': 4.092, 'norm_x_g': 8.0, 'norm_ffn_g': 5.537}
    for name, (base, spread) in spreads.items():
        noise = np.random.default_rng([zlib.crc32(name.encode()), seed]).standard_normal(out[name].shape)
        drawn = base * np.exp(spread * noise) if base else spread * noise
        out[name] = __import__('jax').numpy.asarray(drawn.astype(out[name].dtype))
    for name, factor in factors.items():
        out[name] = (out[name] * factor).astype(out[name].dtype)
    return out
```

```python
from contextlib import ExitStack

import numpy as np

import concourse.bass as bass
from concourse import mybir

ALU = mybir.AluOpType
ACT = mybir.ActivationFunctionType
AX = mybir.AxisListType.X
F32 = mybir.dt.float32
U32 = mybir.dt.uint32
I32 = mybir.dt.int32
ds = bass.DynSlice

P = 128
D = 2048
KC = D // P
TP, TS = 256, 8
T = TP + TS
RWC = 27
C_R, C_K, C_V, C_WA, C_G = 0, 8, 16, 24, 25
C_Q, C_KC, C_VC, C_KS, C_VS, C_KW, C_VW, C_GL = 27, 35, 37, 39, 41, 43, 45, 47
NCH = 48
CH = 32
NB = TP // CH
NCB = TP // 16 - 1
N_PHYS = 160
PG = 16
NCS = 127
NBLK = 33
RING = 4
NEG = -1e30
DECAY = -float(np.exp(-0.5))

VEC = {}
_at = 0
for _n, _c in [("mix", 16), ("x", 16), ("ffn", 16), ("f", 16), ("mem", 16), ("nsa", 8), ("mu", RWC),
               ("w0", 8), ("a0", 8), ("kk", 8), ("ka", 8), ("rk", 8), ("lg", 8), ("lb", 8), ("b1", 2)]:
    VEC[_n] = (_at, _c)
    _at += _c
NVEC = _at

CON = {}
_at = 0
for _n, _c in [("ident", 128), ("ones", 128), ("bones", 128), ("tri", 256), ("scan", 256),
               ("causal", 512), ("cmask", 2 * NCB), ("cvalid", 2), ("gsum", 32), ("gexp", 128),
               ("gate", 3 * 128), ("bsel", 8), ("eps", 2), ("iota", 128), ("i16", 16)]:
    CON[_n] = (_at, _c)
    _at += _c
NCON = _at


def constants():
    c = np.zeros((P, NCON), np.float32)
    p = np.arange(P)[:, None]
    f = np.arange(P)[None, :]

    def put(name, v, rows=P):
        a, n = CON[name]
        c[:rows, a:a + n] = v

    put("ident", p == f)
    put("ones", 1.0)
    put("bones", p // 64 == f // 64)
    same = p // CH == f // CH
    put("tri", np.concatenate([same & (p < f), same & (p <= f)], 1))
    put("scan", np.arange(TP)[None, :] % CH != 0)
    key = np.arange(TP)[None, :]
    put("causal", np.concatenate([np.where(key <= p + P * t, 0.0, NEG) for t in range(2)], 1))
    end = np.arange(NCB)[None, :] * 16 + 31
    put("cmask", np.concatenate([np.where(end <= p + P * t, 0.0, NEG) for t in range(2)], 1))
    put("cvalid", np.concatenate([p + P * t >= 31 for t in range(2)], 1))
    put("gsum", p // 4 == np.arange(32)[None, :])
    put("gexp", (np.arange(32)[:, None] == f // 4), 32)
    head = ((f // 64) * 2 + (f // 4) % 2) * 4 + f % 4
    put("gate", np.concatenate([(np.arange(48)[:, None] == head * 3 + br) for br in range(3)], 1), 48)
    put("bsel", (p // 8) % 8 == np.arange(8)[None, :])
    c[:, CON["eps"][0]] = 1e-6
    c[:, CON["eps"][0] + 1] = 64e-5
    put("iota", f)
    put("i16", np.arange(16)[None, :])
    return c


class Ctx:
    pass


def build(nc, d):
    g = Ctx()
    with ExitStack() as top:
        names = [0]

        def sb(st, name, shape, dt=F32):
            names[0] += 1
            return st.enter_context(nc.sbuf_tensor(f"{name}_{names[0]}", shape, dt))

        def sem(name):
            names[0] += 1
            return top.enter_context(nc.semaphore(f"{name}_{names[0]}"))

        ps = top.enter_context(nc.psum_tensor("ps", [P, 8, 512], F32))
        con = sb(top, "con", [P, NCON])
        vec = sb(top, "vec", [P, NVEC])

        def cst(name, rows=P):
            a, n = CON[name]
            return con[0:rows, a:a + n]

        def vcol(name, c, lo=0, hi=P):
            a = VEC[name][0] + c
            return vec[lo:hi, a:a + 1]

        ident, ones, bones = cst("ident"), cst("ones"), cst("bones")
        dve_step, act_step, pool_step = sem("dve_step"), sem("act_step"), sem("pool_step")
        steps = {"dve": 0, "act": 0, "pool": 0}

        def link(eng, ins):
            steps["dve"] += 1
            ins.then_inc(dve_step, 1)
            eng.wait_ge(dve_step, steps["dve"])

        def alink(eng, ins):
            steps["act"] += 1
            ins.then_inc(act_step, 1)
            eng.wait_ge(act_step, steps["act"])

        landed = [sem(f"tile{k}_landed") for k in range(RING)]
        used = [sem(f"tile{k}_used") for k in range(RING)]
        drained = [sem(f"bank{k}_drained") for k in range(RING)]
        rounds = [1]

        moved = sem("moved")
        n_moved = [0]

        def credit(sems):
            with ExitStack() as st:
                z = sb(st, "credit", [1, len(sems)])
                with nc.Block() as block:
                    @block.gpsimd
                    def _(pool):
                        for n, s in enumerate(sems):
                            pool.memset(z[:, n:n + 1], 0.0).then_inc(s, 1)

        def loads(pairs):
            with nc.Block() as block:
                @block.sync
                def _(sp):
                    for a, b in pairs:
                        sp.dma_start(a, b).then_inc(moved, 16)
                    n_moved[0] += 16 * len(pairs)
                    sp.wait_ge(moved, n_moved[0])

        stores = loads

        s_sq, s_sum, s_rt = sem("squared"), sem("summed"), sem("root")
        norms = [0, 0]

        def rms(src, dst, gain, nch, t):
            n0, c0 = norms
            norms[0] += 1
            norms[1] += nch
            width = nch * P
            with ExitStack() as st:
                sq = sb(st, "sq", [P, 2, t])
                rt = sb(st, "rt", [P, t])
                rr = sb(st, "rr", [P, t])
                with nc.Block() as block:
                    @block.scalar
                    def _(act):
                        for c in range(nch):
                            if c >= 2:
                                act.wait_ge(s_sum, c0 + c - 1)
                            act.activation(sq[:, c % 2, :], src[:, c, :], ACT.Square).then_inc(s_sq, 1)
                        act.wait_ge(s_sum, c0 + nch)
                        act.activation(rt[:, :], ps[:, 0, 0:t], ACT.Sqrt, bias=cst("eps")[:, 0:1],
                                       scale=1.0 / width).then_inc(s_rt, 1)

                    @block.tensor
                    def _(pe):
                        for c in range(nch):
                            pe.wait_ge(s_sq, c0 + c + 1)
                            pe.matmul(ps[:, 0, 0:t], ones, sq[:, c % 2, :], start=(c == 0),
                                      stop=(c == nch - 1)).then_inc(s_sum, 1)

                    @block.vector
                    def _(dve):
                        dve.wait_ge(s_rt, n0 + 1)
                        link(dve, dve.reciprocal(rr[:, :], rt[:, :]))
                        for c in range(nch):
                            dve.scalar_tensor_tensor(dst[:, c, :], src[:, c, :], vcol(gain, c), rr[:, :],
                                                     ALU.mult, ALU.mult)

        def project(w, src, dst, n, ring, residual=False):
            r0 = rounds[0]
            per = n // RING
            rounds[0] += per
            with nc.Block() as block:
                @block.sync
                def _(sp):
                    with sp.Fori(0, per) as i:
                        for k in range(RING):
                            sp.wait_ge(used[k], i + r0)
                            sp.dma_start(ring[:, k, :], w[ds(i * RING + k, 1), :, :].rearrange("a p n -> p (a n)")
                                         ).then_inc(landed[k], 16)

                @block.tensor
                def _(pe):
                    with pe.Fori(0, per) as i:
                        for k in range(RING):
                            pe.wait_ge(landed[k], (i + r0) * 16)
                            pe.wait_ge(drained[k], i + r0)
                            for c in range(KC):
                                mm = pe.matmul(ps[:, k, 0:T], ring[:, k, c * P:(c + 1) * P], src[:, c, :],
                                               start=(c == 0), stop=(c == KC - 1))
                            mm.then_inc(used[k], 1)

                def drain(eng, i, k):
                    eng.wait_ge(used[k], i + (r0 + 1))
                    to = dst[:, ds(i * RING + k, 1), :].rearrange("p a t -> p (a t)")
                    if residual:
                        ins = eng.tensor_tensor(to, ps[:, k, 0:T], to, ALU.add)
                    elif eng is nc.scalar:
                        ins = eng.activation(to, ps[:, k, 0:T], ACT.Copy)
                    else:
                        ins = eng.tensor_copy(to, ps[:, k, 0:T])
                    ins.then_inc(drained[k], 1)

                if not residual:
                    @block.scalar
                    def _(act):
                        with act.Fori(0, per) as i:
                            for k in range(0, RING, 2):
                                drain(nc.scalar, i, k)

                @block.vector
                def _(dve):
                    with dve.Fori(0, per) as i:
                        for k in range(0 if residual else 1, RING, 1 if residual else 2):
                            drain(nc.vector, i, k)

        g.nc = nc
        g.d = d
        g.sb = sb
        g.sem = sem
        g.ps = ps
        g.cst = cst
        g.vcol = vcol
        g.ident = ident
        g.ones = ones
        g.bones = bones
        g.link = link
        g.alink = alink
        g.rms = rms
        g.credit = credit
        g.heads_mm = sem("head_sums")
        g.heads_used = sem("head_sums_used")
        g.heads = [0]
        g.project = project
        g.loads = loads
        g.stores = stores
        g.con = con
        g.vec = vec
        g.landed = landed
        g.used = used
        g.drained = drained
        g.rounds = rounds

        credit(used + drained)
        loads([(con[:, :], d["consts"]), (vec[:, :], d["vecs"])])
        with ExitStack() as st:
            cat = sb(st, "cat", [P, KC, T])
            with ExitStack() as s3:
                uT = sb(s3, "uT", [P, NCH, T])
                with ExitStack() as s4:
                    hT = sb(s4, "hT", [P, KC, T])
                    ring = sb(s4, "ring", [P, RING, D])
                    loads([(hT[:, :, :], d["x"])])
                    rms(hT, hT, "mix", KC, T)
                    project(d["w_in"], hT, uT, NCH, ring)
                stores([(d["o_shift"], uT[:, 0:RWC, TP - 1:T]), (d["o_kv"], uT[:, C_KC:C_GL, :])]
                       + [(d["o_win"][i, :, 0:511, :], d["win"][i, :, 1:512, :]) for i in range(2)])
                rwkv(g, uT, cat)
                nsa_prompt(g, uT, cat)
                nsa_sample(g, uT, cat)
            rms(cat[:, 8:16, :], cat[:, 8:16, :], "nsa", 8, T)
            xT = top.enter_context(nc.sbuf_tensor("xT", [P, KC, T], F32, side="right"))
            with ExitStack() as s2:
                ring = sb(s2, "ring", [P, RING, D])
                loads([(xT[:, :, :], d["x"])])
                project(d["w_out"], cat, xT, KC, ring, residual=True)
        with ExitStack() as st:
            memk = sb(st, "memk", [P, 4, TP])
            memv = sb(st, "memv", [P, 2, 512])
            memory(g, memk, memv)
            cross(g, memk, memv, xT)
        peer(g, xT)
        with ExitStack() as st:
            y = sb(st, "y", [P, KC, T])
            rms(xT, y, "f", KC, T)
            stores([(d["o_y"], y[:, :, :])])


def memory(g, memk, memv):
    nc, d, ps = g.nc, g.d, g.ps
    with ExitStack() as st:
        mT = g.sb(st, "mT", [P, KC, TP])
        wk = g.sb(st, "wk", [P, KC, 512])
        wv = g.sb(st, "wv", [P, KC, 512])
        g.loads([(mT[:, :, :], d["mem"]), (wk[:, :, :], d["xk"]), (wv[:, :, :], d["xv"])])
        g.rms(mT, mT, "mem", KC, TP)
        s_mm, s_out = g.sem("mem_products"), g.sem("mem_copied")
        with nc.Block() as block:
            @block.tensor
            def _(pe):
                for h in range(4):
                    for c in range(KC):
                        mm = pe.matmul(ps[:, h, 0:TP], wk[:, c, h * P:(h + 1) * P], mT[:, c, :],
                                       start=(c == 0), stop=(c == KC - 1))
                    mm.then_inc(s_mm, 1)
                for m in range(2):
                    for c in range(KC):
                        mm = pe.matmul(ps[:, 4 + m, :], mT[:, c, m * P:(m + 1) * P], wv[:, c, :],
                                       start=(c == 0), stop=(c == KC - 1))
                    mm.then_inc(s_mm, 1)

            @block.vector
            def _(dve):
                for h in range(4):
                    dve.wait_ge(s_mm, h + 1)
                    dve.tensor_copy(memk[:, h, :], ps[:, h, 0:TP]).then_inc(s_out, 1)
                for m in range(2):
                    dve.wait_ge(s_mm, 5 + m)
                    dve.tensor_copy(memv[:, m, :], ps[:, 4 + m, :]).then_inc(s_out, 1)
        g.stores([(d["o_memk"], memk[:, :, :]), (d["o_memv"], memv[:, :, :])])


def head_sums(g, src, out_of, n, t=T):
    nc, ps = g.nc, g.ps
    s_mm, s_used, n0 = g.heads_mm, g.heads_used, g.heads[0]
    g.heads[0] += n
    with nc.Block() as block:
        @block.tensor
        def _(pe):
            for m in range(n):
                if m >= 4:
                    pe.wait_ge(s_used, n0 + m - 3)
                pe.matmul(ps[:, m % 4, 0:t], g.bones, src[:, m, :], start=True, stop=True).then_inc(s_mm, 1)

        @block.vector
        def _(dve):
            for m in range(n):
                dve.wait_ge(s_mm, n0 + m + 1)
                out_of(dve, m, ps[:, m % 4, 0:t]).then_inc(s_used, 1)


def rwkv(g, uT, cat):
    nc, d, ps, sb, sem, link, alink = g.nc, g.d, g.ps, g.sb, g.sem, g.link, g.alink
    ident, vcol, cst = g.ident, g.vcol, g.cst
    with ExitStack() as st:
        a_, kp, sg, tmp, rt, y = (sb(st, n, [P, 8, T]) for n in ("a", "kp", "sg", "tmp", "rt", "y"))
        us = uT[:, 0:RWC, :]
        r, k, v = us[:, C_R:C_R + 8, :], us[:, C_K:C_K + 8, :], us[:, C_V:C_V + 8, :]
        kk = k
        gg, bonus = cat[:, 0:8, :], cat[:, 8:16, :]
        with ExitStack() as s1:
            shift = sb(s1, "shift", [P, RWC, TS])
            wa2 = sb(s1, "wa2", [P, 1024])
            g2a = sb(s1, "g2a", [P, 1024])
            g2b = sb(s1, "g2b", [32, 1024])
            oka = sb(s1, "oka", [P, 8])
            diff = sb(s1, "diff", [P, 4, T])
            s_in, s_lo, s_mm, s_sig = sem("rw_in"), sem("rw_low"), sem("rw_mm"), sem("rw_sig")
            s_us = sem("rw_mixed")
            with nc.Block() as block:
                @block.sync
                def _(sp):
                    for a, b in [(shift[:, :, :], d["shift"]), (wa2[:, :], d["wa2"]),
                                 (g2a[:, :], d["rw_g2"][0:P, :]), (g2b[:, :], d["rw_g2"][P:160, :])]:
                        sp.dma_start(a, b).then_inc(s_in, 16)

                @block.vector
                def _(dve):
                    dve.wait_ge(s_in, 64)
                    for n, c in enumerate(reversed(range(RWC))):
                        df = diff[:, n % 4, :]
                        if n >= 4:
                            dve.wait_ge(s_us, n - 3)
                        dve.tensor_tensor(df[:, 1:TP], us[:, c, 0:TP - 1], us[:, c, 1:TP], ALU.subtract)
                        dve.tensor_scalar(df[:, 0:1], us[:, c, 0:1], -1.0, None, ALU.mult)
                        link(dve, dve.tensor_tensor(df[:, TP:T], shift[:, c, :], us[:, c, TP:T], ALU.subtract))
                        dve.scalar_tensor_tensor(us[:, c, :], df, vcol("mu", c), us[:, c, :],
                                                 ALU.mult, ALU.add).then_inc(s_us, 1)

                @block.scalar
                def _(act):
                    act.wait_ge(s_us, 3)
                    act.activation(us[0:64, C_WA, :], us[0:64, C_WA, :], ACT.Tanh).then_inc(s_lo, 1)
                    act.activation(us[:, C_G, :], us[:, C_G, :], ACT.Sigmoid).then_inc(s_lo, 1)
                    act.activation(us[0:32, C_G + 1, :], us[0:32, C_G + 1, :], ACT.Sigmoid).then_inc(s_lo, 1)
                    for m in range(8):
                        act.wait_ge(s_mm, m + 1)
                        act.activation(sg[:, m, :], ps[:, 3 * (m % 2), 0:T], ACT.Sigmoid, bias=vcol("w0", m))
                        act.activation(a_[:, m, :], ps[:, 3 * (m % 2) + 1, 0:T], ACT.Sigmoid, bias=vcol("a0", m))
                        act.activation(gg[:, m, :], ps[:, 3 * (m % 2) + 2, 0:T], ACT.Copy).then_inc(s_sig, 1)

                @block.tensor
                def _(pe):
                    pe.wait_ge(s_lo, 3)
                    for m in range(8):
                        if m >= 2:
                            pe.wait_ge(s_sig, m - 1)
                        cs = slice(m * P, (m + 1) * P)
                        pe.matmul(ps[:, 3 * (m % 2), 0:T], wa2[0:64, cs], us[0:64, C_WA, :], start=True, stop=True)
                        pe.matmul(ps[:, 3 * (m % 2) + 1, 0:T], wa2[64:P, cs], us[64:P, C_WA, :],
                                  start=True, stop=True)
                        pe.matmul(ps[:, 3 * (m % 2) + 2, 0:T], g2a[:, cs], us[:, C_G, :], start=True, stop=False)
                        pe.matmul(ps[:, 3 * (m % 2) + 2, 0:T], g2b[:, cs], us[0:32, C_G + 1, :],
                                  start=False, stop=True).then_inc(s_mm, 1)

            with nc.Block() as block:
                @block.vector
                def _(dve):
                    a0 = VEC["ka"][0]
                    link(dve, dve.tensor_scalar(oka[:, :], g.vec[:, a0:a0 + 8], -1.0, 1.0, ALU.mult, ALU.add))
                    for m in range(8):
                        last = dve.tensor_scalar(kp[:, m, :], a_[:, m, :], vcol("ka", m), oka[:, m:m + 1],
                                                 ALU.mult, ALU.add)
                    link(dve, last)
                    link(dve, dve.tensor_tensor(kp[:, :, :], kp[:, :, :], k, ALU.mult))
                    for m in range(8):
                        last = dve.tensor_scalar(kk[:, m, :], k[:, m, :], vcol("kk", m), None, ALU.mult)
                    link(dve, last)
                    dve.tensor_tensor(tmp[:, :, :], kk, kk, ALU.mult)
                    for m in range(8):
                        dve.scalar_tensor_tensor(bonus[:, m, :], r[:, m, :], vcol("rk", m), kp[:, m, :],
                                                 ALU.mult, ALU.mult)
        head_sums(g, tmp, lambda dve, m, s: dve.tensor_scalar(rt[:, m, :], s, 1e-24, None, ALU.max), 8)
        head_sums(g, bonus, lambda dve, m, s: dve.tensor_tensor(bonus[:, m, :], s, v[:, m, :], ALU.mult), 8)
        with nc.Block() as block:
            @block.scalar
            def _(act):
                act.activation(rt[:, :, :], rt[:, :, :], ACT.Sqrt)
        with nc.Block() as block:
            @block.vector
            def _(dve):
                link(dve, dve.reciprocal(tmp[:, :, :], rt[:, :, :]))
                dve.tensor_tensor(kk[:, :, :], kk[:, :, :], tmp[:, :, :], ALU.mult)
        b_ = a_
        with nc.Block() as block:
            @block.vector
            def _(dve):
                dve.tensor_tensor(b_[:, :, :], kk[:, :, :], a_[:, :, :], ALU.mult)

        rwkv_sample(g, r, v, kk, kp, b_, sg, y)
        rwkv_prompt(g, uT, kp, b_, sg, tmp, rt, y)

        head_sums(g, y, lambda dve, m, s: dve.scalar_tensor_tensor(y[:, m, :], s, -1.0 / 64, y[:, m, :],
                                                                   ALU.mult, ALU.add), 8)
        with nc.Block() as block:
            @block.vector
            def _(dve):
                dve.tensor_tensor(tmp[:, :, :], y[:, :, :], y[:, :, :], ALU.mult)
        head_sums(g, tmp, lambda dve, m, s: dve.tensor_copy(rt[:, m, :], s), 8)
        with nc.Block() as block:
            @block.scalar
            def _(act):
                act.activation(rt[:, :, :], rt[:, :, :], ACT.Sqrt, bias=cst("eps")[:, 1:2], scale=1.0 / 64)
        with nc.Block() as block:
            @block.vector
            def _(dve):
                link(dve, dve.reciprocal(tmp[:, :, :], rt[:, :, :]))
                link(dve, dve.tensor_tensor(y[:, :, :], y[:, :, :], tmp[:, :, :], ALU.mult))
                for m in range(8):
                    dve.tensor_scalar(y[:, m, :], y[:, m, :], vcol("lg", m), vcol("lb", m), ALU.mult, ALU.add)
        with nc.Block() as block:
            @block.vector
            def _(dve):
                link(dve, dve.tensor_tensor(y[:, :, :], y[:, :, :], bonus[:, :, :], ALU.add))
                dve.tensor_tensor(cat[:, 0:8, :], y[:, :, :], gg[:, :, :], ALU.mult)


def rwkv_prompt(g, uT, kp, b_, sg, tmp, rt, y):
    nc, d, ps, sb, sem, link, alink = g.nc, g.d, g.ps, g.sb, g.sem, g.link, g.alink
    ident, cst = g.ident, g.cst
    r, kk, v = uT[:, 0:8, 0:TP], uT[:, 8:16, 0:TP], uT[:, 16:24, :]
    bt, kt = b_[:, :, 0:TP], kp[:, :, 0:TP]
    with ExitStack() as st:
        pc = sb(st, "pc", [P, NB, 8])
        state = sb(st, "state", [P, NB + 1, 8, 64])
        qT = sb(st, "qT", [P, 8, TP])
        t2, e, cum = y[:, :, 0:TP], tmp[:, :, 0:TP], rt[:, :, 0:TP]
        s_cum, s_e, s_x = sem("cum"), sem("e"), sem("e_used")
        with nc.Block() as block:
            @block.vector
            def _(dve):
                for m in range(8):
                    dve.tensor_tensor_scan(cum[:, m, :], cst("scan"), sg[:, m, 0:TP], 0.0,
                                           ALU.mult, ALU.add)
                link(dve, dve.memset(state[:, 0, :, :], 0.0))
                dve.tensor_tensor(t2, cum, sg[:, :, 0:TP], ALU.subtract).then_inc(s_cum, 1)
                dve.wait_ge(s_e, 1)
                dve.tensor_copy(pc[:, :, :], e[:, :, CH - 1:TP:CH].rearrange("p m n -> p n m"))
                dve.tensor_tensor(r, e, r, ALU.mult).then_inc(s_x, 1)
                dve.wait_ge(s_e, 2)
                dve.tensor_tensor(bt, e, bt, ALU.mult)
                dve.tensor_tensor(kt, e, kt, ALU.mult).then_inc(s_x, 1)
                link(dve, dve.tensor_scalar(kk, kk, -1.0, None, ALU.mult))
                dve.wait_ge(s_e, 3)
                dve.tensor_tensor(kk, e, kk, ALU.mult)

            @block.scalar
            def _(act):
                act.wait_ge(s_cum, 1)
                act.activation(e, cum, ACT.Exp, scale=DECAY).then_inc(s_e, 1)
                act.wait_ge(s_x, 1)
                act.activation(e, cum, ACT.Exp, scale=-DECAY).then_inc(s_e, 1)
                act.wait_ge(s_x, 2)
                act.activation(e, t2, ACT.Exp, scale=DECAY).then_inc(s_e, 1)

        for tile in range(2):
            rwkv_tile(g, tile, uT, bt, kt, v, pc, state, qT, y)

        s_mm, s_used = sem("y_mm"), sem("y_used")
        with nc.Block() as block:
            @block.tensor
            def _(pe):
                for m in range(8):
                    if m >= 4:
                        pe.wait_ge(s_used, m - 3)
                    for h in range(2):
                        rows = slice(64 * h, 64 * h + 64)
                        for c in range(NB):
                            mm = pe.matmul(ps[rows, m % 4, c * CH:(c + 1) * CH], state[rows, c, m, :],
                                           qT[rows, m, c * CH:(c + 1) * CH], start=True, stop=True)
                    mm.then_inc(s_mm, 1)

            @block.vector
            def _(dve):
                for m in range(8):
                    dve.wait_ge(s_mm, m + 1)
                    dve.tensor_tensor(y[:, m, 0:TP], ps[:, m % 4, 0:TP], y[:, m, 0:TP], ALU.add).then_inc(s_used, 1)
        g.stores([(d["o_pwkv"], state[:, NB, :, :])])


def rwkv_tile(g, tile, uT, bt, kt, v, pc, state, qT, y):
    nc, ps, sb, sem, link = g.nc, g.ps, g.sb, g.sem, g.link
    ident, cst = g.ident, g.cst
    tok = slice(tile * P, (tile + 1) * P)
    tri = cst("tri")
    with ExitStack() as st:
        rows4 = sb(st, "rows4", [P, 4, 8, P])
        w = sb(st, "w", [P, 16, P])
        at = sb(st, "at", [P, 4, 8, 64])
        s_tr, s_cp = sem("rows_turned"), sem("rows_copied")
        with nc.Block() as block:
            @block.tensor
            def _(pe):
                for m in range(8):
                    if m >= 4:
                        pe.wait_ge(s_cp, m - 3)
                    for n, src in enumerate((uT[:, 8 + m, tok], bt[:, m, tok], kt[:, m, tok], v[:, m, tok])):
                        mm = pe.transpose(ps[:, m % 4, n * P:(n + 1) * P], src, ident)
                    mm.then_inc(s_tr, 1)

            @block.vector
            def _(dve):
                for m in range(8):
                    dve.wait_ge(s_tr, m + 1)
                    dve.tensor_copy(rows4[:, :, m, :], ps[:, m % 4, :].rearrange("p (n c) -> p n c", n=4)
                                    ).then_inc(s_cp, 1)

        at_bank = (6, 7, 0, 1)
        xs = sb(st, "xs", [P, 2, 4, P])
        ms = sb(st, "ms", [P, 2, 4, P])
        rs = sb(st, "rs", [P, 2, 4, P])
        rb = sb(st, "rb", [P, 4, P])
        nt = sb(st, "nt", [P, 4, P])
        rk = sb(st, "rk", [P, 4, P])
        nv = sb(st, "nv", [P, 4, 64])
        s_pe, s_v = sem("tile_pe"), sem("tile_dve")
        with nc.Block() as block:
            n_pe, n_v = [0], [0]

            @block.tensor
            def _(pe):
                def step(mm):
                    n_pe[0] += 1
                    mm.then_inc(s_pe, 1)
                    pe.wait_ge(s_v, n_pe[0])

                for grp in range(4):
                    heads = [(2 * grp + i % 2, i // 2) for i in range(4)]
                    for i, (m, h) in enumerate(heads):
                        rows = slice(64 * h, 64 * h + 64)
                        arm = uT[rows, m:m + 9:8, tok]
                        pe.matmul(ps[:, i // 2, 256 * (i % 2):256 * (i % 2) + 256], bt[rows, m, tok], arm,
                                  start=True, stop=True)
                        mm = pe.matmul(ps[:, 2 + i // 2, 256 * (i % 2):256 * (i % 2) + 256], kt[rows, m, tok],
                                       arm, start=True, stop=True)
                    step(mm)
                    for i in range(4):
                        pe.transpose(ps[:, 4, i * P:(i + 1) * P], xs[:, 0, i, :], ident)
                    for i, (m, h) in enumerate(heads):
                        mm = pe.matmul(ps[:, 5, i * 64:i * 64 + 64], nt[:, i, :],
                                       rows4[:, 3, m, 64 * h:64 * h + 64], start=True, stop=True)
                    step(mm)
                    for n in range(4):
                        a, b = n % 2, (n + 1) % 2
                        for i in range(4):
                            mm = pe.matmul(ps[:, 0, i * P:(i + 1) * P], xs[:, a, i, :], ms[:, a, i, :],
                                           start=True, stop=True)
                            if n < 3:
                                mm = pe.matmul(ps[:, 1, i * P:(i + 1) * P], ms[:, a, i, :], xs[:, a, i, :],
                                               start=True, stop=True)
                        step(mm)
                        for i in range(4):
                            mm = pe.matmul(ps[:, 2, i * P:(i + 1) * P], ms[:, b, i, :], rs[:, a, i, :],
                                           start=True, stop=True)
                        step(mm)
                    for i, (m, h) in enumerate(heads):
                        pe.matmul(ps[:, 3, i * P:i * P + 64], rs[:, 0, i, :], rows4[:, 0, m, 64 * h:64 * h + 64],
                                  start=True, stop=True)
                        mm = pe.matmul(ps[:, 3, i * P + 64:(i + 1) * P], rs[:, 0, i, :], nv[:, i, :],
                                       start=True, stop=True)
                    step(mm)
                    for i, (m, h) in enumerate(heads):
                        rows = slice(64 * h, 64 * h + 64)
                        wh = w[:, 4 * grp + i, :]
                        at_ = slice((i % 2) * P, (i % 2) * P + P)
                        pe.matmul(ps[rows, 4, at_], wh[:, 0:64], rb[:, i, :], start=True, stop=True)
                        pe.matmul(ps[rows, 5, at_], wh[:, 64:P], rb[:, i, :], start=True, stop=False)
                        mm = pe.matmul(ps[rows, 5, at_], rows4[:, 3, m, 64 * h:64 * h + 64], rk[:, i, :],
                                       start=False, stop=True)
                    step(mm)
                    for i, (m, h) in enumerate(heads):
                        rows = slice(64 * h, 64 * h + 64)
                        for c in range(4):
                            tk = slice(CH * c, CH * c + CH)
                            mm = pe.matmul(ps[rows, at_bank[c], (i % 2) * 64:(i % 2) * 64 + 64],
                                           w[tk, 4 * grp + i, 0:64], rows4[tk, 1, m, 64 * h:64 * h + 64],
                                           start=True, stop=True, tile_position=(CH * c, 64 * h))
                    step(mm)

            @block.vector
            def _(dve):
                def take():
                    n_v[0] += 1
                    dve.wait_ge(s_pe, n_v[0])

                for grp in range(4):
                    take()
                    for i2 in range(2):
                        two = slice(2 * i2, 2 * i2 + 2)
                        bank = ps[:, i2, :].rearrange("p (i a t) -> p i a t", i=2, a=2)
                        bankk = ps[:, 2 + i2, :].rearrange("p (i a t) -> p i a t", i=2, a=2)
                        strict = tri[:, 0:P].unsqueeze(1).broadcast_to([P, 2, P])
                        incl = tri[:, P:2 * P].unsqueeze(1).broadcast_to([P, 2, P])
                        dve.tensor_tensor(xs[:, 0, two, :], bank[:, :, 1, :], strict, ALU.mult)
                        dve.tensor_tensor(rb[:, two, :], bank[:, :, 0, :], incl, ALU.mult)
                        dve.tensor_tensor(nt[:, two, :], bankk[:, :, 1, :], strict, ALU.mult)
                        last = dve.tensor_tensor(rk[:, two, :], bankk[:, :, 0, :], incl, ALU.mult)
                    last.then_inc(s_v, 1)
                    take()
                    dve.tensor_copy(ms[:, 0, :, :].rearrange("p i t -> p (i t)"), ps[:, 4, :])
                    dve.wait_ge(s_v, n_v[0] - 1)
                    dve.tensor_tensor(rs[:, 0, :, :], xs[:, 0, :, :],
                                      ident.unsqueeze(1).broadcast_to([P, 4, P]), ALU.add)
                    dve.tensor_copy(nv[:, :, :].rearrange("p i t -> p (i t)"), ps[:, 5, 0:256]).then_inc(s_v, 1)
                    for n in range(4):
                        a, b = n % 2, (n + 1) % 2
                        take()
                        if n < 3:
                            dve.tensor_copy(xs[:, b, :, :].rearrange("p i t -> p (i t)"), ps[:, 1, :])
                        dve.tensor_copy(ms[:, b, :, :].rearrange("p i t -> p (i t)"), ps[:, 0, :]).then_inc(s_v, 1)
                        take()
                        dve.wait_ge(s_v, n_v[0] - 1)
                        dve.tensor_tensor(rs[:, b, :, :].rearrange("p i t -> p (i t)"), ps[:, 2, :],
                                          rs[:, a, :, :].rearrange("p i t -> p (i t)"), ALU.add).then_inc(s_v, 1)
                    take()
                    dve.tensor_copy(w[:, 4 * grp:4 * grp + 4, :].rearrange("p i t -> p (i t)"), ps[:, 3, :]
                                    ).then_inc(s_v, 1)
                    take()
                    m2 = slice(2 * grp, 2 * grp + 2)
                    dve.tensor_tensor(qT[:, m2, tok], ps[:, 4, 0:256].rearrange("p (m t) -> p m t", m=2),
                                      uT[:, m2, tok], ALU.add)
                    dve.tensor_copy(y[:, m2, tok], ps[:, 5, 0:256].rearrange("p (m t) -> p m t", m=2)).then_inc(s_v, 1)
                    take()
                    for h in range(2):
                        rows = slice(64 * h, 64 * h + 64)
                        eye = ident[rows, rows].unsqueeze(1).broadcast_to([64, 2, 64])
                        for c in range(4):
                            last = dve.tensor_tensor(at[rows, c, m2, :],
                                                     ps[rows, at_bank[c], 0:P].rearrange("p (m j) -> p m j", m=2), eye, ALU.add)
                    last.then_inc(s_v, 1)

        s_st, s_ev = sem("state_mm"), sem("state_new")
        with nc.Block() as block:
            @block.tensor
            def _(pe):
                for c in range(4):
                    tk = slice(CH * c, CH * c + CH)
                    if c >= 1:
                        pe.wait_ge(s_ev, c)
                    for m in range(8):
                        for h in range(2):
                            rows = slice(64 * h, 64 * h + 64)
                            out = ps[rows, c % 2, m * 64:m * 64 + 64]
                            pos = (CH * c, 64 * h)
                            pe.matmul(out, rows4[tk, 1, m, 64 * h:64 * h + 64], w[tk, 4 * (m // 2) + 2 * h + m % 2, 64:P],
                                      start=True, stop=False, tile_position=pos)
                            pe.matmul(out, rows4[tk, 2, m, 64 * h:64 * h + 64], rows4[tk, 3, m, 64 * h:64 * h + 64],
                                      start=False, stop=False, tile_position=pos)
                            mm = pe.matmul(out, at[rows, c, m, :], state[rows, 4 * tile + c, m, :],
                                           start=False, stop=True)
                    mm.then_inc(s_st, 1)

            @block.vector
            def _(dve):
                for c in range(4):
                    dve.wait_ge(s_st, c + 1)
                    n = 4 * tile + c
                    dve.tensor_tensor(state[:, n + 1, :, :], ps[:, c % 2, :].rearrange("p (m j) -> p m j", m=8),
                                      pc[:, n, :].unsqueeze(2).broadcast_to([P, 8, 64]), ALU.mult).then_inc(s_ev, 1)


def rwkv_sample(g, r, v, kk, kp, b_, sg, y):
    nc, d, ps, sb, sem, link = g.nc, g.d, g.ps, g.sb, g.sem, g.link
    ident = g.ident
    with ExitStack() as st:
        S = sb(st, "S", [P, 64, 64])
        big = sb(st, "big", [P, 64, 64])
        vs = sb(st, "vs", [P, 6, 64])
        packed = sb(st, "packed", [P, 6, TS, 8])
        sa = sb(st, "sa", [P, 64])
        yr = sb(st, "yr", [P, 64])
        s_in, s_pk, s_tr, s_cp, s_y, s_yt, s_out = (sem(n) for n in (
            "st_in", "packed", "turned", "rows", "y_rows", "y_turned", "st_out"))
        with nc.Block() as block:
            @block.sync
            def _(sp):
                sp.dma_start(S[:, :, :].rearrange("p i j -> p (i j)"), d["wkv"]).then_inc(s_in, 16)
                sp.wait_ge(s_y, 1)
                sp.dma_start(d["o_swkv"], S[:, :, :].rearrange("p i j -> p (i j)")).then_inc(s_out, 16)
                sp.wait_ge(s_out, 16)

            @block.tensor
            def _(pe):
                pe.wait_ge(s_pk, 1)
                for n in range(6):
                    for h in range(2):
                        rows = slice(64 * h, 64 * h + 64)
                        mm = pe.matmul(ps[rows, 0, n * 64:n * 64 + 64],
                                       packed[rows, n, :, :].rearrange("p b m -> p (b m)"), ident[rows, rows],
                                       start=True, stop=True)
                mm.then_inc(s_tr, 1)
                pe.wait_ge(s_y, 1)
                for h in range(2):
                    rows = slice(64 * h, 64 * h + 64)
                    mm = pe.matmul(ps[rows, 1, 0:64], yr[rows, :], ident[rows, rows], start=True, stop=True)
                mm.then_inc(s_yt, 1)

            @block.vector
            def _(dve):
                for n, x in enumerate((r, v, kk, kp, b_, sg)):
                    dve.tensor_copy(packed[:, n, :, :], x[:, :, TP:T].rearrange("p m b -> p b m"))
                link(dve, dve.memset(sa[:, :], 0.0))
                dve.tensor_copy(yr[:, :], sa[:, :]).then_inc(s_pk, 1)
                dve.wait_ge(s_tr, 1)
                dve.tensor_copy(vs[:, :, :].rearrange("p n c -> p (n c)"), ps[:, 0, 0:384]).then_inc(s_cp, 1)
                dve.wait_ge(s_cp, 2)
                dve.wait_ge(s_in, 16)

                def over_i(n):
                    return vs[:, n, :].unsqueeze(1).broadcast_to([P, 64, 64])

                def over_j(x):
                    return x.unsqueeze(2).broadcast_to([P, 64, 64])

                link(dve, dve.tensor_tensor(big[:, :, :], S[:, :, :], over_i(2), ALU.mult))
                dve.tensor_reduce(sa[:, :], big[:, :, :], AX, ALU.add, negate=True)
                link(dve, dve.tensor_tensor(S[:, :, :], S[:, :, :], over_i(5), ALU.mult))
                link(dve, dve.tensor_tensor(big[:, :, :], over_j(sa[:, :]), over_i(4), ALU.mult))
                link(dve, dve.tensor_tensor(S[:, :, :], S[:, :, :], big[:, :, :], ALU.add))
                link(dve, dve.tensor_tensor(big[:, :, :], over_j(vs[:, 1, :]), over_i(3), ALU.mult))
                link(dve, dve.tensor_tensor(S[:, :, :], S[:, :, :], big[:, :, :], ALU.add))
                link(dve, dve.tensor_tensor(big[:, :, :], S[:, :, :], over_i(0), ALU.mult))
                dve.tensor_reduce(yr[:, :], big[:, :, :], AX, ALU.add).then_inc(s_y, 1)
                dve.wait_ge(s_yt, 1)
                dve.tensor_copy(y[:, :, TP:T].rearrange("p m b -> p b m"),
                                ps[:, 1, 0:64].rearrange("p (b m) -> p b m", b=TS))

            @block.scalar
            def _(act):
                act.wait_ge(s_cp, 1)
                act.activation(vs[:, 5, :], vs[:, 5, :], ACT.Exp, scale=DECAY).then_inc(s_cp, 1)


def nsa_prompt(g, uT, cat):
    nc, d, ps, sb, sem, link = g.nc, g.d, g.ps, g.sb, g.sem, g.link
    ident, cst, vcol = g.ident, g.cst, g.vcol
    with ExitStack() as st:
        vnat = sb(st, "vnat", [P, 2, 2, 256])
        gates = sb(st, "gates", [P, 2, 48])
        kcb = sb(st, "kcb", [P, 2, NCB])
        vcb = sb(st, "vcb", [NCB, 4, 64])
        with ExitStack() as s1:
            w1 = sb(s1, "w1", [P, 2, 32, P])
            w2 = sb(s1, "w2", [P, 2, 64])
            hid = sb(s1, "hid", [P, 2, 2, 2, NCB])
            s_in, s_sg, s_mm, s_cp, s_h = (sem(n) for n in ("np_in", "np_gates", "np_mm", "np_copied", "np_hid"))
            with nc.Block() as block:
                @block.sync
                def _(sp):
                    sp.dma_start(w1[:, :, :, :], d["cmp_w1_twice"]).then_inc(s_in, 16)
                    sp.dma_start(w2[:, :, :], d["cmp_w2"]).then_inc(s_in, 16)

                @block.tensor
                def _(pe):
                    for n, c0 in enumerate((C_VS, C_VW)):
                        for t in range(2):
                            for p in range(2):
                                mm = pe.transpose(ps[:, n, (2 * t + p) * P:(2 * t + p + 1) * P],
                                                  uT[:, c0 + p, t * P:(t + 1) * P], ident)
                        mm.then_inc(s_mm, 1)
                    pe.wait_ge(s_sg, 1)
                    for t in range(2):
                        mm = pe.transpose(ps[:, 2, t * 48:t * 48 + 48], uT[0:48, C_GL, t * P:(t + 1) * P],
                                          ident[0:48, 0:48])
                    mm.then_inc(s_mm, 1)
                    pe.wait_ge(s_in, 32)
                    for kv in range(2):
                        for h in range(2):
                            rows = slice(64 * h, 64 * h + 64)
                            for l in range(32):
                                mm = pe.matmul(ps[:, 3 + 2 * kv + h, 0:2 * NCB], w1[rows, kv, l, :],
                                               uT[rows, C_KC + 2 * kv:C_KC + 2 * kv + 2, l:l + 16 * (NCB - 1) + 1:16],
                                               start=(l == 0), stop=(l == 31))
                        mm.then_inc(s_mm, 1)
                    pe.wait_ge(s_h, 4)
                    for h in range(2):
                        for p in range(2):
                            pe.matmul(ps[64 * h:64 * h + 64, 7, p * NCB:(p + 1) * NCB], w2[:, 0, :],
                                      hid[:, 0, h, p, :], start=True, stop=True)
                    for h in range(2):
                        for p in range(2):
                            kh = 2 * p + h
                            mm = pe.matmul(ps[0:NCB, 7, 64 + kh * 64:128 + kh * 64], hid[:, 1, h, p, :],
                                           w2[:, 1, :], start=True, stop=True)
                    mm.then_inc(s_mm, 1)

                @block.scalar
                def _(act):
                    act.activation(uT[0:48, C_GL, :], uT[0:48, C_GL, :], ACT.Sigmoid).then_inc(s_sg, 1)
                    for kv in range(2):
                        act.wait_ge(s_mm, 4 + kv)
                        for h in range(2):
                            act.activation(hid[:, kv, h, :, :],
                                           ps[:, 3 + 2 * kv + h, 0:2 * NCB].rearrange("p (a c) -> p a c", a=2),
                                           ACT.Gelu_apprx_tanh, bias=vcol("b1", kv)).then_inc(s_h, 1)

                @block.vector
                def _(dve):
                    for n in range(2):
                        dve.wait_ge(s_mm, n + 1)
                        dve.tensor_copy(vnat[:, n, :, :].rearrange("p t c -> p (t c)"), ps[:, n, :])
                    dve.wait_ge(s_mm, 3)
                    dve.tensor_copy(gates[:, :, :].rearrange("p t c -> p (t c)"), ps[:, 2, 0:96])
                    dve.wait_ge(s_mm, 6)
                    dve.tensor_copy(kcb[:, :, :].rearrange("p a c -> p (a c)"), ps[:, 7, 0:2 * NCB])
                    dve.tensor_copy(vcb[:, :, :].rearrange("p a c -> p (a c)"), ps[0:NCB, 7, 64:320])

        gates_p = sb(st, "gates_p", [P, 2, 48])
        S = sb(st, "S", [P, 2, 3, TP])
        mx, nm, sm, gr = (sb(st, n, [P, 2, 3]) for n in ("mx", "nm", "sm", "gr"))
        pT = sb(st, "pT", [P, 2, 5, P])
        units = [(p, gq, t, h) for p in range(2) for gq in range(4) for t in range(2) for h in range(2)]
        N = len(units)
        s_pad, s_sc, s_m, s_nm, s_ex, s_p, s_tr, s_pt, s_pv, s_o = (sem(n) for n in (
            "padded", "scores", "masked", "maxima", "exps", "weights", "turned", "turned_copied", "products", "taken"))
        with nc.Block() as block:
            @block.tensor
            def _(pe):
                def scores(u):
                    p, gq, t, h = units[u]
                    rows = slice(64 * h, 64 * h + 64)
                    q = uT[rows, C_Q + 4 * p + gq, t * P:(t + 1) * P]
                    if u >= 2:
                        pe.wait_ge(s_m, u - 1)
                    pe.matmul(ps[:, h, 0:TP], q, uT[rows, C_KS + p, 0:TP], start=True, stop=True)
                    pe.matmul(ps[:, h, TP:2 * TP], q, uT[rows, C_KW + p, 0:TP], start=True, stop=True)
                    pe.matmul(ps[:, 2 + h, 0:NCB], q, kcb[rows, p, :], start=True, stop=True).then_inc(s_sc, 1)

                def turn(u):
                    pe.wait_ge(s_p, u + 1)
                    if u >= 1:
                        pe.wait_ge(s_pt, u)
                    for n in range(4):
                        pe.transpose(ps[:, 4, n * P:(n + 1) * P], S[:, u % 2, n // 2, (n % 2) * P:(n % 2 + 1) * P], ident)
                    pe.transpose(ps[0:NCB, 5, 0:P], S[:, u % 2, 2, 0:NCB], ident).then_inc(s_tr, 1)

                def pv(u):
                    p, gq, t, h = units[u]
                    pe.wait_ge(s_pt, u + 1)
                    pair = u // 2
                    if h == 0 and pair >= 2:
                        pe.wait_ge(s_o, pair - 1)
                    kc = (2 * p + h) * 64
                    out = ps[64 * h:64 * h + 64, 6 + pair % 2, 0:P]
                    for n in range(2):
                        for kt in range(t + 1):
                            pe.matmul(out, vnat[:, n, kt, kc:kc + 64], pT[:, u % 2, 2 * n + kt, :],
                                      start=(n == 0 and kt == 0), stop=False)
                    pe.matmul(out, vcb[:, 2 * p + h, :], pT[0:NCB, u % 2, 4, :], start=False, stop=True).then_inc(s_pv, 1)

                scores(0)
                for u in range(N):
                    if u + 1 < N:
                        scores(u + 1)
                    turn(u)
                    if u >= 1:
                        pv(u - 1)
                pv(N - 1)

            @block.vector
            def _(dve):
                def first(u):
                    p, gq, t, h = units[u]
                    dve.wait_ge(s_sc, u + 1)
                    if u >= 2:
                        dve.wait_ge(s_tr, u - 1)
                    mask = cst("causal")[:, t * TP:(t + 1) * TP].unsqueeze(1).broadcast_to([P, 2, TP])
                    dve.tensor_tensor(S[:, u % 2, 0:2, :], ps[:, h, :].rearrange("p (a k) -> p a k", a=2), mask, ALU.add)
                    dve.tensor_tensor(S[:, u % 2, 2, 0:NCB], ps[:, 2 + h, 0:NCB],
                                      cst("cmask")[:, t * NCB:(t + 1) * NCB], ALU.add).then_inc(s_m, 1)
                    dve.wait_ge(s_m, u + 1)
                    link(dve, dve.tensor_reduce(mx[:, u % 2, :], S[:, u % 2, :, :], AX, ALU.max))
                    dve.tensor_scalar(nm[:, u % 2, :], mx[:, u % 2, :], -0.125, None, ALU.mult).then_inc(s_nm, 1)

                def second(u):
                    p, gq, t, h = units[u]
                    a = ((2 * p + h) * 4 + gq) * 3
                    dve.wait_ge(s_ex, u + 1)
                    link(dve, dve.reciprocal(gr[:, u % 2, :], sm[:, u % 2, :]))
                    link(dve, dve.tensor_tensor(gr[:, u % 2, :], gr[:, u % 2, :], gates_p[:, t, a:a + 3], ALU.mult))
                    dve.tensor_scalar(S[:, u % 2, 2, 0:NCB], S[:, u % 2, 2, 0:NCB], gr[:, u % 2, 2:3], None, ALU.mult)
                    dve.tensor_tensor(S[:, u % 2, 0:2, :], S[:, u % 2, 0:2, :],
                                      gr[:, u % 2, 0:2].unsqueeze(2).broadcast_to([P, 2, TP]), ALU.mult
                                      ).then_inc(s_p, 1)

                for t in range(2):
                    src = gates[:, t, :].rearrange("p (h n) -> p h n", n=3)
                    dst = gates_p[:, t, :].rearrange("p (h n) -> p h n", n=3)
                    dve.tensor_copy(dst[:, :, 0:2], src[:, :, 1:3])
                    dve.tensor_scalar(dst[:, :, 2], src[:, :, 0], cst("cvalid")[:, t:t + 1], None, ALU.mult)
                link(dve, dve.memset(S[:, :, 2, :], NEG))
                for u in range(N + 1):
                    if u < N:
                        first(u)
                    if u >= 1:
                        second(u - 1)

            @block.scalar
            def _(act):
                def exps(u):
                    act.wait_ge(s_nm, u + 1)
                    for n, w in enumerate((TP, TP, NCB)):
                        ins = act.activation(S[:, u % 2, n, 0:w], S[:, u % 2, n, 0:w], ACT.Exp, scale=0.125,
                                             bias=nm[:, u % 2, n:n + 1], accum_out=sm[:, u % 2, n:n + 1])
                    ins.then_inc(s_ex, 1)

                def copy(u):
                    act.wait_ge(s_tr, u + 1)
                    if u >= 2:
                        act.wait_ge(s_pv, u - 1)
                    act.activation(pT[:, u % 2, 0:4, :].rearrange("p n t -> p (n t)"), ps[:, 4, :], ACT.Copy)
                    act.activation(pT[0:NCB, u % 2, 4, :], ps[0:NCB, 5, 0:P], ACT.Copy).then_inc(s_pt, 1)

                def take(pair):
                    p, gq, t, _ = units[2 * pair]
                    act.wait_ge(s_pv, 2 * pair + 2)
                    act.activation(cat[:, 8 + 4 * p + gq, t * P:(t + 1) * P], ps[:, 6 + pair % 2, 0:P],
                                   ACT.Copy).then_inc(s_o, 1)

                for u in range(N + 2):
                    if u < N:
                        exps(u)
                    if 1 <= u <= N:
                        copy(u - 1)
                    if u >= 3 and u % 2 == 1:
                        take((u - 3) // 2)


def nsa_sample(g, uT, cat):
    nc, d, ps, sb, sem, link, alink = g.nc, g.d, g.ps, g.sb, g.sem, g.link, g.alink
    ident, ones, cst, vcol = g.ident, g.ones, g.cst, g.vcol
    PW = 2 * P
    with ExitStack() as st:
        Q = sb(st, "Q", [P, 16 * P])
        vcb = sb(st, "vcb", [P, 8, 256])
        gate = sb(st, "gate", [P, 3])
        ptab = sb(st, "ptab", [1, P], I32)
        SLOTS = 5
        s_q, s_g, s_t, s_ge = sem("q_zero"), sem("gate_mm"), sem("table_in"), sem("gate_rows")
        with ExitStack() as s1:
            t8 = sb(s1, "t8", [P, 3, 8])
            with nc.Block() as block:
                @block.sync
                def _(sp):
                    sp.dma_start(ptab[:, :], d["page_table"]).then_inc(s_t, 16)
                    sp.wait_ge(s_t, 16)

                @block.tensor
                def _(pe):
                    for n in range(3):
                        mm = pe.matmul(ps[:, 0, 8 * n:8 * n + 8], cst("gate", 48)[:, n * P:(n + 1) * P],
                                       uT[0:48, C_GL, TP:T], start=True, stop=True)
                    mm.then_inc(s_g, 1)

                @block.vector
                def _(dve):
                    link(dve, dve.memset(Q[:, :], 0.0))
                    for p in range(2):
                        for h in range(2):
                            for gq in range(4):
                                a = p * 1088 + h * 4 + gq
                                rows = slice(64 * h, 64 * h + 64)
                                dve.tensor_copy(Q[rows, a:a + 136 * 7 + 1:136], uT[rows, C_Q + 4 * p + gq, TP:T])
                    dve.wait_ge(s_g, 1)
                    link(dve, dve.tensor_tensor(t8[:, :, :], ps[:, 0, 0:24].rearrange("p (n b) -> p n b", n=3),
                                                cst("bsel").unsqueeze(1).broadcast_to([P, 3, 8]), ALU.mult))
                    dve.tensor_reduce(gate[:, :], t8[:, :, :], AX, ALU.add)

        def q_of(p, b):
            n = p * 8 + b
            return Q[:, n * P:(n + 1) * P]

        with ExitStack() as s1:
            pages = sb(s1, "pages", [P, SLOTS, PG, PW])
            w1 = sb(s1, "w1", [P, 2, 16, P])
            w2 = sb(s1, "w2", [P, 2, 64])
            lo = sb(s1, "lo", [P, 512])
            hs = sb(s1, "hs", [P, 4, NCS])
            hid = sb(s1, "hid", [P, 4, NCS])
            kcb = sb(s1, "kcb", [P, 2, NCS])
            s_in = sem("weights_in")
            s_pg = [sem(f"pages{k}") for k in range(SLOTS)]
            s_done, s_lh, s_lo, s_hs, s_hid, s_cb, s_cbc, s_c = (sem(n) for n in (
                "pages_used", "lohi", "lo_copied", "sums", "hidden", "compressed", "compressed_copied", "c_scores"))
            with nc.Block() as block:
                @block.sync
                def _(sp):
                    sp.dma_start(w1[:, :, :, :], d["cmp_w1"]).then_inc(s_in, 16)
                    sp.dma_start(w2[:, :, :], d["cmp_w2"]).then_inc(s_in, 16)
                    for b in range(TS):
                        slots = []
                        for which in range(3):
                            n = 3 * b + which
                            if n >= SLOTS:
                                sp.wait_ge(s_done, n - SLOTS + 1)
                            slots.append(n % SLOTS)
                        with sp.Fori(0, PG) as j:
                            page = sp.value_load(ptab[0:1, ds(j + b * PG, 1)], min_val=0, max_val=N_PHYS - 1)
                            for which, name in enumerate(("cmp_k", "cmp_v", "slc_k")):
                                sp.dma_start(pages[:, slots[which], ds(j, 1), :],
                                             d[name][ds(page, 1), :, :].rearrange("a p n -> p a n")
                                             ).then_inc(s_pg[slots[which]], 16)

                @block.tensor
                def _(pe):
                    def arrived(n):
                        pe.wait_ge(s_pg[n % SLOTS], 16 * PG * (n // SLOTS + 1))

                    pe.wait_ge(s_in, 32)
                    for b in range(TS):
                        for kv in range(2):
                            n, m = 3 * b + kv, 2 * b + kv
                            arrived(n)
                            if m >= 1:
                                pe.wait_ge(s_hs, m)
                            for part in range(2):
                                for l in range(8):
                                    chs = pages[:, n % SLOTS, :, l * 32:(l + 1) * 32].rearrange(
                                        "p g (k c) -> p k g c", k=4)
                                    mm = pe.matmul(ps[:, 5 + part, :], w1[:, kv, 8 * part + l, :], chs,
                                                   start=(l == 0), stop=(l == 7))
                                mm.then_inc(s_lh, 1)
                            if kv == 1:
                                pe.wait_ge(s_lh, 2 * m + 2)
                            pe.wait_ge(s_hid, m + 1)
                            if kv == 0:
                                for kh in range(4):
                                    mm = pe.matmul(ps[64 * (kh % 2):64 * (kh % 2) + 64, 7,
                                                      (kh // 2) * P:(kh // 2) * P + NCS],
                                                   w2[:, 0, :], hid[:, kh, :], start=True, stop=True)
                                mm.then_inc(s_cb, 1)
                                pe.wait_ge(s_cbc, m + 1)
                                for p in range(2):
                                    mm = pe.matmul(ps[:, 4, 0:NCS], q_of(p, b), kcb[:, p, :],
                                                   start=(b == 0 and p == 0), stop=(b == TS - 1 and p == 1))
                                mm.then_inc(s_c, 1)
                            else:
                                for kh in range(4):
                                    mm = pe.matmul(ps[0:NCS, 7, 256 + kh * 64:320 + kh * 64], hid[:, kh, :],
                                                   w2[:, 1, :], start=True, stop=True)
                                mm.then_inc(s_cb, 1)
                                pe.wait_ge(s_cbc, m + 1)
                        n = 3 * b + 2
                        arrived(n)
                        for p in range(2):
                            for q in range(4):
                                mm = pe.matmul(ps[:, q, :], q_of(p, b),
                                               pages[:, n % SLOTS, 4 * q:4 * q + 4, p * P:(p + 1) * P],
                                               start=(b == 0 and p == 0), stop=(b == TS - 1 and p == 1))
                        mm.then_inc(s_done, 3)

                @block.scalar
                def _(act):
                    for m in range(2 * TS):
                        act.wait_ge(s_lh, 2 * m + 1)
                        act.activation(lo[:, :], ps[:, 5, :], ACT.Copy).then_inc(s_lo, 1)
                        act.wait_ge(s_hs, m + 1)
                        act.activation(hid[:, :, :], hs[:, :, :], ACT.Gelu_apprx_tanh, bias=vcol("b1", m % 2)
                                       ).then_inc(s_hid, 1)

                @block.vector
                def _(dve):
                    for m in range(2 * TS):
                        dve.wait_ge(s_lh, 2 * m + 2)
                        dve.wait_ge(s_lo, m + 1)
                        dve.tensor_tensor(hs[:, :, :], ps[:, 6, :].rearrange("p (k c) -> p k c", k=4)[:, :, 1:P],
                                          lo[:, :].rearrange("p (k c) -> p k c", k=4)[:, :, 0:NCS], ALU.add
                                          ).then_inc(s_hs, 1)
                        dve.wait_ge(s_cb, m + 1)
                        if m % 2 == 0:
                            if m >= 2:
                                dve.wait_ge(s_c, m // 2)
                            dve.tensor_copy(kcb[:, :, :], ps[:, 7, 0:256].rearrange("p (a c) -> p a c", a=2)[:, :, 0:NCS]
                                            ).then_inc(s_cbc, 1)
                        else:
                            dve.tensor_copy(vcb[0:NCS, m // 2, :], ps[0:NCS, 7, 256:512]).then_inc(s_cbc, 1)

        with ExitStack() as s1:
            wk = sb(s1, "wk", [P, TS, 2, 512])
            s_in, s_new, s_w = sem("window_in"), sem("window_new"), sem("window_scores")
            with nc.Block() as block:
                @block.sync
                def _(sp):
                    sp.dma_start(wk[:, :, :, :], d["win_k"]).then_inc(s_in, 16)

                @block.vector
                def _(dve):
                    dve.wait_ge(s_in, 16)
                    dve.tensor_copy(wk[:, :, :, 0], uT[:, C_KW:C_KW + 2, TP:T].rearrange("p a b -> p b a")
                                    ).then_inc(s_new, 1)

                @block.tensor
                def _(pe):
                    pe.wait_ge(s_new, 1)
                    for b in range(TS):
                        for p in range(2):
                            pe.matmul(ps[:, 5, :], q_of(p, b), wk[:, b, p, :],
                                      start=(b == 0 and p == 0), stop=(b == TS - 1 and p == 1))
                            pe.matmul(ps[:, 6, 0:1], q_of(p, b), uT[:, C_KS + p, TP + b:TP + b + 1],
                                      start=(b == 0 and p == 0), stop=(b == TS - 1 and p == 1))

        A_W, A_C, A_N, A_E = 2048, 2560, 2560 + NCS, 2560 + P
        W = sb(st, "W", [P, A_E])
        pT = sb(st, "pT", [P, 21, P])
        nm, sm, gr = (sb(st, n, [P, 3]) for n in ("nm", "sm", "gr"))
        with ExitStack() as s1:
            imp = sb(s1, "imp", [32, 4 * NBLK + 4])
            ims = sb(s1, "ims", [32, NBLK])
            wk2 = sb(s1, "wk2", [32, NBLK])
            t8 = sb(s1, "t8", [32, 8])
            blk = sb(s1, "blk", [P, NBLK])
            s_v, s_a, s_p = sem("nm_ready"), sem("exp_ready"), sem("pe_ready")
            with nc.Block() as block:
                @block.vector
                def _(dve):
                    link(dve, dve.tensor_copy(W[:, A_C:A_C + NCS], ps[:, 4, 0:NCS]))
                    link(dve, dve.tensor_reduce(nm[:, 0:1], W[:, A_C:A_C + NCS], AX, ALU.max))
                    dve.tensor_scalar(nm[:, 0:1], nm[:, 0:1], -0.125, None, ALU.mult).then_inc(s_v, 1)
                    dve.memset(imp[:, :], 0.0)
                    dve.wait_ge(s_a, 1)
                    link(dve, dve.reciprocal(gr[:, 0:1], sm[:, 0:1]))
                    dve.tensor_scalar(W[:, A_C:A_C + NCS], W[:, A_C:A_C + NCS], gr[:, 0:1], None, ALU.mult
                                      ).then_inc(s_v, 1)
                    dve.wait_ge(s_p, 1)
                    link(dve, dve.tensor_copy(imp[:, 1:NCS + 1], ps[0:32, 7, 0:NCS]))
                    quad = imp[:, 0:4 * NBLK].rearrange("p (j q) -> p j q", q=4)
                    nxt = imp[:, 4:4 * NBLK + 4].rearrange("p (j q) -> p j q", q=4)
                    dve.tensor_tensor(wk2[:, :], quad[:, :, 0], nxt[:, :, 0], ALU.add)
                    link(dve, dve.tensor_reduce(ims[:, :], quad[:, :, 1:4], AX, ALU.add))
                    link(dve, dve.scalar_tensor_tensor(ims[:, :], wk2[:, :], 0.5, ims[:, :], ALU.mult, ALU.add))
                    dve.memset(ims[:, 0:1], 1e30)
                    link(dve, dve.memset(ims[:, NBLK - 2:NBLK], 1e30))
                    link(dve, dve.max(t8[:, :], ims[:, :]))
                    link(dve, dve.match_replace(wk2[:, :], t8[:, :], ims[:, :], -3e38))
                    link(dve, dve.max(t8[:, :], wk2[:, :]))
                    link(dve, dve.match_replace(ims[:, :], t8[:, :], wk2[:, :], -3e38))
                    dve.tensor_scalar(wk2[:, :], ims[:, :], -2e38, None, ALU.is_lt).then_inc(s_v, 1)
                    dve.wait_ge(s_p, 2)
                    link(dve, dve.tensor_scalar(blk[:, :], ps[:, 7, P:P + NBLK], -1.0, -NEG, ALU.add, ALU.mult))
                    for q in range(4):
                        dve.tensor_tensor(W[:, 512 * q:512 * q + 512].rearrange("p (j l) -> p j l", l=64),
                                          ps[:, q, :].rearrange("p (j l) -> p j l", l=64),
                                          blk[:, 8 * q:8 * q + 8].unsqueeze(2).broadcast_to([P, 8, 64]), ALU.add)
                    dve.tensor_copy(W[:, A_W:A_C], ps[:, 5, :])
                    link(dve, dve.tensor_copy(W[:, A_N:A_E], ps[:, 6, 0:1]))
                    dve.tensor_reduce(nm[:, 1:2], W[:, 0:A_W], AX, ALU.max)
                    link(dve, dve.tensor_reduce(nm[:, 2:3], W[:, A_W:A_C], AX, ALU.max))
                    link(dve, dve.tensor_tensor(nm[:, 1:2], nm[:, 1:2], W[:, A_N:A_E], ALU.max))
                    dve.tensor_scalar(nm[:, 1:3], nm[:, 1:3], -0.125, None, ALU.mult).then_inc(s_v, 1)
                    dve.wait_ge(s_a, 2)
                    link(dve, dve.tensor_tensor(sm[:, 1:2], sm[:, 1:2], W[:, A_N:A_E], ALU.add))
                    link(dve, dve.reciprocal(gr[:, 1:3], sm[:, 1:3]))
                    link(dve, dve.tensor_tensor(gr[:, 1:3], gr[:, 1:3], gate[:, 1:3], ALU.mult))
                    dve.tensor_scalar(W[:, 0:A_W], W[:, 0:A_W], gr[:, 1:2], None, ALU.mult)
                    dve.tensor_scalar(W[:, A_N:A_E], W[:, A_N:A_E], gr[:, 1:2], None, ALU.mult)
                    dve.tensor_scalar(W[:, A_W:A_C], W[:, A_W:A_C], gr[:, 2:3], None, ALU.mult)
                    dve.tensor_scalar(W[:, A_C:A_N], W[:, A_C:A_N], gate[:, 0:1], None, ALU.mult)

                @block.scalar
                def _(act):
                    act.wait_ge(s_v, 1)
                    act.activation(W[:, A_C:A_N], W[:, A_C:A_N], ACT.Exp, scale=0.125, bias=nm[:, 0:1],
                                   accum_out=sm[:, 0:1]).then_inc(s_a, 1)
                    act.wait_ge(s_v, 4)
                    act.activation(W[:, 0:A_W], W[:, 0:A_W], ACT.Exp, scale=0.125, bias=nm[:, 1:2],
                                   accum_out=sm[:, 1:2])
                    act.activation(W[:, A_N:A_E], W[:, A_N:A_E], ACT.Exp, scale=0.125, bias=nm[:, 1:2])
                    act.activation(W[:, A_W:A_C], W[:, A_W:A_C], ACT.Exp, scale=0.125, bias=nm[:, 2:3],
                                   accum_out=sm[:, 2:3]).then_inc(s_a, 1)

                @block.tensor
                def _(pe):
                    pe.wait_ge(s_v, 2)
                    pe.matmul(ps[0:32, 7, 0:NCS], cst("gsum"), W[:, A_C:A_N], start=True, stop=True).then_inc(s_p, 1)
                    pe.wait_ge(s_v, 3)
                    pe.matmul(ps[:, 7, P:P + NBLK], cst("gexp", 32), wk2[:, :], start=True, stop=True).then_inc(s_p, 1)

        with ExitStack() as s1:
            pages = sb(s1, "vpages", [P, 2, PG, PW])
            wv = sb(s1, "wv", [P, TS, 4, PW])
            diag = sb(s1, "diag", [P, 2, P])
            o = sb(s1, "o", [P, P])
            t = sb(s1, "t", [P, P])
            t2 = sb(s1, "t2", [P, P])
            s_in, s_d, s_tr, s_cp, s_pv, s_o, s_z = (sem(n) for n in (
                "wv_in", "diag_made", "w_turned", "w_copied", "pv_done", "o_copied", "zeroed"))
            s_pg = [sem(f"vpages{k}") for k in range(2)]
            with nc.Block() as block:
                @block.sync
                def _(sp):
                    sp.dma_start(wv[:, :, :, :], d["win_v"]).then_inc(s_in, 16)
                    for b in range(TS):
                        if b >= 2:
                            sp.wait_ge(s_pv, b - 1)
                        with sp.Fori(0, PG) as j:
                            page = sp.value_load(ptab[0:1, ds(j + b * PG, 1)], min_val=0, max_val=N_PHYS - 1)
                            sp.dma_start(pages[:, b % 2, ds(j, 1), :],
                                         d["slc_v"][ds(page, 1), :, :].rearrange("a p n -> p a n")
                                         ).then_inc(s_pg[b % 2], 16)

                @block.tensor
                def _(pe):
                    pe.wait_ge(s_d, 1)
                    for n in range(2):
                        pe.matmul(ps[:, 6, n * P:(n + 1) * P], ones, diag[:, n, :], start=True, stop=True)
                    for n in range(21):
                        if n % 4 == 0 and n >= 8:
                            pe.wait_ge(s_cp, n // 4 - 1)
                        w = P if n < 20 else NCS
                        mm = pe.transpose(ps[0:w, (n // 4) % 2, (n % 4) * P:(n % 4 + 1) * P], W[:, n * P:n * P + w], ident)
                        if n % 4 == 3 or n == 20:
                            mm.then_inc(s_tr, 1)
                    pe.wait_ge(s_cp, 6)
                    pe.wait_ge(s_in, 16)
                    for b in range(TS):
                        pe.wait_ge(s_pg[b % 2], 16 * PG * (b // 2 + 1))
                        for p in range(2):
                            cols = slice(p * 64 + b * 8, p * 64 + b * 8 + 8)
                            pc = slice(p * P, (p + 1) * P)
                            for n in range(16):
                                pe.matmul(ps[:, 7, cols], pages[:, b % 2, n, pc], pT[:, n, cols],
                                          start=(n == 0), stop=False)
                            for n in range(4):
                                pe.matmul(ps[:, 7, cols], wv[:, b, n, pc], pT[:, 16 + n, cols], start=False, stop=False)
                            mm = pe.matmul(ps[:, 7, cols], vcb[0:NCS, b, pc], pT[0:NCS, 20, cols],
                                           start=False, stop=True)
                        mm.then_inc(s_pv, 1)

                @block.vector
                def _(dve):
                    dve.tensor_scalar(diag[:, 0, :], ident, W[:, A_N:A_E], None, ALU.mult)
                    link(dve, dve.tensor_scalar(diag[:, 1, :], ident, W[:, A_W:A_W + 1], None, ALU.mult))
                    dve.memset(W[:, A_W:A_W + 1], 0.0).then_inc(s_d, 1)
                    for n in range(6):
                        dve.wait_ge(s_tr, n + 1)
                        k = 4 if n < 5 else 1
                        w = P if n < 5 else NCS
                        dve.tensor_copy(pT[0:w, 4 * n:4 * n + k, :].rearrange("p n t -> p (n t)"), ps[0:w, n % 2, 0:k * P]
                                        ).then_inc(s_cp, 1)
                    for n, (c0, dst) in enumerate(((C_VS, t), (C_VW, t2))):
                        new = uT[:, c0:c0 + 2, TP:T]
                        dve.tensor_tensor(dst[:, :].rearrange("p (a b r) -> p a b r", a=2, b=8),
                                          ps[:, 6, n * P:(n + 1) * P].rearrange("p (a b r) -> p a b r", a=2, b=8),
                                          new.unsqueeze(3).broadcast_to([P, 2, 8, 8]), ALU.mult)
                    link(dve, dve.memset(o[:, 0:1], 0.0))
                    dve.wait_ge(s_pv, TS)
                    link(dve, dve.tensor_tensor(t[:, :], t[:, :], t2[:, :], ALU.add))
                    link(dve, dve.tensor_tensor(o[:, :], ps[:, 7, 0:P], t[:, :], ALU.add))
                    for p in range(2):
                        for h in range(2):
                            rows = slice(64 * h, 64 * h + 64)
                            src = o[rows, 64 * p:64 * p + 64].rearrange("q (b k e) -> q k e b", b=8, k=2)[:, h]
                            dve.tensor_copy(cat[rows, 8 + 4 * p:12 + 4 * p, TP:T], src)


def cross(g, memk, memv, xT):
    nc, d, ps, sb, sem, link = g.nc, g.d, g.ps, g.sb, g.sem, g.link
    ident, cst = g.ident, g.cst
    SC = float(P) ** -0.5
    with ExitStack() as st:
        qx = sb(st, "qx", [P, 4, T])
        ox = sb(st, "ox", [P, 4, T])
        with ExitStack() as s1:
            hx = sb(s1, "hx", [P, KC, T])
            ring = sb(s1, "ring", [P, RING, D])
            g.rms(xT, hx, "x", KC, T)
            g.project(d["xq"], hx, qx, 4, ring)
        wo = sb(st, "wo", [P, 4, D])
        ck = sb(st, "ck", [P, TS, 4, TP])
        cv = sb(st, "cv", [P, TS, 2, 512])
        Q = sb(st, "Q", [P, 32 * 32])
        S = sb(st, "S", [P, 9, TP])
        pT = sb(st, "pT", [P, 9, 2, P])
        mx, nm, sm, rs = (sb(st, n, [P, 9]) for n in ("mx", "nm", "sm", "rs"))
        s_in, s_q, s_sc, s_nm, s_ex, s_p, s_tr, s_cp, s_pv, s_o = (sem(n) for n in (
            "x_in", "x_q", "x_scores", "x_max", "x_exp", "x_weights", "x_turned", "x_copied", "x_products", "x_taken"))
        with nc.Block() as block:
            @block.sync
            def _(sp):
                sp.dma_start(ck[:, :, :, :], d["mem_k"]).then_inc(s_in, 16)
                sp.dma_start(cv[:, :, :, :], d["mem_v"]).then_inc(s_in, 16)
                sp.dma_start(wo[:, :, :], d["xo"]).then_inc(s_in, 16)

            @block.tensor
            def _(pe):
                for u in range(8):
                    h, t = u // 2, u % 2
                    pe.matmul(ps[:, u // 2, t * TP:(t + 1) * TP], qx[:, h, t * P:(t + 1) * P], memk[:, h, :],
                              start=True, stop=True).then_inc(s_sc, 1)
                pe.wait_ge(s_in, 48)
                pe.wait_ge(s_q, 1)
                for n in range(32):
                    mm = pe.matmul(ps[0:32, 4, 0:TP], Q[:, n * 32:(n + 1) * 32], ck[:, n // 4, n % 4, :],
                                   start=(n == 0), stop=(n == 31))
                mm.then_inc(s_sc, 1)
                for u in range(9):
                    r = P if u < 8 else 32
                    pe.wait_ge(s_p, u + 1)
                    if u >= 2:
                        pe.wait_ge(s_cp, u - 1)
                    for m in range(2):
                        mm = pe.transpose(ps[:, 5 + u % 2, m * P:m * P + r], S[0:r, u, m * P:(m + 1) * P], ident[0:r, 0:r])
                    mm.then_inc(s_tr, 1)
                for u in range(8):
                    h = u // 2
                    pe.wait_ge(s_cp, u + 1)
                    if u >= 4:
                        pe.wait_ge(s_o, u - 3)
                    for m in range(2):
                        mm = pe.matmul(ps[:, u % 4, 0:P], memv[:, m, h * P:(h + 1) * P], pT[:, u, m, :],
                                       start=(m == 0), stop=(m == 1))
                    mm.then_inc(s_pv, 1)
                pe.wait_ge(s_cp, 9)
                for n in range(32):
                    b, h = n // 4, n % 4
                    for m in range(2):
                        mm = pe.matmul(ps[:, 7, n:n + 1], cv[:, b, m, h * P:(h + 1) * P], pT[:, 8, m, n:n + 1],
                                       start=(m == 0), stop=(m == 1))
                mm.then_inc(s_pv, 1)

            @block.vector
            def _(dve):
                link(dve, dve.memset(Q[:, :], 0.0))
                dve.tensor_copy(Q[:, 0:33 * 31 + 1:33].rearrange("p (b h) -> p b h", h=4),
                                qx[:, :, TP:T].rearrange("p h b -> p b h")).then_inc(s_q, 1)
                for u in range(9):
                    r = P if u < 8 else 32
                    src = ps[0:r, u // 2, (u % 2) * TP:(u % 2 + 1) * TP]
                    dve.wait_ge(s_sc, min(2 * (u // 2) + 2, 9))
                    link(dve, dve.tensor_reduce(mx[0:r, u:u + 1], src, AX, ALU.max))
                    dve.tensor_scalar(nm[0:r, u:u + 1], mx[0:r, u:u + 1], -SC, None, ALU.mult).then_inc(s_nm, 1)
                for u in range(9):
                    r = P if u < 8 else 32
                    dve.wait_ge(s_ex, u + 1)
                    link(dve, dve.reciprocal(rs[0:r, u:u + 1], sm[0:r, u:u + 1]))
                    dve.tensor_scalar(S[0:r, u, :], S[0:r, u, :], rs[0:r, u:u + 1], None, ALU.mult).then_inc(s_p, 1)
                for u in range(9):
                    r = P if u < 8 else 32
                    dve.wait_ge(s_tr, u + 1)
                    dve.tensor_copy(pT[:, u, :, 0:r], ps[:, 5 + u % 2, 0:TP].rearrange("p (m t) -> p m t", m=2)[:, :, 0:r]
                                    ).then_inc(s_cp, 1)
                for u in range(8):
                    dve.wait_ge(s_pv, u + 1)
                    dve.tensor_copy(ox[:, u // 2, (u % 2) * P:(u % 2 + 1) * P], ps[:, u % 4, 0:P]).then_inc(s_o, 1)
                dve.wait_ge(s_pv, 9)
                dve.tensor_copy(ox[:, :, TP:T].rearrange("p h b -> p b h"),
                                ps[:, 7, 0:32].rearrange("p (b h) -> p b h", h=4))

            @block.scalar
            def _(act):
                for u in range(9):
                    r = P if u < 8 else 32
                    act.wait_ge(s_nm, min(2 * (u // 2) + 2, 9))
                    act.activation(S[0:r, u, :], ps[0:r, u // 2, (u % 2) * TP:(u % 2 + 1) * TP], ACT.Exp, scale=SC,
                                   bias=nm[0:r, u:u + 1], accum_out=sm[0:r, u:u + 1]).then_inc(s_ex, 1)

        s_mm, s_add = sem("xo_products"), sem("xo_added")
        with nc.Block() as block:
            @block.tensor
            def _(pe):
                for m in range(KC):
                    if m >= 4:
                        pe.wait_ge(s_add, m - 3)
                    for c in range(4):
                        mm = pe.matmul(ps[:, m % 4, 0:T], wo[:, c, m * P:(m + 1) * P], ox[:, c, :],
                                       start=(c == 0), stop=(c == 3))
                    mm.then_inc(s_mm, 1)

            @block.vector
            def _(dve):
                for m in range(KC):
                    dve.wait_ge(s_mm, m + 1)
                    dve.tensor_tensor(xT[:, m, :], ps[:, m % 4, 0:T], xT[:, m, :], ALU.add).then_inc(s_add, 1)


def peer(g, xT):
    nc, d, ps, sb, sem, link = g.nc, g.d, g.ps, g.sb, g.sem, g.link
    ident, cst = g.ident, g.cst
    landed, used, drained, rounds = g.landed, g.used, g.drained, g.rounds
    g.stores([(d["residual"], xT[:, :, :])])
    g.rms(xT, xT, "ffn", KC, T)
    with ExitStack() as st:
        iT, jT, gT = (sb(st, n, [P, T]) for n in ("iT", "jT", "gT"))
        choose(g, xT, iT, jT, gT)
        G = sb(st, "G", [P, P, T])
        spread(g, iT, jT, gT, G)
        with ExitStack() as s1:
            ring = sb(s1, "ring", [P, RING, D])
            u_stage(g, xT, G, ring)
            g.loads([(xT[:, :, :], d["residual"])])
            v_stage(g, xT, G, ring)


def choose(g, hf, iT, jT, gT):
    nc, d, ps, sb, sem, link = g.nc, g.d, g.ps, g.sb, g.sem, g.link
    ident, cst = g.ident, g.cst
    LOW = -3e38
    with ExitStack() as st:
        q = sb(st, "q", [P, 16, T])
        with ExitStack() as s1:
            ring = sb(s1, "ring", [P, RING, D])
            g.project(d["peer_wq"], hf, q, 16, ring)
        keys = sb(st, "keys", [P, 16, P])
        s = sb(st, "s", [P, 16, P])
        s2 = sb(st, "s2", [P, 16, P])
        sv = sb(st, "sv", [P, 16, 16])
        si = sb(st, "si", [P, 16, 16], U32)
        sf = sb(st, "sf", [P, 16, 16])
        cand = sb(st, "cand", [P, 8, 256])
        cand2 = sb(st, "cand2", [P, 8, 256])
        cv = sb(st, "cv", [P, 8, 16])
        ci = sb(st, "ci", [P, 8, 16], U32)
        hl = sb(st, "hl", [P, 2, P], U32)
        hf2 = sb(st, "hf2", [P, 2, P])
        hot = sb(st, "hot", [P, P, 16])
        res = sb(st, "res", [P, 3, P])
        z = sb(st, "z", [P, 8])
        g.loads([(keys[:, :, :], d["peer_keys"])])
        s_mm, s_cp, s_v, s_e, s_r, s_tr = (sem(n) for n in (
            "key_scores", "scores_copied", "shifted", "exps", "choices", "choices_turned"))
        with nc.Block() as block:
            tiles_ = [(0, P), (P, P), (TP, TS)]

            @block.tensor
            def _(pe):
                for t, (a, n) in enumerate(tiles_):
                    if t >= 1:
                        pe.wait_ge(s_cp, t)
                    for c in range(16):
                        mm = pe.matmul(ps[0:n, c // 4, (c % 4) * P:(c % 4 + 1) * P], q[:, c, a:a + n], keys[:, c, :],
                                       start=True, stop=True)
                    mm.then_inc(s_mm, 1)
                    pe.wait_ge(s_r, t + 1)
                    for k in range(3):
                        mm = pe.transpose(ps[:, 4, k * P:k * P + n], res[0:n, k, :], ident[0:n, 0:n])
                    mm.then_inc(s_tr, 1)

            @block.scalar
            def _(act):
                for t, (a, n) in enumerate(tiles_):
                    act.wait_ge(s_mm, t + 1)
                    if t >= 1:
                        act.wait_ge(s_r, t)
                    for c in range(4):
                        ins = act.activation(s[0:n, 4 * c:4 * c + 4, :].rearrange("p a k -> p (a k)"), ps[0:n, c, :], ACT.Copy)
                    ins.then_inc(s_cp, 1)
                    act.wait_ge(s_v, t + 1)
                    act.activation(res[0:n, 2, :], res[0:n, 2, :], ACT.Exp).then_inc(s_e, 1)

            @block.vector
            def _(dve):
                def top16(n, x, y, vals, idx, count):
                    for c in range(count):
                        last = dve.max(vals[0:n, c, 0:8], x[0:n, c, :])
                    link(dve, last)
                    for c in range(count):
                        dve.max_index(idx[0:n, c, 0:8], vals[0:n, c, 0:8], x[0:n, c, :])
                        last = dve.match_replace(y[0:n, c, :], vals[0:n, c, 0:8], x[0:n, c, :], LOW)
                    link(dve, last)
                    for c in range(count):
                        last = dve.max(vals[0:n, c, 8:16], y[0:n, c, :])
                    link(dve, last)
                    for c in range(count):
                        last = dve.max_index(idx[0:n, c, 8:16], vals[0:n, c, 8:16], y[0:n, c, :])
                    link(dve, last)

                for t, (a, n) in enumerate(tiles_):
                    dve.wait_ge(s_cp, t + 1)
                    top16(n, s, s2, sv, si, 16)
                    dve.tensor_copy(sf[0:n, :, :], si[0:n, :, :])
                    for h in range(8):
                        last = dve.tensor_tensor(cand[0:n, h, :].rearrange("p (i j) -> p i j", j=16),
                                                 sv[0:n, 2 * h, :].unsqueeze(2).broadcast_to([n, 16, 16]),
                                                 sv[0:n, 2 * h + 1, :].unsqueeze(1).broadcast_to([n, 16, 16]), ALU.add)
                    link(dve, last)
                    top16(n, cand, cand2, cv, ci, 8)
                    if t >= 1:
                        dve.wait_ge(s_tr, t)
                    dve.tensor_tensor(res[0:n, 2, :].rearrange("p (h k) -> p h k", k=16), cv[0:n, :, :],
                                      cv[0:n, :, 0:1].broadcast_to([n, 8, 16]), ALU.subtract).then_inc(s_v, 1)
                    flat = ci[0:n, :, :].rearrange("p h k -> p (h k)")
                    dve.tensor_scalar(hl[0:n, 0, :], flat, 4, None, ALU.logical_shift_right)
                    link(dve, dve.tensor_scalar(hl[0:n, 1, :], flat, 15, None, ALU.bitwise_and))
                    link(dve, dve.tensor_copy(hf2[0:n, :, :], hl[0:n, :, :]))
                    for k in range(2):
                        link(dve, dve.tensor_tensor(hot[0:n, :, :], hf2[0:n, k, :].unsqueeze(2).broadcast_to([n, P, 16]),
                                                    cst("i16")[0:n, :].unsqueeze(1).broadcast_to([n, P, 16]), ALU.is_equal))
                        for h in range(8):
                            last = dve.tensor_tensor(hot[0:n, 16 * h:16 * h + 16, :], hot[0:n, 16 * h:16 * h + 16, :],
                                                     sf[0:n, 2 * h + k, :].unsqueeze(1).broadcast_to([n, 16, 16]), ALU.mult)
                        link(dve, last)
                        link(dve, dve.tensor_reduce(res[0:n, k, :], hot[0:n, :, :], AX, ALU.add))
                    dve.wait_ge(s_e, t + 1)
                    ex = res[0:n, 2, :].rearrange("p (h k) -> p h k", k=16)
                    link(dve, dve.tensor_reduce(z[0:n, :], ex, AX, ALU.add))
                    link(dve, dve.reciprocal(z[0:n, :], z[0:n, :]))
                    dve.tensor_tensor(ex, ex, z[0:n, :].unsqueeze(2).broadcast_to([n, 8, 16]), ALU.mult).then_inc(s_r, 1)
                    dve.wait_ge(s_tr, t + 1)
                    for k, dst in enumerate((iT, jT, gT)):
                        last = dve.tensor_copy(dst[:, a:a + n], ps[:, 4, k * P:k * P + n])
                    link(dve, last)


def spread(g, iT, jT, gT, G):
    nc, ps, sb, sem = g.nc, g.ps, g.sb, g.sem
    cst = g.cst
    GT = 4
    with ExitStack() as st:
        A0 = sb(st, "A0", [P, 2, GT, P])
        A = sb(st, "A", [P, 2, GT, P])
        B = sb(st, "B", [P, 2, GT, P])
        s_a0, s_a, s_b, s_mm, s_g = ([sem(f"{n}{k}") for k in range(2)] for n in (
            "hot_i", "gated_i", "hot_j", "gates_mm", "gates_copied"))
        N = T // GT // 2
        io = cst("iota").unsqueeze(1).broadcast_to([P, GT, P])

        def col(x, i, k):
            return x[:, ds(i * (2 * GT) + k * GT, GT)].unsqueeze(2).broadcast_to([P, GT, P])

        g.credit(s_a + s_mm + s_g)
        with nc.Block() as block:
            @block.vector
            def _(dve):
                with dve.Fori(0, N) as i:
                    for k in range(2):
                        dve.wait_ge(s_a[k], i + 1)
                        dve.tensor_tensor(A0[:, k, :, :], io, col(iT, i, k), ALU.is_equal).then_inc(s_a0[k], 1)
                        dve.wait_ge(s_mm[k], i + 1)
                        dve.tensor_tensor(B[:, k, :, :], io, col(jT, i, k), ALU.is_equal).then_inc(s_b[k], 1)

            @block.gpsimd
            def _(pool):
                with pool.Fori(0, N) as i:
                    for k in range(2):
                        pool.wait_ge(s_a0[k], i + 1)
                        pool.wait_ge(s_mm[k], i + 1)
                        pool.tensor_tensor(A[:, k, :, :], A0[:, k, :, :], col(gT, i, k), ALU.mult).then_inc(s_a[k], 1)

            @block.tensor
            def _(pe):
                with pe.Fori(0, N) as i:
                    for k in range(2):
                        pe.wait_ge(s_a[k], i + 2)
                        pe.wait_ge(s_b[k], i + 1)
                        pe.wait_ge(s_g[k], i + 1)
                        for t in range(GT):
                            mm = pe.matmul(ps[:, k, t * P:(t + 1) * P], A[:, k, t, :], B[:, k, t, :],
                                           start=True, stop=True)
                        mm.then_inc(s_mm[k], 1)

            @block.scalar
            def _(act):
                with act.Fori(0, N) as i:
                    for k in range(2):
                        act.wait_ge(s_mm[k], i + 2)
                        act.activation(G[:, :, ds(i * (2 * GT) + k * GT, GT)],
                                       ps[:, k, :].rearrange("p (t j) -> p j t", t=GT), ACT.Copy).then_inc(s_g[k], 1)


def u_stage(g, hf, G, ring):
    nc, d, ps, sb, sem = g.nc, g.d, g.ps, g.sb, g.sem
    landed, used, drained = g.landed, g.used, g.drained
    r0, N = g.rounds[0], P // RING
    g.rounds[0] += N
    with ExitStack() as st:
        a = sb(st, "act", [P, RING, T])
        s_mul = [sem(f"gated{k}") for k in range(RING)]
        g.credit(s_mul)
        with nc.Block() as block:
            @block.sync
            def _(sp):
                with sp.Fori(0, N) as i:
                    for k in range(RING):
                        sp.wait_ge(used[k], i + r0)
                        sp.dma_start(ring[:, k, :], d["peer_u"][ds(i * RING + k, 1), :, :].rearrange("a p n -> p (a n)")
                                     ).then_inc(landed[k], 16)

            @block.tensor
            def _(pe):
                with pe.Fori(0, N) as i:
                    for k in range(RING):
                        pe.wait_ge(landed[k], (i + r0) * 16)
                        pe.wait_ge(drained[k], i + r0)
                        for c in range(KC):
                            mm = pe.matmul(ps[:, k, 0:T], ring[:, k, c * P:(c + 1) * P], hf[:, c, :],
                                           start=(c == 0), stop=(c == KC - 1))
                        mm.then_inc(used[k], 1)

            @block.scalar
            def _(act):
                with act.Fori(0, N) as i:
                    for k in range(RING):
                        act.wait_ge(used[k], i + (r0 + 1))
                        act.wait_ge(s_mul[k], i + 1)
                        act.activation(a[:, k, :], ps[:, k, 0:T], ACT.Gelu_apprx_tanh).then_inc(drained[k], 1)

            @block.vector
            def _(dve):
                with dve.Fori(0, N) as i:
                    for k in range(RING):
                        dve.wait_ge(drained[k], i + (r0 + 1))
                        row = G[:, ds(i * RING + k, 1), :].rearrange("p a t -> p (a t)")
                        dve.tensor_tensor(row, a[:, k, :], row, ALU.mult).then_inc(s_mul[k], 1)


def v_stage(g, xT, G, ring):
    nc, d, ps, sb, sem, link = g.nc, g.d, g.ps, g.sb, g.sem, g.link
    landed, used = g.landed, g.used
    N = P // 2 // RING
    with ExitStack() as st:
        zero = sb(st, "zero", [P, P])
        s_z, s_acc, s_add = sem("zero_made"), sem("half_summed"), sem("half_added")
        with nc.Block() as block:
            @block.sync
            def _(sp):
                for half in range(2):
                    r0 = g.rounds[0] + half * N
                    with sp.Fori(0, N) as i:
                        for k in range(RING):
                            sp.wait_ge(used[k], i + r0)
                            sp.dma_start(ring[:, k, :], d["peer_v"][ds(i * RING + (k + half * N * RING), 1), :, :]
                                         .rearrange("a p n -> p (a n)")).then_inc(landed[k], 16)

            @block.tensor
            def _(pe):
                pe.wait_ge(s_z, 1)
                for half in range(2):
                    r0 = g.rounds[0] + half * N
                    if half:
                        pe.wait_ge(s_add, 8)
                    for c in range(8):
                        pe.matmul(ps[:, c, 0:T], zero[:, :], xT[:, 0, :], start=True, stop=False)
                    with pe.Fori(0, N) as i:
                        for k in range(RING):
                            pe.wait_ge(landed[k], (i + r0) * 16)
                            for j in range(2):
                                h = G[:, ds(i * (2 * RING) + (2 * k + j), 1), :].rearrange("p a t -> p (a t)")
                                for c in range(8):
                                    mm = pe.matmul(ps[:, c, 0:T], ring[:, k, j * 1024 + c * P:j * 1024 + (c + 1) * P],
                                                   h, start=False, stop=False)
                            mm.then_inc(used[k], 1)
                    for c in range(8):
                        pe.matmul(ps[:, c, 0:T], zero[:, :], G[:, 0, :], start=False, stop=True).then_inc(s_acc, 1)

            @block.vector
            def _(dve):
                dve.memset(zero[:, :], 0.0).then_inc(s_z, 1)
                for half in range(2):
                    for c in range(8):
                        dve.wait_ge(s_acc, 8 * half + c + 1)
                        dve.tensor_tensor(xT[:, 8 * half + c, :], ps[:, c, 0:T], xT[:, 8 * half + c, :], ALU.add
                                          ).then_inc(s_add, 1)
        g.rounds[0] += 2 * N


def feature_major(x):
    t, f = x.shape
    return np.ascontiguousarray(x.reshape(t, f // P, P).transpose(2, 1, 0))


def tiles(w):
    k, n = w.shape
    return np.ascontiguousarray(w.reshape(k // P, P, n // P, P).transpose(2, 1, 0, 3).reshape(n // P, P, k))


def lay_out(i):
    i = {k: np.asarray(v) for k, v in i.items()}
    out = {"consts": constants()}
    rw = 3360
    order = np.arange(1024).reshape(2, 2, 4, 64).transpose(0, 2, 1, 3).reshape(-1)

    def chunks(v):
        return np.pad(v.reshape(-1), (0, -v.size % P)).reshape(-1, P).T

    out["vecs"] = np.ascontiguousarray(np.concatenate([chunks(v) for v in (
        i["norm_mix_g"], i["norm_x_g"], i["norm_ffn_g"], i["norm_f_g"], i["mem_norm_g"],
        i["nsa_norm_g"][order], i["rw_mu"], i["rw_w0"], i["rw_a0"], i["rw_k_k"], i["rw_k_a"], i["rw_r_k"],
        i["rw_lnx_g"], i["rw_lnx_b"], i["cmp_b1"])], 1))
    out["x"] = feature_major(np.concatenate([i["x_prompt"][0], i["x_sample"][:, 0]], 0))
    out["mem"] = feature_major(i["mem_prompt"][0])
    w = i["w_in"]
    wide = np.zeros((D, NCH * P), w.dtype)
    wide[:, :rw] = w[:, :rw]
    wide[:, C_Q * P:C_KC * P] = w[:, rw:rw + 1024][:, order]
    wide[:, C_KC * P:C_KC * P + 1584] = w[:, rw + 1024:]
    out["w_in"] = tiles(wide)
    out["w_out"] = tiles(np.concatenate([i["w_out"][:1024], i["w_out"][1024:][order]], 0))
    for n in ("xk", "xv"):
        out[n] = np.ascontiguousarray(i[n].reshape(KC, P, 512).transpose(1, 0, 2))
    out["shift"] = feature_major(np.pad(i["state_rwkv_shift"], ((0, 0), (0, RWC * P - rw))))
    out["wa2"] = np.concatenate([i["rw_w2"], i["rw_a2"]], 0)
    out["rw_g2"] = i["rw_g2"]
    out["wkv"] = np.ascontiguousarray(i["state_rwkv_wkv"].reshape(8, 8, 2, 4096).transpose(2, 0, 1, 3).reshape(P, 4096))
    out["win"] = np.ascontiguousarray(np.stack([i["cache_win_k"], i["cache_win_v"]], 0).reshape(2, 8, 512, 256))
    dup = i["cmp_w1"].transpose(2, 0, 1, 3)
    out["cmp_w1_twice"] = np.ascontiguousarray(np.concatenate([dup, dup], 0))
    out["cmp_w1"] = np.ascontiguousarray(i["cmp_w1"].reshape(2, 16, P, P).transpose(2, 0, 1, 3))
    out["cmp_w2"] = np.ascontiguousarray(i["cmp_w2"].transpose(1, 0, 2))
    for n in ("cmp_k", "cmp_v"):
        c = i[f"cache_{n}"].reshape(N_PHYS, 8, 8, 2, 4, 64)
        out[n] = np.ascontiguousarray(c.transpose(0, 3, 5, 2, 4, 1).reshape(N_PHYS, P, 256))
    out["slc_k"] = np.ascontiguousarray(
        i["cache_slc_k"].reshape(N_PHYS, P, 2, 2, 64).transpose(0, 3, 4, 2, 1).reshape(N_PHYS, P, 256))
    out["slc_v"] = i["cache_slc_v"].reshape(N_PHYS, P, 256)
    out["win_k"] = np.ascontiguousarray(i["cache_win_k"].reshape(8, 512, 2, 2, 64).transpose(3, 4, 0, 2, 1)
                                        .reshape(P, 8, 2, 512))
    out["win_v"] = np.ascontiguousarray(i["cache_win_v"].reshape(8, 4, P, 256).transpose(2, 0, 1, 3))
    out["page_table"] = i["page_table"].reshape(1, P)
    out["xq"] = tiles(i["xq"])
    out["mem_k"] = np.ascontiguousarray(i["cache_mem_k"].transpose(3, 0, 2, 1))
    out["mem_v"] = np.ascontiguousarray(i["cache_mem_v"].reshape(8, 2, P, 512).transpose(2, 0, 1, 3))
    out["xo"] = np.ascontiguousarray(i["xo"].reshape(4, P, D).transpose(1, 0, 2))
    out["peer_wq"] = tiles(i["peer_wq"])
    out["peer_keys"] = np.ascontiguousarray(i["peer_sub_keys"].reshape(16, P, P).transpose(2, 0, 1))
    out["peer_u"] = np.ascontiguousarray(i["peer_u"].reshape(P, P, KC, P).transpose(1, 3, 2, 0).reshape(P, P, D))
    out["peer_v"] = np.ascontiguousarray(i["peer_v"].reshape(P, 64, 2, 2, 1024).transpose(3, 1, 0, 2, 4)
                                         .reshape(P, P, D))
    return out


OUTS = {"o_y": (P, KC, T), "o_shift": (P, RWC, 9), "o_kv": (P, 12, T), "o_win": (2, 8, 511, 256),
        "o_memk": (P, 4, TP), "o_memv": (P, 2, 512), "o_pwkv": (P, 8, 64), "o_swkv": (P, 4096)}


def kernel(**inputs):
    import concourse.bacc as bacc
    from concourse.bass_utils import run_bass_kernel_spmd

    nc = bacc.Bacc("TRN2", target_bir_lowering=False, num_devices=1)
    arrays = lay_out(inputs)
    d = {n: nc.dram_tensor(f"in_{n}", a.shape, mybir.dt.from_np(a.dtype), kind="ExternalInput").ap()
         for n, a in arrays.items()}
    for n, s in OUTS.items():
        d[n] = nc.dram_tensor(n, s, F32, kind="ExternalOutput").ap()
    d["residual"] = nc.dram_tensor("residual", (P, KC, T), F32, kind="Internal").ap()
    build(nc, d)
    r = run_bass_kernel_spmd(nc, [{f"in_{n}": a for n, a in arrays.items()}], core_ids=[0]).results[0]

    y = r["o_y"].transpose(2, 1, 0).reshape(T, D)
    shift = r["o_shift"].transpose(2, 1, 0).reshape(9, RWC * P)[:, :3360]
    kv = r["o_kv"].transpose(2, 1, 0).reshape(T, 6, 4, 64)
    pk = [np.ascontiguousarray(kv[None, :TP, n]) for n in range(6)]
    sk = [np.ascontiguousarray(kv[TP:, None, n]) for n in range(6)]
    memk = r["o_memk"].transpose(2, 1, 0)[None]
    memv = r["o_memv"].transpose(1, 0, 2).reshape(1, TP, 4, P)
    pwkv = r["o_pwkv"].reshape(2, 64, 8, 64).transpose(2, 0, 3, 1).reshape(1, 16, 64, 64)
    swkv = r["o_swkv"].reshape(2, 8, 8, 64, 64).transpose(1, 2, 0, 3, 4).reshape(8, 16, 64, 64)
    win = [np.concatenate([r["o_win"][n].reshape(8, 511, 4, 64), sk[4 + n]], 1) for n in range(2)]
    out = (y[None, :TP], y[TP:, None], shift[:1], pwkv, *pk, memk, memv, shift[1:], swkv, *sk[:4], *win)
    return tuple(np.ascontiguousarray(a) for a in out)
```

```python
from contextlib import ExitStack

import numpy as np

import concourse.bass as bass
from concourse import mybir

ALU = mybir.AluOpType
ACT = mybir.ActivationFunctionType
AX = mybir.AxisListType.X
F32 = mybir.dt.float32
U32 = mybir.dt.uint32
I32 = mybir.dt.int32
ds = bass.DynSlice

P = 128
D = 2048
KC = D // P
TP, TS = 256, 8
T = TP + TS
RWC = 27
C_R, C_K, C_V, C_WA, C_G = 0, 8, 16, 24, 25
C_Q, C_KC, C_VC, C_KS, C_VS, C_KW, C_VW, C_GL = 27, 35, 37, 39, 41, 43, 45, 47
NCH = 48
CH = 32
NB = TP // CH
NCB = TP // 16 - 1
N_PHYS = 160
PG = 16
NCS = 127
NBLK = 33
RING = 4
NEG = -1e30
DECAY = -float(np.exp(-0.5))

VEC = {}
_at = 0
for _n, _c in [("mix", 16), ("x", 16), ("ffn", 16), ("f", 16), ("mem", 16), ("nsa", 8), ("mu", RWC),
               ("w0", 8), ("a0", 8), ("kk", 8), ("ka", 8), ("rk", 8), ("lg", 8), ("lb", 8), ("b1", 2)]:
    VEC[_n] = (_at, _c)
    _at += _c
NVEC = _at

CON = {}
_at = 0
for _n, _c in [("ident", 128), ("ones", 128), ("bones", 128), ("tri", 256), ("scan", 256),
               ("causal", 512), ("cmask", 2 * NCB), ("cvalid", 2), ("gsum", 32), ("gexp", 128),
               ("gate", 3 * 128), ("bsel", 8), ("eps", 2), ("iota", 128), ("i16", 16)]:
    CON[_n] = (_at, _c)
    _at += _c
NCON = _at


def constants():
    c = np.zeros((P, NCON), np.float32)
    p = np.arange(P)[:, None]
    f = np.arange(P)[None, :]

    def put(name, v, rows=P):
        a, n = CON[name]
        c[:rows, a:a + n] = v

    put("ident", p == f)
    put("ones", 1.0)
    put("bones", p // 64 == f // 64)
    same = p // CH == f // CH
    put("tri", np.concatenate([same & (p < f), same & (p <= f)], 1))
    put("scan", np.arange(TP)[None, :] % CH != 0)
    key = np.arange(TP)[None, :]
    put("causal", np.concatenate([np.where(key <= p + P * t, 0.0, NEG) for t in range(2)], 1))
    end = np.arange(NCB)[None, :] * 16 + 31
    put("cmask", np.concatenate([np.where(end <= p + P * t, 0.0, NEG) for t in range(2)], 1))
    put("cvalid", np.concatenate([p + P * t >= 31 for t in range(2)], 1))
    put("gsum", p // 4 == np.arange(32)[None, :])
    put("gexp", (np.arange(32)[:, None] == f // 4), 32)
    head = ((f // 64) * 2 + (f // 4) % 2) * 4 + f % 4
    put("gate", np.concatenate([(np.arange(48)[:, None] == head * 3 + br) for br in range(3)], 1), 48)
    put("bsel", (p // 8) % 8 == np.arange(8)[None, :])
    c[:, CON["eps"][0]] = 1e-6
    c[:, CON["eps"][0] + 1] = 64e-5
    put("iota", f)
    put("i16", np.arange(16)[None, :])
    return c


class Ctx:
    pass


def build(nc, d):
    g = Ctx()
    with ExitStack() as top:
        names = [0]

        def sb(st, name, shape, dt=F32):
            names[0] += 1
            return st.enter_context(nc.sbuf_tensor(f"{name}_{names[0]}", shape, dt))

        def sem(name):
            names[0] += 1
            return top.enter_context(nc.semaphore(f"{name}_{names[0]}"))

        ps = top.enter_context(nc.psum_tensor("ps", [P, 8, 512], F32))
        con = sb(top, "con", [P, NCON])
        vec = sb(top, "vec", [P, NVEC])

        def cst(name, rows=P):
            a, n = CON[name]
            return con[0:rows, a:a + n]

        def vcol(name, c, lo=0, hi=P):
            a = VEC[name][0] + c
            return vec[lo:hi, a:a + 1]

        ident, ones, bones = cst("ident"), cst("ones"), cst("bones")
        dve_step, act_step, pool_step = sem("dve_step"), sem("act_step"), sem("pool_step")
        steps = {"dve": 0, "act": 0, "pool": 0}

        def link(eng, ins):
            steps["dve"] += 1
            ins.then_inc(dve_step, 1)
            eng.wait_ge(dve_step, steps["dve"])

        def alink(eng, ins):
            steps["act"] += 1
            ins.then_inc(act_step, 1)
            eng.wait_ge(act_step, steps["act"])

        landed = [sem(f"tile{k}_landed") for k in range(RING)]
        used = [sem(f"tile{k}_used") for k in range(RING)]
        drained = [sem(f"bank{k}_drained") for k in range(RING)]
        rounds = [1]

        moved = sem("moved")
        n_moved = [0]

        def credit(sems):
            with ExitStack() as st:
                z = sb(st, "credit", [1, len(sems)])
                with nc.Block() as block:
                    @block.gpsimd
                    def _(pool):
                        for n, s in enumerate(sems):
                            pool.memset(z[:, n:n + 1], 0.0).then_inc(s, 1)

        def loads(pairs):
            with nc.Block() as block:
                @block.sync
                def _(sp):
                    for a, b in pairs:
                        sp.dma_start(a, b).then_inc(moved, 16)
                    n_moved[0] += 16 * len(pairs)
                    sp.wait_ge(moved, n_moved[0])

        stored = sem("stored")
        n_stored = [0]

        def send(sp, pairs):
            for a, b in pairs:
                sp.dma_start(a, b).then_inc(stored, 16)
                n_stored[0] += 16

        s_sq, s_sum, s_rt = sem("squared"), sem("summed"), sem("root")
        norms = [0, 0]

        def rms(src, dst, gain, nch, t, ahead=None):
            n0, c0 = norms
            norms[0] += 1
            norms[1] += nch
            width = nch * P
            with ExitStack() as st:
                sq = sb(st, "sq", [P, 2, t])
                rt = sb(st, "rt", [P, t])
                rr = sb(st, "rr", [P, t])
                with nc.Block() as block:
                    if ahead is not None:
                        block.sync(ahead)

                    @block.scalar
                    def _(act):
                        for c in range(nch):
                            if c >= 2:
                                act.wait_ge(s_sum, c0 + c - 1)
                            act.activation(sq[:, c % 2, :], src[:, c, :], ACT.Square).then_inc(s_sq, 1)
                        act.wait_ge(s_sum, c0 + nch)
                        act.activation(rt[:, :], ps[:, 0, 0:t], ACT.Sqrt, bias=cst("eps")[:, 0:1],
                                       scale=1.0 / width).then_inc(s_rt, 1)

                    @block.tensor
                    def _(pe):
                        for c in range(nch):
                            pe.wait_ge(s_sq, c0 + c + 1)
                            pe.matmul(ps[:, 0, 0:t], ones, sq[:, c % 2, :], start=(c == 0),
                                      stop=(c == nch - 1)).then_inc(s_sum, 1)

                    @block.vector
                    def _(dve):
                        dve.wait_ge(s_rt, n0 + 1)
                        link(dve, dve.reciprocal(rr[:, :], rt[:, :]))
                        for c in range(nch):
                            dve.scalar_tensor_tensor(dst[:, c, :], src[:, c, :], vcol(gain, c), rr[:, :],
                                                     ALU.mult, ALU.mult)

        def prime(sp, w, ring):
            for k in range(RING):
                sp.dma_start(ring[:, k, :], w[k]).then_inc(landed[k], 16)

        def project(w, src, dst, n, ring, residual=False, ahead=None):
            r0 = rounds[0]
            per = n // RING
            rounds[0] += per
            with nc.Block() as block:
                @block.sync
                def _(sp):
                    if per > 1:
                        with sp.Fori(1, per) as i:
                            for k in range(RING):
                                sp.wait_ge(used[k], i + r0)
                                sp.dma_start(ring[:, k, :], w[ds(i * RING + k, 1), :, :].rearrange("a p n -> p (a n)")
                                             ).then_inc(landed[k], 16)
                    if ahead is not None:
                        ahead(sp)

                @block.tensor
                def _(pe):
                    with pe.Fori(0, per) as i:
                        for k in range(RING):
                            pe.wait_ge(landed[k], (i + r0) * 16)
                            pe.wait_ge(drained[k], i + r0)
                            for c in range(KC):
                                mm = pe.matmul(ps[:, k, 0:T], ring[:, k, c * P:(c + 1) * P], src[:, c, :],
                                               start=(c == 0), stop=(c == KC - 1))
                            mm.then_inc(used[k], 1)

                def drain(eng, i, k):
                    eng.wait_ge(used[k], i + (r0 + 1))
                    to = dst[:, ds(i * RING + k, 1), :].rearrange("p a t -> p (a t)")
                    if residual:
                        ins = eng.tensor_tensor(to, ps[:, k, 0:T], to, ALU.add)
                    elif eng is nc.scalar:
                        ins = eng.activation(to, ps[:, k, 0:T], ACT.Copy)
                    else:
                        ins = eng.tensor_copy(to, ps[:, k, 0:T])
                    ins.then_inc(drained[k], 1)

                if not residual:
                    @block.scalar
                    def _(act):
                        with act.Fori(0, per) as i:
                            for k in range(0, RING, 2):
                                drain(nc.scalar, i, k)

                @block.vector
                def _(dve):
                    with dve.Fori(0, per) as i:
                        for k in range(0 if residual else 1, RING, 1 if residual else 2):
                            drain(nc.vector, i, k)

        g.nc = nc
        g.d = d
        g.sb = sb
        g.sem = sem
        g.ps = ps
        g.cst = cst
        g.vcol = vcol
        g.ident = ident
        g.ones = ones
        g.bones = bones
        g.link = link
        g.alink = alink
        g.rms = rms
        g.credit = credit
        g.heads_mm = sem("head_sums")
        g.heads_used = sem("head_sums_used")
        g.heads = [0]
        g.project = project
        g.loads = loads
        g.send = send
        g.stored = stored
        g.n_stored = n_stored
        g.prime = prime
        g.con = con
        g.vec = vec
        g.landed = landed
        g.used = used
        g.drained = drained
        g.rounds = rounds

        credit(used + drained)
        with ExitStack() as st:
            cat = sb(st, "cat", [P, KC, T])
            with ExitStack() as s3:
                uT = sb(s3, "uT", [P, NCH, T])
                with ExitStack() as s4:
                    hT = sb(s4, "hT", [P, KC, T])
                    ring = sb(s4, "ring", [P, RING, D])
                    loads([(con[:, :], d["consts"]), (vec[:, :], d["vecs"]), (hT[:, :, :], d["x"])])
                    rms(hT, hT, "mix", KC, T, ahead=lambda sp: prime(sp, d["w_in"], ring))
                    project(d["w_in"], hT, uT, NCH, ring)
                rwkv(g, uT, cat)
                nsa_prompt(g, uT, cat)
                nsa_sample(g, uT, cat)
            xT = top.enter_context(nc.sbuf_tensor("xT", [P, KC, T], F32, side="right"))
            ring = top.enter_context(nc.sbuf_tensor("ring", [P, RING, D], F32, side="right"))
            mem_st = ExitStack()
            memk = mem_st.enter_context(nc.sbuf_tensor("memk", [P, 4, TP], F32, side="right"))
            memv = mem_st.enter_context(nc.sbuf_tensor("memv", [P, 2, 512], F32, side="right"))
            mT = sb(st, "mT", [P, KC, TP])
            wk = sb(st, "wk", [P, KC, 512])
            wv = sb(st, "wv", [P, KC, 512])
            s_x, s_mem = sem("x_again"), sem("memory_in")

            def early(sp):
                prime(sp, d["w_out"], ring)
                sp.dma_start(xT[:, :, :], d["x"]).then_inc(s_x, 16)
                for a, b in ((mT, "mem"), (wk, "xk"), (wv, "xv")):
                    sp.dma_start(a[:, :, :], d[b]).then_inc(s_mem, 16)
                sp.wait_ge(s_x, 16)

            rms(cat[:, 8:16, :], cat[:, 8:16, :], "nsa", 8, T, ahead=early)
            project(d["w_out"], cat, xT, KC, ring, residual=True,
                    ahead=lambda sp: sp.wait_ge(s_mem, 48))
            memory(g, memk, memv, mT, wk, wv)
        cross(g, memk, memv, xT, ring)
        mem_st.close()
        peer(g, xT, ring)
        with ExitStack() as st:
            y = sb(st, "y", [P, KC, T])
            rms(xT, y, "f", KC, T)
            loads([(d["o_y"], y[:, :, :])])
        with nc.Block() as block:
            @block.sync
            def _(sp):
                sp.wait_ge(stored, n_stored[0])


def memory(g, memk, memv, mT, wk, wv):
    nc, d, ps = g.nc, g.d, g.ps
    if True:
        g.rms(mT, mT, "mem", KC, TP)
        s_mm, s_out = g.sem("mem_products"), g.sem("mem_copied")
        with nc.Block() as block:
            @block.tensor
            def _(pe):
                for h in range(4):
                    for c in range(KC):
                        mm = pe.matmul(ps[:, h, 0:TP], wk[:, c, h * P:(h + 1) * P], mT[:, c, :],
                                       start=(c == 0), stop=(c == KC - 1))
                    mm.then_inc(s_mm, 1)
                for m in range(2):
                    for c in range(KC):
                        mm = pe.matmul(ps[:, 4 + m, :], mT[:, c, m * P:(m + 1) * P], wv[:, c, :],
                                       start=(c == 0), stop=(c == KC - 1))
                    mm.then_inc(s_mm, 1)

            @block.vector
            def _(dve):
                for h in range(4):
                    dve.wait_ge(s_mm, h + 1)
                    dve.tensor_copy(memk[:, h, :], ps[:, h, 0:TP]).then_inc(s_out, 1)
                for m in range(2):
                    dve.wait_ge(s_mm, 5 + m)
                    dve.tensor_copy(memv[:, m, :], ps[:, 4 + m, :]).then_inc(s_out, 1)

            @block.sync
            def _(sp):
                sp.wait_ge(s_out, 6)
                g.send(sp, [(d["o_memk"], memk[:, :, :]), (d["o_memv"], memv[:, :, :])])


def head_sums(g, src, out_of, n, t=T):
    nc, ps = g.nc, g.ps
    s_mm, s_used, n0 = g.heads_mm, g.heads_used, g.heads[0]
    g.heads[0] += n
    with nc.Block() as block:
        @block.tensor
        def _(pe):
            for m in range(n):
                if m >= 4:
                    pe.wait_ge(s_used, n0 + m - 3)
                pe.matmul(ps[:, m % 4, 0:t], g.bones, src[:, m, :], start=True, stop=True).then_inc(s_mm, 1)

        @block.vector
        def _(dve):
            for m in range(n):
                dve.wait_ge(s_mm, n0 + m + 1)
                out_of(dve, m, ps[:, m % 4, 0:t]).then_inc(s_used, 1)


def rwkv(g, uT, cat):
    nc, d, ps, sb, sem, link, alink = g.nc, g.d, g.ps, g.sb, g.sem, g.link, g.alink
    ident, vcol, cst = g.ident, g.vcol, g.cst
    g.loads([(d["o_shift"], uT[:, 0:RWC, TP - 1:T])])
    with ExitStack() as st:
        a_, kp, sg, tmp, rt, y = (sb(st, n, [P, 8, T]) for n in ("a", "kp", "sg", "tmp", "rt", "y"))
        us = uT[:, 0:RWC, :]
        r, k, v = us[:, C_R:C_R + 8, :], us[:, C_K:C_K + 8, :], us[:, C_V:C_V + 8, :]
        kk = k
        gg, bonus = cat[:, 0:8, :], cat[:, 8:16, :]
        with ExitStack() as s1:
            shift = sb(s1, "shift", [P, RWC, TS])
            wa2 = sb(s1, "wa2", [P, 1024])
            g2a = sb(s1, "g2a", [P, 1024])
            g2b = sb(s1, "g2b", [32, 1024])
            oka = sb(s1, "oka", [P, 8])
            diff = sb(s1, "diff", [P, 4, T])
            s_in, s_lo, s_mm, s_sig = sem("rw_in"), sem("rw_low"), sem("rw_mm"), sem("rw_sig")
            s_us = sem("rw_mixed")
            with nc.Block() as block:
                @block.sync
                def _(sp):
                    for a, b in [(shift[:, :, :], d["shift"]), (wa2[:, :], d["wa2"]),
                                 (g2a[:, :], d["rw_g2"][0:P, :]), (g2b[:, :], d["rw_g2"][P:160, :])]:
                        sp.dma_start(a, b).then_inc(s_in, 16)
                    g.send(sp, [(d["o_kv"], uT[:, C_KC:C_GL, :])]
                           + [(d["o_win"][i, :, 0:511, :], d["win"][i, :, 1:512, :]) for i in range(2)])

                @block.vector
                def _(dve):
                    dve.wait_ge(s_in, 64)
                    for n, c in enumerate(reversed(range(RWC))):
                        df = diff[:, n % 4, :]
                        if n >= 4:
                            dve.wait_ge(s_us, n - 3)
                        dve.tensor_tensor(df[:, 1:TP], us[:, c, 0:TP - 1], us[:, c, 1:TP], ALU.subtract)
                        dve.tensor_scalar(df[:, 0:1], us[:, c, 0:1], -1.0, None, ALU.mult)
                        link(dve, dve.tensor_tensor(df[:, TP:T], shift[:, c, :], us[:, c, TP:T], ALU.subtract))
                        dve.scalar_tensor_tensor(us[:, c, :], df, vcol("mu", c), us[:, c, :],
                                                 ALU.mult, ALU.add).then_inc(s_us, 1)

                @block.scalar
                def _(act):
                    act.wait_ge(s_us, 3)
                    act.activation(us[0:64, C_WA, :], us[0:64, C_WA, :], ACT.Tanh).then_inc(s_lo, 1)
                    act.activation(us[:, C_G, :], us[:, C_G, :], ACT.Sigmoid).then_inc(s_lo, 1)
                    act.activation(us[0:32, C_G + 1, :], us[0:32, C_G + 1, :], ACT.Sigmoid).then_inc(s_lo, 1)
                    for m in range(8):
                        act.wait_ge(s_mm, m + 1)
                        act.activation(sg[:, m, :], ps[:, 3 * (m % 2), 0:T], ACT.Sigmoid, bias=vcol("w0", m))
                        act.activation(a_[:, m, :], ps[:, 3 * (m % 2) + 1, 0:T], ACT.Sigmoid, bias=vcol("a0", m))
                        act.activation(gg[:, m, :], ps[:, 3 * (m % 2) + 2, 0:T], ACT.Copy).then_inc(s_sig, 1)

                @block.tensor
                def _(pe):
                    pe.wait_ge(s_lo, 3)
                    for m in range(8):
                        if m >= 2:
                            pe.wait_ge(s_sig, m - 1)
                        cs = slice(m * P, (m + 1) * P)
                        pe.matmul(ps[:, 3 * (m % 2), 0:T], wa2[0:64, cs], us[0:64, C_WA, :], start=True, stop=True)
                        pe.matmul(ps[:, 3 * (m % 2) + 1, 0:T], wa2[64:P, cs], us[64:P, C_WA, :],
                                  start=True, stop=True)
                        pe.matmul(ps[:, 3 * (m % 2) + 2, 0:T], g2a[:, cs], us[:, C_G, :], start=True, stop=False)
                        pe.matmul(ps[:, 3 * (m % 2) + 2, 0:T], g2b[:, cs], us[0:32, C_G + 1, :],
                                  start=False, stop=True).then_inc(s_mm, 1)

            with nc.Block() as block:
                @block.vector
                def _(dve):
                    a0 = VEC["ka"][0]
                    link(dve, dve.tensor_scalar(oka[:, :], g.vec[:, a0:a0 + 8], -1.0, 1.0, ALU.mult, ALU.add))
                    for m in range(8):
                        last = dve.tensor_scalar(kp[:, m, :], a_[:, m, :], vcol("ka", m), oka[:, m:m + 1],
                                                 ALU.mult, ALU.add)
                    link(dve, last)
                    link(dve, dve.tensor_tensor(kp[:, :, :], kp[:, :, :], k, ALU.mult))
                    for m in range(8):
                        last = dve.tensor_scalar(kk[:, m, :], k[:, m, :], vcol("kk", m), None, ALU.mult)
                    link(dve, last)
                    dve.tensor_tensor(tmp[:, :, :], kk, kk, ALU.mult)
                    for m in range(8):
                        dve.scalar_tensor_tensor(bonus[:, m, :], r[:, m, :], vcol("rk", m), kp[:, m, :],
                                                 ALU.mult, ALU.mult)
        head_sums(g, tmp, lambda dve, m, s: dve.tensor_scalar(rt[:, m, :], s, 1e-24, None, ALU.max), 8)
        head_sums(g, bonus, lambda dve, m, s: dve.tensor_tensor(bonus[:, m, :], s, v[:, m, :], ALU.mult), 8)
        with nc.Block() as block:
            @block.scalar
            def _(act):
                act.activation(rt[:, :, :], rt[:, :, :], ACT.Sqrt)
        with nc.Block() as block:
            @block.vector
            def _(dve):
                link(dve, dve.reciprocal(tmp[:, :, :], rt[:, :, :]))
                dve.tensor_tensor(kk[:, :, :], kk[:, :, :], tmp[:, :, :], ALU.mult)
        b_ = a_
        with nc.Block() as block:
            @block.vector
            def _(dve):
                dve.tensor_tensor(b_[:, :, :], kk[:, :, :], a_[:, :, :], ALU.mult)

        rwkv_sample(g, r, v, kk, kp, b_, sg, y)
        rwkv_prompt(g, uT, kp, b_, sg, tmp, rt, y)

        head_sums(g, y, lambda dve, m, s: dve.scalar_tensor_tensor(y[:, m, :], s, -1.0 / 64, y[:, m, :],
                                                                   ALU.mult, ALU.add), 8)
        with nc.Block() as block:
            @block.vector
            def _(dve):
                dve.tensor_tensor(tmp[:, :, :], y[:, :, :], y[:, :, :], ALU.mult)
        head_sums(g, tmp, lambda dve, m, s: dve.tensor_copy(rt[:, m, :], s), 8)
        with nc.Block() as block:
            @block.scalar
            def _(act):
                act.activation(rt[:, :, :], rt[:, :, :], ACT.Sqrt, bias=cst("eps")[:, 1:2], scale=1.0 / 64)
        with nc.Block() as block:
            @block.vector
            def _(dve):
                link(dve, dve.reciprocal(tmp[:, :, :], rt[:, :, :]))
                link(dve, dve.tensor_tensor(y[:, :, :], y[:, :, :], tmp[:, :, :], ALU.mult))
                for m in range(8):
                    dve.tensor_scalar(y[:, m, :], y[:, m, :], vcol("lg", m), vcol("lb", m), ALU.mult, ALU.add)
        with nc.Block() as block:
            @block.vector
            def _(dve):
                link(dve, dve.tensor_tensor(y[:, :, :], y[:, :, :], bonus[:, :, :], ALU.add))
                dve.tensor_tensor(cat[:, 0:8, :], y[:, :, :], gg[:, :, :], ALU.mult)


def rwkv_prompt(g, uT, kp, b_, sg, tmp, rt, y):
    nc, d, ps, sb, sem, link, alink = g.nc, g.d, g.ps, g.sb, g.sem, g.link, g.alink
    ident, cst = g.ident, g.cst
    r, kk, v = uT[:, 0:8, 0:TP], uT[:, 8:16, 0:TP], uT[:, 16:24, :]
    bt, kt = b_[:, :, 0:TP], kp[:, :, 0:TP]
    with ExitStack() as st:
        pc = sb(st, "pc", [P, NB, 8])
        state = sb(st, "state", [P, NB + 1, 8, 64])
        qT = sb(st, "qT", [P, 8, TP])
        t2, e, cum = y[:, :, 0:TP], tmp[:, :, 0:TP], rt[:, :, 0:TP]
        s_cum, s_e, s_x = sem("cum"), sem("e"), sem("e_used")
        with nc.Block() as block:
            @block.vector
            def _(dve):
                for m in range(8):
                    dve.tensor_tensor_scan(cum[:, m, :], cst("scan"), sg[:, m, 0:TP], 0.0,
                                           ALU.mult, ALU.add)
                link(dve, dve.memset(state[:, 0, :, :], 0.0))
                dve.tensor_tensor(t2, cum, sg[:, :, 0:TP], ALU.subtract).then_inc(s_cum, 1)
                dve.wait_ge(s_e, 1)
                dve.tensor_copy(pc[:, :, :], e[:, :, CH - 1:TP:CH].rearrange("p m n -> p n m"))
                dve.tensor_tensor(r, e, r, ALU.mult).then_inc(s_x, 1)
                dve.wait_ge(s_e, 2)
                dve.tensor_tensor(bt, e, bt, ALU.mult)
                dve.tensor_tensor(kt, e, kt, ALU.mult).then_inc(s_x, 1)
                link(dve, dve.tensor_scalar(kk, kk, -1.0, None, ALU.mult))
                dve.wait_ge(s_e, 3)
                dve.tensor_tensor(kk, e, kk, ALU.mult)

            @block.scalar
            def _(act):
                act.wait_ge(s_cum, 1)
                act.activation(e, cum, ACT.Exp, scale=DECAY).then_inc(s_e, 1)
                act.wait_ge(s_x, 1)
                act.activation(e, cum, ACT.Exp, scale=-DECAY).then_inc(s_e, 1)
                act.wait_ge(s_x, 2)
                act.activation(e, t2, ACT.Exp, scale=DECAY).then_inc(s_e, 1)

        for tile in range(2):
            rwkv_tile(g, tile, uT, bt, kt, v, pc, state, qT, y, (tmp, rt, sg))

        s_mm, s_used = sem("y_mm"), sem("y_used")
        with nc.Block() as block:
            @block.tensor
            def _(pe):
                for m in range(8):
                    if m >= 4:
                        pe.wait_ge(s_used, m - 3)
                    for h in range(2):
                        rows = slice(64 * h, 64 * h + 64)
                        for c in range(NB):
                            mm = pe.matmul(ps[rows, m % 4, c * CH:(c + 1) * CH], state[rows, c, m, :],
                                           qT[rows, m, c * CH:(c + 1) * CH], start=True, stop=True)
                    mm.then_inc(s_mm, 1)

            @block.vector
            def _(dve):
                for m in range(8):
                    dve.wait_ge(s_mm, m + 1)
                    dve.tensor_tensor(y[:, m, 0:TP], ps[:, m % 4, 0:TP], y[:, m, 0:TP], ALU.add).then_inc(s_used, 1)
        g.loads([(d["o_pwkv"], state[:, NB, :, :])])


def rwkv_tile(g, tile, uT, bt, kt, v, pc, state, qT, y, spare):
    nc, ps, sb, sem, link = g.nc, g.ps, g.sb, g.sem, g.link
    ident, cst = g.ident, g.cst
    tok = slice(tile * P, (tile + 1) * P)
    tri = cst("tri")
    with ExitStack() as st:
        rows4 = sb(st, "rows4", [P, 4, 8, P])
        w = sb(st, "w", [P, 16, P])
        at = sb(st, "at", [P, 4, 8, 64])
        s_tr, s_cp = sem("rows_turned"), sem("rows_copied")
        with nc.Block() as block:
            @block.tensor
            def _(pe):
                for m in range(8):
                    if m >= 4:
                        pe.wait_ge(s_cp, m - 3)
                    for n, src in enumerate((uT[:, 8 + m, tok], bt[:, m, tok], kt[:, m, tok], v[:, m, tok])):
                        mm = pe.transpose(ps[:, m % 4, n * P:(n + 1) * P], src, ident)
                    mm.then_inc(s_tr, 1)

            @block.vector
            def _(dve):
                for m in range(8):
                    dve.wait_ge(s_tr, m + 1)
                    dve.tensor_copy(rows4[:, :, m, :], ps[:, m % 4, :].rearrange("p (n c) -> p n c", n=4)
                                    ).then_inc(s_cp, 1)

        sizes = [("xs", 2, P), ("ms", 2, P), ("rs", 2, P), ("rb", 1, P), ("nt", 1, P), ("rk", 1, P), ("nv", 1, 64)]
        bufs = [{n: sb(st, n, [P, k, 4, c]) for n, k, c in sizes}, {}]
        flat = [x[:, :, :].rearrange("p m t -> p (m t)") for x in spare]
        for x, names in zip(flat, (("xs", "ms"), ("rs", "rb", "nt"), ("rk", "nv"))):
            at0 = 0
            for n, k, c in sizes:
                if n in names:
                    bufs[1][n] = x[:, at0:at0 + k * 4 * c].rearrange("p (k i c) -> p k i c", k=k, i=4)
                    at0 += k * 4 * c
        s_pe, s_v = sem("tile_pe"), sem("tile_dve")
        STEPS = 13

        def heads_of(grp):
            return [(2 * grp + i % 2, i // 2) for i in range(4)]

        with nc.Block() as block:
            @block.tensor
            def _(pe):
                def step(n, grp, B, b0):
                    heads = heads_of(grp)
                    if n == 0:
                        for i, (m, h) in enumerate(heads):
                            rows = slice(64 * h, 64 * h + 64)
                            arm = uT[rows, m:m + 9:8, tok]
                            half = slice(256 * (i % 2), 256 * (i % 2) + 256)
                            pe.matmul(ps[:, b0 + i // 2, half], bt[rows, m, tok], arm, start=True, stop=True)
                            mm = pe.matmul(ps[:, b0 + 2 + i // 2, half], kt[rows, m, tok], arm, start=True, stop=True)
                    elif n == 1:
                        for i in range(4):
                            pe.transpose(ps[:, b0, i * P:(i + 1) * P], B["xs"][:, 0, i, :], ident)
                        for i, (m, h) in enumerate(heads):
                            mm = pe.matmul(ps[:, b0 + 1, i * 64:i * 64 + 64], B["nt"][:, 0, i, :],
                                           rows4[:, 3, m, 64 * h:64 * h + 64], start=True, stop=True)
                    elif n < 10:
                        q = (n - 2) // 2
                        a, b = q % 2, (q + 1) % 2
                        if n % 2 == 0:
                            for i in range(4):
                                mm = pe.matmul(ps[:, b0, i * P:(i + 1) * P], B["xs"][:, a, i, :], B["ms"][:, a, i, :],
                                               start=True, stop=True)
                                if q < 3:
                                    mm = pe.matmul(ps[:, b0 + 1, i * P:(i + 1) * P], B["ms"][:, a, i, :],
                                                   B["xs"][:, a, i, :], start=True, stop=True)
                        else:
                            for i in range(4):
                                mm = pe.matmul(ps[:, b0 + 2, i * P:(i + 1) * P], B["ms"][:, b, i, :],
                                               B["rs"][:, a, i, :], start=True, stop=True)
                    elif n == 10:
                        for i, (m, h) in enumerate(heads):
                            inv = B["rs"][:, 0, i, :]
                            pe.matmul(ps[:, b0 + 3, i * P:i * P + 64], inv, rows4[:, 0, m, 64 * h:64 * h + 64],
                                      start=True, stop=True)
                            mm = pe.matmul(ps[:, b0 + 3, i * P + 64:(i + 1) * P], inv, B["nv"][:, 0, i, :],
                                           start=True, stop=True)
                    elif n == 11:
                        for i, (m, h) in enumerate(heads):
                            rows = slice(64 * h, 64 * h + 64)
                            wh = w[:, 4 * grp + i, :]
                            at_ = slice((i % 2) * P, (i % 2) * P + P)
                            pe.matmul(ps[rows, b0, at_], wh[:, 0:64], B["rb"][:, 0, i, :], start=True, stop=True)
                            pe.matmul(ps[rows, b0 + 1, at_], wh[:, 64:P], B["rb"][:, 0, i, :], start=True, stop=False)
                            mm = pe.matmul(ps[rows, b0 + 1, at_], rows4[:, 3, m, 64 * h:64 * h + 64],
                                           B["rk"][:, 0, i, :], start=False, stop=True)
                    else:
                        for i, (m, h) in enumerate(heads):
                            rows = slice(64 * h, 64 * h + 64)
                            for c in range(4):
                                tk = slice(CH * c, CH * c + CH)
                                mm = pe.matmul(ps[rows, b0 + c, (i % 2) * 64:(i % 2) * 64 + 64],
                                               w[tk, 4 * grp + i, 0:64], rows4[tk, 1, m, 64 * h:64 * h + 64],
                                               start=True, stop=True, tile_position=(CH * c, 64 * h))
                    mm.then_inc(s_pe, 1)

                count = 0
                for two in range(2):
                    for n in range(STEPS):
                        for k in range(2):
                            if count >= 2:
                                pe.wait_ge(s_v, count - 1)
                            step(n, 2 * two + k, bufs[k], 4 * k)
                            count += 1

            @block.vector
            def _(dve):
                def answer(n, grp, B, b0, count):
                    def wide(x):
                        return x.rearrange("p i t -> p (i t)")

                    if n == 0:
                        strict = tri[:, 0:P].unsqueeze(1).broadcast_to([P, 2, P])
                        incl = tri[:, P:2 * P].unsqueeze(1).broadcast_to([P, 2, P])
                        for i2 in range(2):
                            two = slice(2 * i2, 2 * i2 + 2)
                            bank = ps[:, b0 + i2, :].rearrange("p (i a t) -> p i a t", i=2, a=2)
                            bankk = ps[:, b0 + 2 + i2, :].rearrange("p (i a t) -> p i a t", i=2, a=2)
                            dve.tensor_tensor(B["xs"][:, 0, two, :], bank[:, :, 1, :], strict, ALU.mult)
                            dve.tensor_tensor(B["rb"][:, 0, two, :], bank[:, :, 0, :], incl, ALU.mult)
                            dve.tensor_tensor(B["nt"][:, 0, two, :], bankk[:, :, 1, :], strict, ALU.mult)
                            last = dve.tensor_tensor(B["rk"][:, 0, two, :], bankk[:, :, 0, :], incl, ALU.mult)
                    elif n == 1:
                        dve.tensor_copy(wide(B["ms"][:, 0, :, :]), ps[:, b0, :])
                        dve.wait_ge(s_v, count - 1)
                        dve.tensor_tensor(B["rs"][:, 0, :, :], B["xs"][:, 0, :, :],
                                          ident.unsqueeze(1).broadcast_to([P, 4, P]), ALU.add)
                        last = dve.tensor_copy(wide(B["nv"][:, 0, :, :]), ps[:, b0 + 1, 0:256])
                    elif n < 10:
                        q = (n - 2) // 2
                        a, b = q % 2, (q + 1) % 2
                        if n % 2 == 0:
                            if q < 3:
                                dve.tensor_copy(wide(B["xs"][:, b, :, :]), ps[:, b0 + 1, :])
                            last = dve.tensor_copy(wide(B["ms"][:, b, :, :]), ps[:, b0, :])
                        else:
                            dve.wait_ge(s_v, count - 1)
                            last = dve.tensor_tensor(wide(B["rs"][:, b, :, :]), ps[:, b0 + 2, :],
                                                     wide(B["rs"][:, a, :, :]), ALU.add)
                    elif n == 10:
                        last = dve.tensor_copy(wide(w[:, 4 * grp:4 * grp + 4, :]), ps[:, b0 + 3, :])
                    elif n == 11:
                        m2 = slice(2 * grp, 2 * grp + 2)
                        dve.tensor_tensor(qT[:, m2, tok], ps[:, b0, 0:256].rearrange("p (m t) -> p m t", m=2),
                                          uT[:, m2, tok], ALU.add)
                        last = dve.tensor_copy(y[:, m2, tok], ps[:, b0 + 1, 0:256].rearrange("p (m t) -> p m t", m=2))
                    else:
                        m2 = slice(2 * grp, 2 * grp + 2)
                        for h in range(2):
                            rows = slice(64 * h, 64 * h + 64)
                            eye = ident[rows, rows].unsqueeze(1).broadcast_to([64, 2, 64])
                            for c in range(4):
                                last = dve.tensor_tensor(at[rows, c, m2, :], ps[rows, b0 + c, 0:P].rearrange(
                                    "p (m j) -> p m j", m=2), eye, ALU.add)
                    last.then_inc(s_v, 1)

                count = 0
                for two in range(2):
                    for n in range(STEPS):
                        for k in range(2):
                            dve.wait_ge(s_pe, count + 1)
                            answer(n, 2 * two + k, bufs[k], 4 * k, count)
                            count += 1

        s_st, s_ev = sem("state_mm"), sem("state_new")
        with nc.Block() as block:
            @block.tensor
            def _(pe):
                for c in range(4):
                    tk = slice(CH * c, CH * c + CH)
                    if c >= 1:
                        pe.wait_ge(s_ev, c)
                    for m in range(8):
                        for h in range(2):
                            rows = slice(64 * h, 64 * h + 64)
                            out = ps[rows, c % 2, m * 64:m * 64 + 64]
                            pos = (CH * c, 64 * h)
                            pe.matmul(out, rows4[tk, 1, m, 64 * h:64 * h + 64], w[tk, 4 * (m // 2) + 2 * h + m % 2, 64:P],
                                      start=True, stop=False, tile_position=pos)
                            pe.matmul(out, rows4[tk, 2, m, 64 * h:64 * h + 64], rows4[tk, 3, m, 64 * h:64 * h + 64],
                                      start=False, stop=False, tile_position=pos)
                            mm = pe.matmul(out, at[rows, c, m, :], state[rows, 4 * tile + c, m, :],
                                           start=False, stop=True)
                    mm.then_inc(s_st, 1)

            @block.vector
            def _(dve):
                for c in range(4):
                    dve.wait_ge(s_st, c + 1)
                    n = 4 * tile + c
                    dve.tensor_tensor(state[:, n + 1, :, :], ps[:, c % 2, :].rearrange("p (m j) -> p m j", m=8),
                                      pc[:, n, :].unsqueeze(2).broadcast_to([P, 8, 64]), ALU.mult).then_inc(s_ev, 1)


def rwkv_sample(g, r, v, kk, kp, b_, sg, y):
    nc, d, ps, sb, sem, link = g.nc, g.d, g.ps, g.sb, g.sem, g.link
    ident = g.ident
    with ExitStack() as st:
        S = sb(st, "S", [P, 64, 64])
        big = sb(st, "big", [P, 64, 64])
        vs = sb(st, "vs", [P, 6, 64])
        packed = sb(st, "packed", [P, 6, TS, 8])
        sa = sb(st, "sa", [P, 64])
        yr = sb(st, "yr", [P, 64])
        s_in, s_pk, s_tr, s_cp, s_y, s_yt, s_out = (sem(n) for n in (
            "st_in", "packed", "turned", "rows", "y_rows", "y_turned", "st_out"))
        with nc.Block() as block:
            @block.sync
            def _(sp):
                sp.dma_start(S[:, :, :].rearrange("p i j -> p (i j)"), d["wkv"]).then_inc(s_in, 16)
                sp.wait_ge(s_y, 1)
                sp.dma_start(d["o_swkv"], S[:, :, :].rearrange("p i j -> p (i j)")).then_inc(s_out, 16)
                sp.wait_ge(s_out, 16)

            @block.tensor
            def _(pe):
                pe.wait_ge(s_pk, 1)
                for n in range(6):
                    for h in range(2):
                        rows = slice(64 * h, 64 * h + 64)
                        mm = pe.matmul(ps[rows, 0, n * 64:n * 64 + 64],
                                       packed[rows, n, :, :].rearrange("p b m -> p (b m)"), ident[rows, rows],
                                       start=True, stop=True)
                mm.then_inc(s_tr, 1)
                pe.wait_ge(s_y, 1)
                for h in range(2):
                    rows = slice(64 * h, 64 * h + 64)
                    mm = pe.matmul(ps[rows, 1, 0:64], yr[rows, :], ident[rows, rows], start=True, stop=True)
                mm.then_inc(s_yt, 1)

            @block.vector
            def _(dve):
                for n, x in enumerate((r, v, kk, kp, b_, sg)):
                    dve.tensor_copy(packed[:, n, :, :], x[:, :, TP:T].rearrange("p m b -> p b m"))
                link(dve, dve.memset(sa[:, :], 0.0))
                dve.tensor_copy(yr[:, :], sa[:, :]).then_inc(s_pk, 1)
                dve.wait_ge(s_tr, 1)
                dve.tensor_copy(vs[:, :, :].rearrange("p n c -> p (n c)"), ps[:, 0, 0:384]).then_inc(s_cp, 1)
                dve.wait_ge(s_cp, 2)
                dve.wait_ge(s_in, 16)

                def over_i(n):
                    return vs[:, n, :].unsqueeze(1).broadcast_to([P, 64, 64])

                def over_j(x):
                    return x.unsqueeze(2).broadcast_to([P, 64, 64])

                link(dve, dve.tensor_tensor(big[:, :, :], S[:, :, :], over_i(2), ALU.mult))
                dve.tensor_reduce(sa[:, :], big[:, :, :], AX, ALU.add, negate=True)
                link(dve, dve.tensor_tensor(S[:, :, :], S[:, :, :], over_i(5), ALU.mult))
                link(dve, dve.tensor_tensor(big[:, :, :], over_j(sa[:, :]), over_i(4), ALU.mult))
                link(dve, dve.tensor_tensor(S[:, :, :], S[:, :, :], big[:, :, :], ALU.add))
                link(dve, dve.tensor_tensor(big[:, :, :], over_j(vs[:, 1, :]), over_i(3), ALU.mult))
                link(dve, dve.tensor_tensor(S[:, :, :], S[:, :, :], big[:, :, :], ALU.add))
                link(dve, dve.tensor_tensor(big[:, :, :], S[:, :, :], over_i(0), ALU.mult))
                dve.tensor_reduce(yr[:, :], big[:, :, :], AX, ALU.add).then_inc(s_y, 1)
                dve.wait_ge(s_yt, 1)
                dve.tensor_copy(y[:, :, TP:T].rearrange("p m b -> p b m"),
                                ps[:, 1, 0:64].rearrange("p (b m) -> p b m", b=TS))

            @block.scalar
            def _(act):
                act.wait_ge(s_cp, 1)
                act.activation(vs[:, 5, :], vs[:, 5, :], ACT.Exp, scale=DECAY).then_inc(s_cp, 1)


def nsa_prompt(g, uT, cat):
    nc, d, ps, sb, sem, link = g.nc, g.d, g.ps, g.sb, g.sem, g.link
    ident, cst, vcol = g.ident, g.cst, g.vcol
    with ExitStack() as st:
        vnat = sb(st, "vnat", [P, 2, 2, 256])
        gates = sb(st, "gates", [P, 2, 48])
        kcb = sb(st, "kcb", [P, 2, NCB])
        vcb = sb(st, "vcb", [NCB, 4, 64])
        with ExitStack() as s1:
            w1 = sb(s1, "w1", [P, 2, 32, P])
            w2 = sb(s1, "w2", [P, 2, 64])
            hid = sb(s1, "hid", [P, 2, 2, 2, NCB])
            s_in, s_sg, s_mm, s_cp, s_h = (sem(n) for n in ("np_in", "np_gates", "np_mm", "np_copied", "np_hid"))
            with nc.Block() as block:
                @block.sync
                def _(sp):
                    sp.dma_start(w1[:, :, :, :], d["cmp_w1_twice"]).then_inc(s_in, 16)
                    sp.dma_start(w2[:, :, :], d["cmp_w2"]).then_inc(s_in, 16)

                @block.tensor
                def _(pe):
                    for n, c0 in enumerate((C_VS, C_VW)):
                        for t in range(2):
                            for p in range(2):
                                mm = pe.transpose(ps[:, n, (2 * t + p) * P:(2 * t + p + 1) * P],
                                                  uT[:, c0 + p, t * P:(t + 1) * P], ident)
                        mm.then_inc(s_mm, 1)
                    pe.wait_ge(s_sg, 1)
                    for t in range(2):
                        mm = pe.transpose(ps[:, 2, t * 48:t * 48 + 48], uT[0:48, C_GL, t * P:(t + 1) * P],
                                          ident[0:48, 0:48])
                    mm.then_inc(s_mm, 1)
                    pe.wait_ge(s_in, 32)
                    for kv in range(2):
                        for h in range(2):
                            rows = slice(64 * h, 64 * h + 64)
                            for l in range(32):
                                mm = pe.matmul(ps[:, 3 + 2 * kv + h, 0:2 * NCB], w1[rows, kv, l, :],
                                               uT[rows, C_KC + 2 * kv:C_KC + 2 * kv + 2, l:l + 16 * (NCB - 1) + 1:16],
                                               start=(l == 0), stop=(l == 31))
                        mm.then_inc(s_mm, 1)
                    pe.wait_ge(s_h, 4)
                    for h in range(2):
                        for p in range(2):
                            pe.matmul(ps[64 * h:64 * h + 64, 7, p * NCB:(p + 1) * NCB], w2[:, 0, :],
                                      hid[:, 0, h, p, :], start=True, stop=True)
                    for h in range(2):
                        for p in range(2):
                            kh = 2 * p + h
                            mm = pe.matmul(ps[0:NCB, 7, 64 + kh * 64:128 + kh * 64], hid[:, 1, h, p, :],
                                           w2[:, 1, :], start=True, stop=True)
                    mm.then_inc(s_mm, 1)

                @block.scalar
                def _(act):
                    act.activation(uT[0:48, C_GL, :], uT[0:48, C_GL, :], ACT.Sigmoid).then_inc(s_sg, 1)
                    for kv in range(2):
                        act.wait_ge(s_mm, 4 + kv)
                        for h in range(2):
                            act.activation(hid[:, kv, h, :, :],
                                           ps[:, 3 + 2 * kv + h, 0:2 * NCB].rearrange("p (a c) -> p a c", a=2),
                                           ACT.Gelu_apprx_tanh, bias=vcol("b1", kv)).then_inc(s_h, 1)

                @block.vector
                def _(dve):
                    for n in range(2):
                        dve.wait_ge(s_mm, n + 1)
                        dve.tensor_copy(vnat[:, n, :, :].rearrange("p t c -> p (t c)"), ps[:, n, :])
                    dve.wait_ge(s_mm, 3)
                    dve.tensor_copy(gates[:, :, :].rearrange("p t c -> p (t c)"), ps[:, 2, 0:96])
                    dve.wait_ge(s_mm, 6)
                    dve.tensor_copy(kcb[:, :, :].rearrange("p a c -> p (a c)"), ps[:, 7, 0:2 * NCB])
                    dve.tensor_copy(vcb[:, :, :].rearrange("p a c -> p (a c)"), ps[0:NCB, 7, 64:320])

        gates_p = sb(st, "gates_p", [P, 2, 48])
        S = sb(st, "S", [P, 2, 3, TP])
        mx, nm, sm, gr = (sb(st, n, [P, 2, 3]) for n in ("mx", "nm", "sm", "gr"))
        pT = sb(st, "pT", [P, 2, 5, P])
        units = [(p, gq, t, h) for p in range(2) for gq in range(4) for t in range(2) for h in range(2)]
        N = len(units)
        s_pad, s_sc, s_m, s_nm, s_ex, s_p, s_tr, s_pt, s_pv, s_o = (sem(n) for n in (
            "padded", "scores", "masked", "maxima", "exps", "weights", "turned", "turned_copied", "products", "taken"))
        with nc.Block() as block:
            @block.tensor
            def _(pe):
                def scores(u):
                    p, gq, t, h = units[u]
                    rows = slice(64 * h, 64 * h + 64)
                    q = uT[rows, C_Q + 4 * p + gq, t * P:(t + 1) * P]
                    if u >= 2:
                        pe.wait_ge(s_m, u - 1)
                    pe.matmul(ps[:, h, 0:TP], q, uT[rows, C_KS + p, 0:TP], start=True, stop=True)
                    pe.matmul(ps[:, h, TP:2 * TP], q, uT[rows, C_KW + p, 0:TP], start=True, stop=True)
                    pe.matmul(ps[:, 2 + h, 0:NCB], q, kcb[rows, p, :], start=True, stop=True).then_inc(s_sc, 1)

                def turn(u):
                    pe.wait_ge(s_p, u + 1)
                    if u >= 1:
                        pe.wait_ge(s_pt, u)
                    for n in range(4):
                        pe.transpose(ps[:, 4, n * P:(n + 1) * P], S[:, u % 2, n // 2, (n % 2) * P:(n % 2 + 1) * P], ident)
                    pe.transpose(ps[0:NCB, 5, 0:P], S[:, u % 2, 2, 0:NCB], ident).then_inc(s_tr, 1)

                def pv(u):
                    p, gq, t, h = units[u]
                    pe.wait_ge(s_pt, u + 1)
                    pair = u // 2
                    if h == 0 and pair >= 2:
                        pe.wait_ge(s_o, pair - 1)
                    kc = (2 * p + h) * 64
                    out = ps[64 * h:64 * h + 64, 6 + pair % 2, 0:P]
                    for n in range(2):
                        for kt in range(t + 1):
                            pe.matmul(out, vnat[:, n, kt, kc:kc + 64], pT[:, u % 2, 2 * n + kt, :],
                                      start=(n == 0 and kt == 0), stop=False)
                    pe.matmul(out, vcb[:, 2 * p + h, :], pT[0:NCB, u % 2, 4, :], start=False, stop=True).then_inc(s_pv, 1)

                scores(0)
                for u in range(N):
                    if u + 1 < N:
                        scores(u + 1)
                    turn(u)
                    if u >= 1:
                        pv(u - 1)
                pv(N - 1)

            @block.vector
            def _(dve):
                def first(u):
                    p, gq, t, h = units[u]
                    dve.wait_ge(s_sc, u + 1)
                    if u >= 2:
                        dve.wait_ge(s_tr, u - 1)
                    mask = cst("causal")[:, t * TP:(t + 1) * TP].unsqueeze(1).broadcast_to([P, 2, TP])
                    dve.tensor_tensor(S[:, u % 2, 0:2, :], ps[:, h, :].rearrange("p (a k) -> p a k", a=2), mask, ALU.add)
                    dve.tensor_tensor(S[:, u % 2, 2, 0:NCB], ps[:, 2 + h, 0:NCB],
                                      cst("cmask")[:, t * NCB:(t + 1) * NCB], ALU.add).then_inc(s_m, 1)
                    dve.wait_ge(s_m, u + 1)
                    link(dve, dve.tensor_reduce(mx[:, u % 2, :], S[:, u % 2, :, :], AX, ALU.max))
                    dve.tensor_scalar(nm[:, u % 2, :], mx[:, u % 2, :], -0.125, None, ALU.mult).then_inc(s_nm, 1)

                def second(u):
                    p, gq, t, h = units[u]
                    a = ((2 * p + h) * 4 + gq) * 3
                    dve.wait_ge(s_ex, u + 1)
                    link(dve, dve.reciprocal(gr[:, u % 2, :], sm[:, u % 2, :]))
                    link(dve, dve.tensor_tensor(gr[:, u % 2, :], gr[:, u % 2, :], gates_p[:, t, a:a + 3], ALU.mult))
                    dve.tensor_scalar(S[:, u % 2, 2, 0:NCB], S[:, u % 2, 2, 0:NCB], gr[:, u % 2, 2:3], None, ALU.mult)
                    dve.tensor_tensor(S[:, u % 2, 0:2, :], S[:, u % 2, 0:2, :],
                                      gr[:, u % 2, 0:2].unsqueeze(2).broadcast_to([P, 2, TP]), ALU.mult
                                      ).then_inc(s_p, 1)

                for t in range(2):
                    src = gates[:, t, :].rearrange("p (h n) -> p h n", n=3)
                    dst = gates_p[:, t, :].rearrange("p (h n) -> p h n", n=3)
                    dve.tensor_copy(dst[:, :, 0:2], src[:, :, 1:3])
                    dve.tensor_scalar(dst[:, :, 2], src[:, :, 0], cst("cvalid")[:, t:t + 1], None, ALU.mult)
                link(dve, dve.memset(S[:, :, 2, :], NEG))
                for u in range(N + 1):
                    if u < N:
                        first(u)
                    if u >= 1:
                        second(u - 1)

            @block.scalar
            def _(act):
                def exps(u):
                    act.wait_ge(s_nm, u + 1)
                    for n, w in enumerate((TP, TP, NCB)):
                        ins = act.activation(S[:, u % 2, n, 0:w], S[:, u % 2, n, 0:w], ACT.Exp, scale=0.125,
                                             bias=nm[:, u % 2, n:n + 1], accum_out=sm[:, u % 2, n:n + 1])
                    ins.then_inc(s_ex, 1)

                def copy(u):
                    act.wait_ge(s_tr, u + 1)
                    if u >= 2:
                        act.wait_ge(s_pv, u - 1)
                    act.activation(pT[:, u % 2, 0:4, :].rearrange("p n t -> p (n t)"), ps[:, 4, :], ACT.Copy)
                    act.activation(pT[0:NCB, u % 2, 4, :], ps[0:NCB, 5, 0:P], ACT.Copy).then_inc(s_pt, 1)

                def take(pair):
                    p, gq, t, _ = units[2 * pair]
                    act.wait_ge(s_pv, 2 * pair + 2)
                    act.activation(cat[:, 8 + 4 * p + gq, t * P:(t + 1) * P], ps[:, 6 + pair % 2, 0:P],
                                   ACT.Copy).then_inc(s_o, 1)

                for u in range(N + 2):
                    if u < N:
                        exps(u)
                    if 1 <= u <= N:
                        copy(u - 1)
                    if u >= 3 and u % 2 == 1:
                        take((u - 3) // 2)


def nsa_sample(g, uT, cat):
    nc, d, ps, sb, sem, link, alink = g.nc, g.d, g.ps, g.sb, g.sem, g.link, g.alink
    ident, ones, cst, vcol = g.ident, g.ones, g.cst, g.vcol
    PW = 2 * P
    with ExitStack() as st:
        free = uT[:, 0:RWC, :].rearrange("p c t -> p (c t)")
        Q = free[:, 0:16 * P]
        vcb = sb(st, "vcb", [P, 8, 256])
        gate = sb(st, "gate", [P, 3])
        ptab = sb(st, "ptab", [1, P], I32)
        s_q, s_g, s_t, s_ge = sem("q_zero"), sem("gate_mm"), sem("table_in"), sem("gate_rows")
        with ExitStack() as s1:
            t8 = sb(s1, "t8", [P, 3, 8])
            with nc.Block() as block:
                @block.sync
                def _(sp):
                    sp.dma_start(ptab[:, :], d["page_table"]).then_inc(s_t, 16)
                    sp.wait_ge(s_t, 16)

                @block.tensor
                def _(pe):
                    for n in range(3):
                        mm = pe.matmul(ps[:, 0, 8 * n:8 * n + 8], cst("gate", 48)[:, n * P:(n + 1) * P],
                                       uT[0:48, C_GL, TP:T], start=True, stop=True)
                    mm.then_inc(s_g, 1)

                @block.vector
                def _(dve):
                    link(dve, dve.memset(Q[:, :], 0.0))
                    for p in range(2):
                        for h in range(2):
                            for gq in range(4):
                                a = p * 1088 + h * 4 + gq
                                rows = slice(64 * h, 64 * h + 64)
                                dve.tensor_copy(Q[rows, a:a + 136 * 7 + 1:136], uT[rows, C_Q + 4 * p + gq, TP:T])
                    dve.wait_ge(s_g, 1)
                    link(dve, dve.tensor_tensor(t8[:, :, :], ps[:, 0, 0:24].rearrange("p (n b) -> p n b", n=3),
                                                cst("bsel").unsqueeze(1).broadcast_to([P, 3, 8]), ALU.mult))
                    dve.tensor_reduce(gate[:, :], t8[:, :, :], AX, ALU.add)

        def q_of(p, b):
            n = p * 8 + b
            return Q[:, n * P:(n + 1) * P]

        with ExitStack() as s1:
            pages = sb(s1, "pages", [P, 2, PG, 3 * PW])
            w1 = free[:, 16 * P:48 * P].rearrange("p (a l h) -> p a l h", a=2, l=16)
            w2 = sb(s1, "w2", [P, 2, 64])
            lo = sb(s1, "lo", [P, 512])
            hs = sb(s1, "hs", [P, 4, NCS])
            hid = sb(s1, "hid", [P, 4, NCS])
            kcb = sb(s1, "kcb", [P, 2, NCS])
            s_in = sem("weights_in")
            s_pg = [sem(f"pages{k}") for k in range(2)]
            s_done, s_lh, s_lo, s_hs, s_hid, s_cb, s_cbc, s_c = (sem(n) for n in (
                "pages_used", "lohi", "lo_copied", "sums", "hidden", "compressed", "compressed_copied", "c_scores"))
            with nc.Block() as block:
                @block.sync
                def _(sp):
                    sp.dma_start(w1[:, :, :, :], d["cmp_w1"]).then_inc(s_in, 16)
                    sp.dma_start(w2[:, :, :], d["cmp_w2"]).then_inc(s_in, 16)
                    for b in range(TS):
                        if b >= 2:
                            sp.wait_ge(s_done, b - 1)
                        with sp.Fori(0, PG) as j:
                            page = sp.value_load(ptab[0:1, ds(j + b * PG, 1)], min_val=0, max_val=N_PHYS - 1)
                            sp.dma_start(pages[:, b % 2, ds(j, 1), :],
                                         d["k_pages"][ds(page, 1), :, :].rearrange("a p n -> p a n")
                                         ).then_inc(s_pg[b % 2], 16)

                @block.tensor
                def _(pe):
                    pe.wait_ge(s_in, 32)
                    for b in range(TS):
                        pe.wait_ge(s_pg[b % 2], 16 * PG * (b // 2 + 1))
                        for kv in range(2):
                            m = 2 * b + kv
                            if m >= 1:
                                pe.wait_ge(s_hs, m)
                            for part in range(2):
                                for l in range(8):
                                    chs = pages[:, b % 2, :, kv * PW + l * 32:kv * PW + (l + 1) * 32].rearrange(
                                        "p g (k c) -> p k g c", k=4)
                                    mm = pe.matmul(ps[:, 5 + part, :], w1[:, kv, 8 * part + l, :], chs,
                                                   start=(l == 0), stop=(l == 7))
                                mm.then_inc(s_lh, 1)
                            if kv == 1:
                                pe.wait_ge(s_lh, 2 * m + 2)
                            pe.wait_ge(s_hid, m + 1)
                            if kv == 0:
                                for kh in range(4):
                                    mm = pe.matmul(ps[64 * (kh % 2):64 * (kh % 2) + 64, 7,
                                                      (kh // 2) * P:(kh // 2) * P + NCS],
                                                   w2[:, 0, :], hid[:, kh, :], start=True, stop=True)
                                mm.then_inc(s_cb, 1)
                                pe.wait_ge(s_cbc, m + 1)
                                for p in range(2):
                                    mm = pe.matmul(ps[:, 4, 0:NCS], q_of(p, b), kcb[:, p, :],
                                                   start=(b == 0 and p == 0), stop=(b == TS - 1 and p == 1))
                                mm.then_inc(s_c, 1)
                            else:
                                for kh in range(4):
                                    mm = pe.matmul(ps[0:NCS, 7, 256 + kh * 64:320 + kh * 64], hid[:, kh, :],
                                                   w2[:, 1, :], start=True, stop=True)
                                mm.then_inc(s_cb, 1)
                                pe.wait_ge(s_cbc, m + 1)
                        for p in range(2):
                            for q in range(4):
                                mm = pe.matmul(ps[:, q, :], q_of(p, b),
                                               pages[:, b % 2, 4 * q:4 * q + 4, 2 * PW + p * P:2 * PW + (p + 1) * P],
                                               start=(b == 0 and p == 0), stop=(b == TS - 1 and p == 1))
                        mm.then_inc(s_done, 1)

                @block.scalar
                def _(act):
                    for m in range(2 * TS):
                        act.wait_ge(s_lh, 2 * m + 1)
                        act.activation(lo[:, :], ps[:, 5, :], ACT.Copy).then_inc(s_lo, 1)
                        act.wait_ge(s_hs, m + 1)
                        act.activation(hid[:, :, :], hs[:, :, :], ACT.Gelu_apprx_tanh, bias=vcol("b1", m % 2)
                                       ).then_inc(s_hid, 1)

                @block.vector
                def _(dve):
                    for m in range(2 * TS):
                        dve.wait_ge(s_lh, 2 * m + 2)
                        dve.wait_ge(s_lo, m + 1)
                        dve.tensor_tensor(hs[:, :, :], ps[:, 6, :].rearrange("p (k c) -> p k c", k=4)[:, :, 1:P],
                                          lo[:, :].rearrange("p (k c) -> p k c", k=4)[:, :, 0:NCS], ALU.add
                                          ).then_inc(s_hs, 1)
                        dve.wait_ge(s_cb, m + 1)
                        if m % 2 == 0:
                            if m >= 2:
                                dve.wait_ge(s_c, m // 2)
                            dve.tensor_copy(kcb[:, :, :], ps[:, 7, 0:256].rearrange("p (a c) -> p a c", a=2)[:, :, 0:NCS]
                                            ).then_inc(s_cbc, 1)
                        else:
                            dve.tensor_copy(vcb[0:NCS, m // 2, :], ps[0:NCS, 7, 256:512]).then_inc(s_cbc, 1)

        VS = 4
        vpages = sb(st, "vpages", [P, VS, PG, PW])
        s_vp = [sem(f"vpages{k}") for k in range(VS)]

        def value_pages(eng, b):
            with eng.Fori(0, PG) as j:
                page = eng.value_load(ptab[0:1, ds(j + b * PG, 1)], min_val=0, max_val=N_PHYS - 1)
                eng.dma_start(vpages[:, b % VS, ds(j, 1), :],
                              d["slc_v"][ds(page, 1), :, :].rearrange("a p n -> p a n")).then_inc(s_vp[b % VS], 16)

        with ExitStack() as s1:
            wk = sb(s1, "wk", [P, TS, 2, 512])
            s_in, s_new, s_w = sem("window_in"), sem("window_new"), sem("window_scores")
            with nc.Block() as block:
                @block.sync
                def _(sp):
                    sp.dma_start(wk[:, :, :, :], d["win_k"]).then_inc(s_in, 16)
                    value_pages(sp, 0)
                    value_pages(sp, 2)

                @block.scalar
                def _(act):
                    value_pages(act, 1)
                    value_pages(act, 3)

                @block.vector
                def _(dve):
                    dve.wait_ge(s_in, 16)
                    dve.tensor_copy(wk[:, :, :, 0], uT[:, C_KW:C_KW + 2, TP:T].rearrange("p a b -> p b a")
                                    ).then_inc(s_new, 1)

                @block.tensor
                def _(pe):
                    pe.wait_ge(s_new, 1)
                    for b in range(TS):
                        for p in range(2):
                            pe.matmul(ps[:, 5, :], q_of(p, b), wk[:, b, p, :],
                                      start=(b == 0 and p == 0), stop=(b == TS - 1 and p == 1))
                            pe.matmul(ps[:, 6, 0:1], q_of(p, b), uT[:, C_KS + p, TP + b:TP + b + 1],
                                      start=(b == 0 and p == 0), stop=(b == TS - 1 and p == 1))

        A_W, A_C, A_N, A_E = 2048, 2560, 2560 + NCS, 2560 + P
        W = sb(st, "W", [P, A_E])
        pT = sb(st, "pT", [P, 21, P])
        nm, sm, gr = (sb(st, n, [P, 3]) for n in ("nm", "sm", "gr"))
        with ExitStack() as s1:
            imp = sb(s1, "imp", [32, 4 * NBLK + 4])
            ims = sb(s1, "ims", [32, NBLK])
            wk2 = sb(s1, "wk2", [32, NBLK])
            t8 = sb(s1, "t8", [32, 8])
            blk = sb(s1, "blk", [P, NBLK])
            s_v, s_a, s_p = sem("nm_ready"), sem("exp_ready"), sem("pe_ready")
            with nc.Block() as block:
                @block.vector
                def _(dve):
                    link(dve, dve.tensor_copy(W[:, A_C:A_C + NCS], ps[:, 4, 0:NCS]))
                    link(dve, dve.tensor_reduce(nm[:, 0:1], W[:, A_C:A_C + NCS], AX, ALU.max))
                    dve.tensor_scalar(nm[:, 0:1], nm[:, 0:1], -0.125, None, ALU.mult).then_inc(s_v, 1)
                    dve.memset(imp[:, :], 0.0)
                    dve.wait_ge(s_a, 1)
                    link(dve, dve.reciprocal(gr[:, 0:1], sm[:, 0:1]))
                    dve.tensor_scalar(W[:, A_C:A_C + NCS], W[:, A_C:A_C + NCS], gr[:, 0:1], None, ALU.mult
                                      ).then_inc(s_v, 1)
                    dve.wait_ge(s_p, 1)
                    link(dve, dve.tensor_copy(imp[:, 1:NCS + 1], ps[0:32, 7, 0:NCS]))
                    quad = imp[:, 0:4 * NBLK].rearrange("p (j q) -> p j q", q=4)
                    nxt = imp[:, 4:4 * NBLK + 4].rearrange("p (j q) -> p j q", q=4)
                    dve.tensor_tensor(wk2[:, :], quad[:, :, 0], nxt[:, :, 0], ALU.add)
                    link(dve, dve.tensor_reduce(ims[:, :], quad[:, :, 1:4], AX, ALU.add))
                    link(dve, dve.scalar_tensor_tensor(ims[:, :], wk2[:, :], 0.5, ims[:, :], ALU.mult, ALU.add))
                    dve.memset(ims[:, 0:1], 1e30)
                    link(dve, dve.memset(ims[:, NBLK - 2:NBLK], 1e30))
                    link(dve, dve.max(t8[:, :], ims[:, :]))
                    link(dve, dve.match_replace(wk2[:, :], t8[:, :], ims[:, :], -3e38))
                    link(dve, dve.max(t8[:, :], wk2[:, :]))
                    link(dve, dve.match_replace(ims[:, :], t8[:, :], wk2[:, :], -3e38))
                    dve.tensor_scalar(wk2[:, :], ims[:, :], -2e38, None, ALU.is_lt).then_inc(s_v, 1)
                    dve.wait_ge(s_p, 2)
                    link(dve, dve.tensor_scalar(blk[:, :], ps[:, 7, P:P + NBLK], -1.0, -NEG, ALU.add, ALU.mult))
                    for q in range(4):
                        dve.tensor_tensor(W[:, 512 * q:512 * q + 512].rearrange("p (j l) -> p j l", l=64),
                                          ps[:, q, :].rearrange("p (j l) -> p j l", l=64),
                                          blk[:, 8 * q:8 * q + 8].unsqueeze(2).broadcast_to([P, 8, 64]), ALU.add)
                    dve.tensor_copy(W[:, A_W:A_C], ps[:, 5, :])
                    link(dve, dve.tensor_copy(W[:, A_N:A_E], ps[:, 6, 0:1]))
                    dve.tensor_reduce(nm[:, 1:2], W[:, 0:A_W], AX, ALU.max)
                    link(dve, dve.tensor_reduce(nm[:, 2:3], W[:, A_W:A_C], AX, ALU.max))
                    link(dve, dve.tensor_tensor(nm[:, 1:2], nm[:, 1:2], W[:, A_N:A_E], ALU.max))
                    dve.tensor_scalar(nm[:, 1:3], nm[:, 1:3], -0.125, None, ALU.mult).then_inc(s_v, 1)
                    dve.wait_ge(s_a, 2)
                    link(dve, dve.tensor_tensor(sm[:, 1:2], sm[:, 1:2], W[:, A_N:A_E], ALU.add))
                    link(dve, dve.reciprocal(gr[:, 1:3], sm[:, 1:3]))
                    link(dve, dve.tensor_tensor(gr[:, 1:3], gr[:, 1:3], gate[:, 1:3], ALU.mult))
                    dve.tensor_scalar(W[:, 0:A_W], W[:, 0:A_W], gr[:, 1:2], None, ALU.mult)
                    dve.tensor_scalar(W[:, A_N:A_E], W[:, A_N:A_E], gr[:, 1:2], None, ALU.mult)
                    dve.tensor_scalar(W[:, A_W:A_C], W[:, A_W:A_C], gr[:, 2:3], None, ALU.mult)
                    dve.tensor_scalar(W[:, A_C:A_N], W[:, A_C:A_N], gate[:, 0:1], None, ALU.mult)

                @block.scalar
                def _(act):
                    act.wait_ge(s_v, 1)
                    act.activation(W[:, A_C:A_N], W[:, A_C:A_N], ACT.Exp, scale=0.125, bias=nm[:, 0:1],
                                   accum_out=sm[:, 0:1]).then_inc(s_a, 1)
                    act.wait_ge(s_v, 4)
                    act.activation(W[:, 0:A_W], W[:, 0:A_W], ACT.Exp, scale=0.125, bias=nm[:, 1:2],
                                   accum_out=sm[:, 1:2])
                    act.activation(W[:, A_N:A_E], W[:, A_N:A_E], ACT.Exp, scale=0.125, bias=nm[:, 1:2])
                    act.activation(W[:, A_W:A_C], W[:, A_W:A_C], ACT.Exp, scale=0.125, bias=nm[:, 2:3],
                                   accum_out=sm[:, 2:3]).then_inc(s_a, 1)

                @block.tensor
                def _(pe):
                    pe.wait_ge(s_v, 2)
                    pe.matmul(ps[0:32, 7, 0:NCS], cst("gsum"), W[:, A_C:A_N], start=True, stop=True).then_inc(s_p, 1)
                    pe.wait_ge(s_v, 3)
                    pe.matmul(ps[:, 7, P:P + NBLK], cst("gexp", 32), wk2[:, :], start=True, stop=True).then_inc(s_p, 1)

        with ExitStack() as s1:
            wv = sb(s1, "wv", [P, TS, 4, PW])
            diag = sb(s1, "diag", [P, 2, P])
            o = sb(s1, "o", [P, P])
            t = sb(s1, "t", [P, P])
            t2 = sb(s1, "t2", [P, P])
            s_in, s_d, s_tr, s_cp, s_pv, s_o, s_z = (sem(n) for n in (
                "wv_in", "diag_made", "w_turned", "w_copied", "pv_done", "o_copied", "zeroed"))
            with nc.Block() as block:
                @block.sync
                def _(sp):
                    sp.dma_start(wv[:, :, :, :], d["win_v"]).then_inc(s_in, 16)
                    sp.wait_ge(g.stored, g.n_stored[0])
                    for b in range(VS, TS, 2):
                        sp.wait_ge(s_pv, b - VS + 1)
                        value_pages(sp, b)

                @block.scalar
                def _(act):
                    for b in range(VS + 1, TS, 2):
                        act.wait_ge(s_pv, b - VS + 1)
                        value_pages(act, b)

                @block.tensor
                def _(pe):
                    pe.wait_ge(s_d, 1)
                    for n in range(2):
                        pe.matmul(ps[:, 6, n * P:(n + 1) * P], ones, diag[:, n, :], start=True, stop=True)
                    for n in range(21):
                        if n % 4 == 0 and n >= 8:
                            pe.wait_ge(s_cp, n // 4 - 1)
                        w = P if n < 20 else NCS
                        mm = pe.transpose(ps[0:w, (n // 4) % 2, (n % 4) * P:(n % 4 + 1) * P], W[:, n * P:n * P + w], ident)
                        if n % 4 == 3 or n == 20:
                            mm.then_inc(s_tr, 1)
                    pe.wait_ge(s_cp, 6)
                    pe.wait_ge(s_in, 16)
                    for b in range(TS):
                        pe.wait_ge(s_vp[b % VS], 16 * PG * (b // VS + 1))
                        for p in range(2):
                            cols = slice(p * 64 + b * 8, p * 64 + b * 8 + 8)
                            pc = slice(p * P, (p + 1) * P)
                            for n in range(16):
                                pe.matmul(ps[:, 7, cols], vpages[:, b % VS, n, pc], pT[:, n, cols],
                                          start=(n == 0), stop=False)
                            for n in range(4):
                                pe.matmul(ps[:, 7, cols], wv[:, b, n, pc], pT[:, 16 + n, cols], start=False, stop=False)
                            mm = pe.matmul(ps[:, 7, cols], vcb[0:NCS, b, pc], pT[0:NCS, 20, cols],
                                           start=False, stop=True)
                        mm.then_inc(s_pv, 1)

                @block.vector
                def _(dve):
                    dve.tensor_scalar(diag[:, 0, :], ident, W[:, A_N:A_E], None, ALU.mult)
                    link(dve, dve.tensor_scalar(diag[:, 1, :], ident, W[:, A_W:A_W + 1], None, ALU.mult))
                    dve.memset(W[:, A_W:A_W + 1], 0.0).then_inc(s_d, 1)
                    for n in range(6):
                        dve.wait_ge(s_tr, n + 1)
                        k = 4 if n < 5 else 1
                        w = P if n < 5 else NCS
                        dve.tensor_copy(pT[0:w, 4 * n:4 * n + k, :].rearrange("p n t -> p (n t)"), ps[0:w, n % 2, 0:k * P]
                                        ).then_inc(s_cp, 1)
                    for n, (c0, dst) in enumerate(((C_VS, t), (C_VW, t2))):
                        new = uT[:, c0:c0 + 2, TP:T]
                        dve.tensor_tensor(dst[:, :].rearrange("p (a b r) -> p a b r", a=2, b=8),
                                          ps[:, 6, n * P:(n + 1) * P].rearrange("p (a b r) -> p a b r", a=2, b=8),
                                          new.unsqueeze(3).broadcast_to([P, 2, 8, 8]), ALU.mult)
                    link(dve, dve.memset(o[:, 0:1], 0.0))
                    dve.wait_ge(s_pv, TS)
                    link(dve, dve.tensor_tensor(t[:, :], t[:, :], t2[:, :], ALU.add))
                    link(dve, dve.tensor_tensor(o[:, :], ps[:, 7, 0:P], t[:, :], ALU.add))
                    for p in range(2):
                        for h in range(2):
                            rows = slice(64 * h, 64 * h + 64)
                            src = o[rows, 64 * p:64 * p + 64].rearrange("q (b k e) -> q k e b", b=8, k=2)[:, h]
                            dve.tensor_copy(cat[rows, 8 + 4 * p:12 + 4 * p, TP:T], src)


def cross(g, memk, memv, xT, ring):
    nc, d, ps, sb, sem, link = g.nc, g.d, g.ps, g.sb, g.sem, g.link
    ident, cst = g.ident, g.cst
    SC = float(P) ** -0.5
    with ExitStack() as st:
        qx = sb(st, "qx", [P, 4, T])
        ox = sb(st, "ox", [P, 4, T])
        wo = sb(st, "wo", [P, 4, D])
        ck = sb(st, "ck", [P, TS, 4, TP])
        cv = sb(st, "cv", [P, TS, 2, 512])
        s_in = sem("x_in")

        def early(sp):
            g.prime(sp, d["xq"], ring)
            sp.dma_start(ck[:, :, :, :], d["mem_k"]).then_inc(s_in, 16)
            sp.dma_start(cv[:, :, :, :], d["mem_v"]).then_inc(s_in, 16)
            sp.dma_start(wo[:, :, :], d["xo"]).then_inc(s_in, 16)

        with ExitStack() as s1:
            hx = sb(s1, "hx", [P, KC, T])
            g.rms(xT, hx, "x", KC, T, ahead=early)
            g.project(d["xq"], hx, qx, 4, ring)
        Q = sb(st, "Q", [P, 32 * 32])
        S = sb(st, "S", [P, 9, TP])
        pT = sb(st, "pT", [P, 9, 2, P])
        mx, nm, sm, rs = (sb(st, n, [P, 9]) for n in ("mx", "nm", "sm", "rs"))
        s_q, s_sc, s_nm, s_ex, s_p, s_tr, s_cp, s_pv, s_o = (sem(n) for n in (
            "x_q", "x_scores", "x_max", "x_exp", "x_weights", "x_turned", "x_copied", "x_products", "x_taken"))
        with nc.Block() as block:
            @block.tensor
            def _(pe):
                for u in range(8):
                    h, t = u // 2, u % 2
                    pe.matmul(ps[:, u // 2, t * TP:(t + 1) * TP], qx[:, h, t * P:(t + 1) * P], memk[:, h, :],
                              start=True, stop=True).then_inc(s_sc, 1)
                pe.wait_ge(s_in, 48)
                pe.wait_ge(s_q, 1)
                for n in range(32):
                    mm = pe.matmul(ps[0:32, 4, 0:TP], Q[:, n * 32:(n + 1) * 32], ck[:, n // 4, n % 4, :],
                                   start=(n == 0), stop=(n == 31))
                mm.then_inc(s_sc, 1)
                for u in range(9):
                    r = P if u < 8 else 32
                    pe.wait_ge(s_p, u + 1)
                    if u >= 2:
                        pe.wait_ge(s_cp, u - 1)
                    for m in range(2):
                        mm = pe.transpose(ps[:, 5 + u % 2, m * P:m * P + r], S[0:r, u, m * P:(m + 1) * P], ident[0:r, 0:r])
                    mm.then_inc(s_tr, 1)
                for u in range(8):
                    h = u // 2
                    pe.wait_ge(s_cp, u + 1)
                    if u >= 4:
                        pe.wait_ge(s_o, u - 3)
                    for m in range(2):
                        mm = pe.matmul(ps[:, u % 4, 0:P], memv[:, m, h * P:(h + 1) * P], pT[:, u, m, :],
                                       start=(m == 0), stop=(m == 1))
                    mm.then_inc(s_pv, 1)
                pe.wait_ge(s_cp, 9)
                for n in range(32):
                    b, h = n // 4, n % 4
                    for m in range(2):
                        mm = pe.matmul(ps[:, 7, n:n + 1], cv[:, b, m, h * P:(h + 1) * P], pT[:, 8, m, n:n + 1],
                                       start=(m == 0), stop=(m == 1))
                mm.then_inc(s_pv, 1)

            @block.vector
            def _(dve):
                link(dve, dve.memset(Q[:, :], 0.0))
                dve.tensor_copy(Q[:, 0:33 * 31 + 1:33].rearrange("p (b h) -> p b h", h=4),
                                qx[:, :, TP:T].rearrange("p h b -> p b h")).then_inc(s_q, 1)
                for u in range(9):
                    r = P if u < 8 else 32
                    src = ps[0:r, u // 2, (u % 2) * TP:(u % 2 + 1) * TP]
                    dve.wait_ge(s_sc, min(2 * (u // 2) + 2, 9))
                    link(dve, dve.tensor_reduce(mx[0:r, u:u + 1], src, AX, ALU.max))
                    dve.tensor_scalar(nm[0:r, u:u + 1], mx[0:r, u:u + 1], -SC, None, ALU.mult).then_inc(s_nm, 1)
                for u in range(9):
                    r = P if u < 8 else 32
                    dve.wait_ge(s_ex, u + 1)
                    link(dve, dve.reciprocal(rs[0:r, u:u + 1], sm[0:r, u:u + 1]))
                    dve.tensor_scalar(S[0:r, u, :], S[0:r, u, :], rs[0:r, u:u + 1], None, ALU.mult).then_inc(s_p, 1)
                for u in range(9):
                    r = P if u < 8 else 32
                    dve.wait_ge(s_tr, u + 1)
                    dve.tensor_copy(pT[:, u, :, 0:r], ps[:, 5 + u % 2, 0:TP].rearrange("p (m t) -> p m t", m=2)[:, :, 0:r]
                                    ).then_inc(s_cp, 1)
                for u in range(8):
                    dve.wait_ge(s_pv, u + 1)
                    dve.tensor_copy(ox[:, u // 2, (u % 2) * P:(u % 2 + 1) * P], ps[:, u % 4, 0:P]).then_inc(s_o, 1)
                dve.wait_ge(s_pv, 9)
                dve.tensor_copy(ox[:, :, TP:T].rearrange("p h b -> p b h"),
                                ps[:, 7, 0:32].rearrange("p (b h) -> p b h", h=4))

            @block.scalar
            def _(act):
                for u in range(9):
                    r = P if u < 8 else 32
                    act.wait_ge(s_nm, min(2 * (u // 2) + 2, 9))
                    act.activation(S[0:r, u, :], ps[0:r, u // 2, (u % 2) * TP:(u % 2 + 1) * TP], ACT.Exp, scale=SC,
                                   bias=nm[0:r, u:u + 1], accum_out=sm[0:r, u:u + 1]).then_inc(s_ex, 1)

        s_mm, s_add = sem("xo_products"), sem("xo_added")
        with nc.Block() as block:
            @block.tensor
            def _(pe):
                for m in range(KC):
                    if m >= 4:
                        pe.wait_ge(s_add, m - 3)
                    for c in range(4):
                        mm = pe.matmul(ps[:, m % 4, 0:T], wo[:, c, m * P:(m + 1) * P], ox[:, c, :],
                                       start=(c == 0), stop=(c == 3))
                    mm.then_inc(s_mm, 1)

            @block.vector
            def _(dve):
                for m in range(KC):
                    dve.wait_ge(s_mm, m + 1)
                    dve.tensor_tensor(xT[:, m, :], ps[:, m % 4, 0:T], xT[:, m, :], ALU.add).then_inc(s_add, 1)


def peer(g, xT, ring):
    nc, d, ps, sb, sem, link = g.nc, g.d, g.ps, g.sb, g.sem, g.link
    s_keys, s_res = g.sem("keys_in"), g.sem("residual_out")
    with ExitStack() as st:
        iT, jT, gT = (sb(st, n, [P, T]) for n in ("iT", "jT", "gT"))
        H = sb(st, "H", [P, P, T])
        spare = H[:, P // 2:P, :].rearrange("p j t -> p (j t)")
        q = spare[:, 0:16 * T].rearrange("p (c t) -> p c t", t=T)
        keys = spare[:, 16 * T:16 * T + 2048].rearrange("p (c k) -> p c k", k=P)

        def early(sp):
            g.prime(sp, d["peer_wq"], ring)
            sp.dma_start(keys, d["peer_keys"]).then_inc(s_keys, 16)

        with nc.Block() as block:
            @block.sync
            def _(sp):
                sp.dma_start(d["residual"], xT[:, :, :]).then_inc(s_res, 16)
                sp.wait_ge(s_res, 16)

        g.rms(xT, xT, "ffn", KC, T, ahead=early)
        g.project(d["peer_wq"], xT, q, 16, ring)
        activate(g, xT, H, q, keys, spare[:, 16 * T + 2048:], s_keys, iT, jT, gT, ring)
        spread(g, iT, jT, gT, H, xT, ring)
        v_stage(g, xT, H, ring)


def activate(g, hf, H, q, keys, spare, s_keys, iT, jT, gT, ring):
    nc, d, ps, sb, sem, link = g.nc, g.d, g.ps, g.sb, g.sem, g.link
    ident, cst = g.ident, g.cst
    landed, used, drained = g.landed, g.used, g.drained
    r0, N = g.rounds[0], P // RING
    g.rounds[0] += N
    LOW = -3e38
    PER = 4
    assert 3 * PER * RING <= P // 2
    with ExitStack() as st:
        s, s2, hot = (spare[:, n * 2048:(n + 1) * 2048] for n in range(3))
        s, s2 = (x.rearrange("p (c k) -> p c k", k=P) for x in (s, s2))
        hot = hot.rearrange("p (c k) -> p c k", k=16)
        cand, cand2 = (spare[:, n * 2048:(n + 1) * 2048].rearrange("p (c k) -> p c k", k=256) for n in (3, 4))
        sv = sb(st, "sv", [P, 16, 16])
        si = sb(st, "si", [P, 16, 16], U32)
        sf = sb(st, "sf", [P, 16, 16])
        cv = sb(st, "cv", [P, 8, 16])
        ci = sb(st, "ci", [P, 8, 16], U32)
        hl = sb(st, "hl", [P, 2, P], U32)
        hf2 = sb(st, "hf2", [P, 2, P])
        res = sb(st, "res", [P, 3, P])
        z = sb(st, "z", [P, 8])
        s_mm, s_cp, s_v, s_e, s_r, s_tr, s_ct = (sem(n) for n in (
            "key_scores", "scores_copied", "shifted", "exps", "choices", "choices_turned", "choices_copied"))
        parts = [(0, P), (P, P), (TP, TS)]
        with nc.Block() as block:
            @block.sync
            def _(sp):
                g.prime(sp, d["peer_u"], ring)
                with sp.Fori(1, N) as i:
                    for k in range(RING):
                        sp.wait_ge(used[k], i + r0)
                        sp.dma_start(ring[:, k, :], d["peer_u"][ds(i * RING + k, 1), :, :].rearrange("a p n -> p (a n)")
                                     ).then_inc(landed[k], 16)

            @block.tensor
            def _(pe):
                def rounds(a, b):
                    with pe.Fori(a, b) as i:
                        for k in range(RING):
                            pe.wait_ge(landed[k], (i + r0) * 16)
                            pe.wait_ge(drained[k], i + r0)
                            for c in range(KC):
                                mm = pe.matmul(ps[:, k, 0:T], ring[:, k, c * P:(c + 1) * P], hf[:, c, :],
                                               start=(c == 0), stop=(c == KC - 1))
                            mm.then_inc(used[k], 1)

                pe.wait_ge(s_keys, 16)
                for t, (a, n) in enumerate(parts):
                    if t >= 1:
                        pe.wait_ge(s_ct, t)
                    for c in range(16):
                        mm = pe.matmul(ps[0:n, 4 + c // 4, (c % 4) * P:(c % 4 + 1) * P], q[:, c, a:a + n], keys[:, c, :],
                                       start=True, stop=True)
                    mm.then_inc(s_mm, 1)
                    rounds(PER * t, PER * (t + 1))
                    pe.wait_ge(s_r, t + 1)
                    for k in range(3):
                        mm = pe.transpose(ps[:, 4, k * P:k * P + n], res[0:n, k, :], ident[0:n, 0:n])
                    mm.then_inc(s_tr, 1)
                rounds(3 * PER, N)

            @block.scalar
            def _(act):
                def rounds(a, b):
                    with act.Fori(a, b) as i:
                        for k in range(RING):
                            act.wait_ge(used[k], i + (r0 + 1))
                            act.activation(H[:, ds(i * RING + k, 1), :].rearrange("p a t -> p (a t)"), ps[:, k, 0:T],
                                           ACT.Gelu_apprx_tanh).then_inc(drained[k], 1)

                for t, (a, n) in enumerate(parts):
                    act.wait_ge(s_mm, t + 1)
                    if t >= 1:
                        act.wait_ge(s_r, t)
                    for c in range(4):
                        ins = act.activation(s[0:n, 4 * c:4 * c + 4, :].rearrange("p a k -> p (a k)"), ps[0:n, 4 + c, :],
                                             ACT.Copy)
                    ins.then_inc(s_cp, 1)
                    rounds(PER * t, PER * t + PER - 1)
                    act.wait_ge(s_v, t + 1)
                    act.activation(res[0:n, 2, :], res[0:n, 2, :], ACT.Exp).then_inc(s_e, 1)
                    rounds(PER * t + PER - 1, PER * (t + 1))
                rounds(3 * PER, P // 2 // RING)
                act.wait_ge(s_ct, 3)
                rounds(P // 2 // RING, N)

            @block.vector
            def _(dve):
                def top16(n, x, y, vals, idx, count):
                    for c in range(count):
                        last = dve.max(vals[0:n, c, 0:8], x[0:n, c, :])
                    link(dve, last)
                    for c in range(count):
                        dve.max_index(idx[0:n, c, 0:8], vals[0:n, c, 0:8], x[0:n, c, :])
                        last = dve.match_replace(y[0:n, c, :], vals[0:n, c, 0:8], x[0:n, c, :], LOW)
                    link(dve, last)
                    for c in range(count):
                        last = dve.max(vals[0:n, c, 8:16], y[0:n, c, :])
                    link(dve, last)
                    for c in range(count):
                        last = dve.max_index(idx[0:n, c, 8:16], vals[0:n, c, 8:16], y[0:n, c, :])
                    link(dve, last)

                for t, (a, n) in enumerate(parts):
                    dve.wait_ge(s_cp, t + 1)
                    top16(n, s, s2, sv, si, 16)
                    dve.tensor_copy(sf[0:n, :, :], si[0:n, :, :])
                    for h in range(8):
                        last = dve.tensor_tensor(cand[0:n, h, :].rearrange("p (i j) -> p i j", j=16),
                                                 sv[0:n, 2 * h, :].unsqueeze(2).broadcast_to([n, 16, 16]),
                                                 sv[0:n, 2 * h + 1, :].unsqueeze(1).broadcast_to([n, 16, 16]), ALU.add)
                    link(dve, last)
                    top16(n, cand, cand2, cv, ci, 8)
                    dve.tensor_tensor(res[0:n, 2, :].rearrange("p (h k) -> p h k", k=16), cv[0:n, :, :],
                                      cv[0:n, :, 0:1].broadcast_to([n, 8, 16]), ALU.subtract).then_inc(s_v, 1)
                    flat = ci[0:n, :, :].rearrange("p h k -> p (h k)")
                    dve.tensor_scalar(hl[0:n, 0, :], flat, 4, None, ALU.logical_shift_right)
                    link(dve, dve.tensor_scalar(hl[0:n, 1, :], flat, 15, None, ALU.bitwise_and))
                    link(dve, dve.tensor_copy(hf2[0:n, :, :], hl[0:n, :, :]))
                    for k in range(2):
                        link(dve, dve.tensor_tensor(hot[0:n, :, :], hf2[0:n, k, :].unsqueeze(2).broadcast_to([n, P, 16]),
                                                    cst("i16")[0:n, :].unsqueeze(1).broadcast_to([n, P, 16]), ALU.is_equal))
                        for h in range(8):
                            last = dve.tensor_tensor(hot[0:n, 16 * h:16 * h + 16, :], hot[0:n, 16 * h:16 * h + 16, :],
                                                     sf[0:n, 2 * h + k, :].unsqueeze(1).broadcast_to([n, 16, 16]), ALU.mult)
                        link(dve, last)
                        link(dve, dve.tensor_reduce(res[0:n, k, :], hot[0:n, :, :], AX, ALU.add))
                    dve.wait_ge(s_e, t + 1)
                    ex = res[0:n, 2, :].rearrange("p (h k) -> p h k", k=16)
                    link(dve, dve.tensor_reduce(z[0:n, :], ex, AX, ALU.add))
                    link(dve, dve.reciprocal(z[0:n, :], z[0:n, :]))
                    dve.tensor_tensor(ex, ex, z[0:n, :].unsqueeze(2).broadcast_to([n, 8, 16]), ALU.mult).then_inc(s_r, 1)
                    dve.wait_ge(s_tr, t + 1)
                    for k, dst in enumerate((iT, jT, gT)):
                        last = dve.tensor_copy(dst[:, a:a + n], ps[:, 4, k * P:k * P + n])
                    last.then_inc(s_ct, 1)
                    dve.wait_ge(s_ct, t + 1)


def spread(g, iT, jT, gT, H, xT, ring):
    nc, d, ps, sb, sem = g.nc, g.d, g.ps, g.sb, g.sem
    cst = g.cst
    GT = 4
    with ExitStack() as st:
        A0 = sb(st, "A0", [P, 2, GT, P])
        A = sb(st, "A", [P, 2, GT, P])
        B = sb(st, "B", [P, 2, GT, P])
        s_a0, s_a, s_b, s_mm, s_g = ([sem(f"{n}{k}") for k in range(2)] for n in (
            "hot_i", "gated_i", "hot_j", "gates_mm", "gates_used"))
        N = T // GT // 2
        io = cst("iota").unsqueeze(1).broadcast_to([P, GT, P])

        def col(x, i, k):
            return x[:, ds(i * (2 * GT) + k * GT, GT)].unsqueeze(2).broadcast_to([P, GT, P])

        g.credit(s_a + s_mm + s_g)
        s_res = sem("residual_in")
        with nc.Block() as block:
            @block.sync
            def _(sp):
                sp.dma_start(xT[:, :, :], d["residual"]).then_inc(s_res, 16)
                g.prime(sp, d["peer_v"], ring)
                sp.wait_ge(s_res, 16)

            @block.vector
            def _(dve):
                def hot(i, k):
                    dve.wait_ge(s_a[k], i + 1)
                    dve.tensor_tensor(A0[:, k, :, :], io, col(iT, i, k), ALU.is_equal).then_inc(s_a0[k], 1)
                    dve.wait_ge(s_mm[k], i + 1)
                    dve.tensor_tensor(B[:, k, :, :], io, col(jT, i, k), ALU.is_equal).then_inc(s_b[k], 1)

                def gate(i, k):
                    dve.wait_ge(s_mm[k], i + 2)
                    to = H[:, :, ds(i * (2 * GT) + k * GT, GT)]
                    dve.tensor_tensor(to, ps[:, k, :].rearrange("p (t j) -> p j t", t=GT), to, ALU.mult
                                      ).then_inc(s_g[k], 1)

                hot(0, 0)
                with dve.Fori(0, N - 1) as i:
                    hot(i, 1)
                    gate(i, 0)
                    hot(i + 1, 0)
                    gate(i, 1)
                hot(N - 1, 1)
                gate(N - 1, 0)
                gate(N - 1, 1)

            @block.gpsimd
            def _(pool):
                with pool.Fori(0, N) as i:
                    for k in range(2):
                        pool.wait_ge(s_a0[k], i + 1)
                        pool.wait_ge(s_mm[k], i + 1)
                        pool.tensor_tensor(A[:, k, :, :], A0[:, k, :, :], col(gT, i, k), ALU.mult).then_inc(s_a[k], 1)

            @block.tensor
            def _(pe):
                with pe.Fori(0, N) as i:
                    for k in range(2):
                        pe.wait_ge(s_a[k], i + 2)
                        pe.wait_ge(s_b[k], i + 1)
                        pe.wait_ge(s_g[k], i + 1)
                        for t in range(GT):
                            mm = pe.matmul(ps[:, k, t * P:(t + 1) * P], A[:, k, t, :], B[:, k, t, :],
                                           start=True, stop=True)
                        mm.then_inc(s_mm[k], 1)


def v_stage(g, xT, G, ring):
    nc, d, ps, sb, sem, link = g.nc, g.d, g.ps, g.sb, g.sem, g.link
    landed, used = g.landed, g.used
    N = P // 2 // RING
    with ExitStack() as st:
        zero = sb(st, "zero", [P, P])
        s_z, s_acc, s_add = sem("zero_made"), sem("half_summed"), sem("half_added")
        with nc.Block() as block:
            @block.sync
            def _(sp):
                for half in range(2):
                    r0 = g.rounds[0] + half * N
                    with sp.Fori(0 if half else 1, N) as i:
                        for k in range(RING):
                            sp.wait_ge(used[k], i + r0)
                            sp.dma_start(ring[:, k, :], d["peer_v"][ds(i * RING + (k + half * N * RING), 1), :, :]
                                         .rearrange("a p n -> p (a n)")).then_inc(landed[k], 16)

            @block.tensor
            def _(pe):
                pe.wait_ge(s_z, 1)
                for half in range(2):
                    r0 = g.rounds[0] + half * N
                    if half:
                        pe.wait_ge(s_add, 8)
                    for c in range(8):
                        pe.matmul(ps[:, c, 0:T], zero[:, :], xT[:, 0, :], start=True, stop=False)
                    with pe.Fori(0, N) as i:
                        for k in range(RING):
                            pe.wait_ge(landed[k], (i + r0) * 16)
                            for j in range(2):
                                h = G[:, ds(i * (2 * RING) + (2 * k + j), 1), :].rearrange("p a t -> p (a t)")
                                for c in range(8):
                                    mm = pe.matmul(ps[:, c, 0:T], ring[:, k, j * 1024 + c * P:j * 1024 + (c + 1) * P],
                                                   h, start=False, stop=False)
                            mm.then_inc(used[k], 1)
                    for c in range(8):
                        pe.matmul(ps[:, c, 0:T], zero[:, :], G[:, 0, :], start=False, stop=True).then_inc(s_acc, 1)

            @block.vector
            def _(dve):
                dve.memset(zero[:, :], 0.0).then_inc(s_z, 1)
                for half in range(2):
                    for c in range(8):
                        dve.wait_ge(s_acc, 8 * half + c + 1)
                        dve.tensor_tensor(xT[:, 8 * half + c, :], ps[:, c, 0:T], xT[:, 8 * half + c, :], ALU.add
                                          ).then_inc(s_add, 1)
        g.rounds[0] += 2 * N


def feature_major(x):
    t, f = x.shape
    return np.ascontiguousarray(x.reshape(t, f // P, P).transpose(2, 1, 0))


def tiles(w):
    k, n = w.shape
    return np.ascontiguousarray(w.reshape(k // P, P, n // P, P).transpose(2, 1, 0, 3).reshape(n // P, P, k))


def lay_out(i):
    i = {k: np.asarray(v) for k, v in i.items()}
    out = {"consts": constants()}
    rw = 3360
    order = np.arange(1024).reshape(2, 2, 4, 64).transpose(0, 2, 1, 3).reshape(-1)

    def chunks(v):
        return np.pad(v.reshape(-1), (0, -v.size % P)).reshape(-1, P).T

    out["vecs"] = np.ascontiguousarray(np.concatenate([chunks(v) for v in (
        i["norm_mix_g"], i["norm_x_g"], i["norm_ffn_g"], i["norm_f_g"], i["mem_norm_g"],
        i["nsa_norm_g"][order], i["rw_mu"], i["rw_w0"], i["rw_a0"], i["rw_k_k"], i["rw_k_a"], i["rw_r_k"],
        i["rw_lnx_g"], i["rw_lnx_b"], i["cmp_b1"])], 1))
    out["x"] = feature_major(np.concatenate([i["x_prompt"][0], i["x_sample"][:, 0]], 0))
    out["mem"] = feature_major(i["mem_prompt"][0])
    w = i["w_in"]
    wide = np.zeros((D, NCH * P), w.dtype)
    wide[:, :rw] = w[:, :rw]
    wide[:, C_Q * P:C_KC * P] = w[:, rw:rw + 1024][:, order]
    wide[:, C_KC * P:C_KC * P + 1584] = w[:, rw + 1024:]
    out["w_in"] = tiles(wide)
    out["w_out"] = tiles(np.concatenate([i["w_out"][:1024], i["w_out"][1024:][order]], 0))
    for n in ("xk", "xv"):
        out[n] = np.ascontiguousarray(i[n].reshape(KC, P, 512).transpose(1, 0, 2))
    out["shift"] = feature_major(np.pad(i["state_rwkv_shift"], ((0, 0), (0, RWC * P - rw))))
    out["wa2"] = np.concatenate([i["rw_w2"], i["rw_a2"]], 0)
    out["rw_g2"] = i["rw_g2"]
    out["wkv"] = np.ascontiguousarray(i["state_rwkv_wkv"].reshape(8, 8, 2, 4096).transpose(2, 0, 1, 3).reshape(P, 4096))
    out["win"] = np.ascontiguousarray(np.stack([i["cache_win_k"], i["cache_win_v"]], 0).reshape(2, 8, 512, 256))
    dup = i["cmp_w1"].transpose(2, 0, 1, 3)
    out["cmp_w1_twice"] = np.ascontiguousarray(np.concatenate([dup, dup], 0))
    out["cmp_w1"] = np.ascontiguousarray(i["cmp_w1"].reshape(2, 16, P, P).transpose(2, 0, 1, 3))
    out["cmp_w2"] = np.ascontiguousarray(i["cmp_w2"].transpose(1, 0, 2))
    pages = []
    for n in ("cmp_k", "cmp_v"):
        c = i[f"cache_{n}"].reshape(N_PHYS, 8, 8, 2, 4, 64)
        pages.append(c.transpose(0, 3, 5, 2, 4, 1).reshape(N_PHYS, P, 256))
    pages.append(i["cache_slc_k"].reshape(N_PHYS, P, 2, 2, 64).transpose(0, 3, 4, 2, 1).reshape(N_PHYS, P, 256))
    out["k_pages"] = np.concatenate(pages, 2)
    out["slc_v"] = i["cache_slc_v"].reshape(N_PHYS, P, 256)
    out["win_k"] = np.ascontiguousarray(i["cache_win_k"].reshape(8, 512, 2, 2, 64).transpose(3, 4, 0, 2, 1)
                                        .reshape(P, 8, 2, 512))
    out["win_v"] = np.ascontiguousarray(i["cache_win_v"].reshape(8, 4, P, 256).transpose(2, 0, 1, 3))
    out["page_table"] = i["page_table"].reshape(1, P)
    out["xq"] = tiles(i["xq"])
    out["mem_k"] = np.ascontiguousarray(i["cache_mem_k"].transpose(3, 0, 2, 1))
    out["mem_v"] = np.ascontiguousarray(i["cache_mem_v"].reshape(8, 2, P, 512).transpose(2, 0, 1, 3))
    out["xo"] = np.ascontiguousarray(i["xo"].reshape(4, P, D).transpose(1, 0, 2))
    out["peer_wq"] = tiles(i["peer_wq"])
    out["peer_keys"] = np.ascontiguousarray(i["peer_sub_keys"].reshape(16, P, P).transpose(2, 0, 1))
    out["peer_u"] = np.ascontiguousarray(i["peer_u"].reshape(P, P, KC, P).transpose(1, 3, 2, 0).reshape(P, P, D))
    out["peer_v"] = np.ascontiguousarray(i["peer_v"].reshape(P, 64, 2, 2, 1024).transpose(3, 1, 0, 2, 4)
                                         .reshape(P, P, D))
    return out


OUTS = {"o_y": (P, KC, T), "o_shift": (P, RWC, 9), "o_kv": (P, 12, T), "o_win": (2, 8, 511, 256),
        "o_memk": (P, 4, TP), "o_memv": (P, 2, 512), "o_pwkv": (P, 8, 64), "o_swkv": (P, 4096)}


def kernel(**inputs):
    import concourse.bacc as bacc
    from concourse.bass_utils import run_bass_kernel_spmd

    nc = bacc.Bacc("TRN2", target_bir_lowering=False, num_devices=1)
    arrays = lay_out(inputs)
    d = {n: nc.dram_tensor(f"in_{n}", a.shape, mybir.dt.from_np(a.dtype), kind="ExternalInput").ap()
         for n, a in arrays.items()}
    for n, s in OUTS.items():
        d[n] = nc.dram_tensor(n, s, F32, kind="ExternalOutput").ap()
    d["residual"] = nc.dram_tensor("residual", (P, KC, T), F32, kind="Internal").ap()
    build(nc, d)
    r = run_bass_kernel_spmd(nc, [{f"in_{n}": a for n, a in arrays.items()}], core_ids=[0]).results[0]

    y = r["o_y"].transpose(2, 1, 0).reshape(T, D)
    shift = r["o_shift"].transpose(2, 1, 0).reshape(9, RWC * P)[:, :3360]
    kv = r["o_kv"].transpose(2, 1, 0).reshape(T, 6, 4, 64)
    pk = [np.ascontiguousarray(kv[None, :TP, n]) for n in range(6)]
    sk = [np.ascontiguousarray(kv[TP:, None, n]) for n in range(6)]
    memk = r["o_memk"].transpose(2, 1, 0)[None]
    memv = r["o_memv"].transpose(1, 0, 2).reshape(1, TP, 4, P)
    pwkv = r["o_pwkv"].reshape(2, 64, 8, 64).transpose(2, 0, 3, 1).reshape(1, 16, 64, 64)
    swkv = r["o_swkv"].reshape(2, 8, 8, 64, 64).transpose(1, 2, 0, 3, 4).reshape(8, 16, 64, 64)
    win = [np.concatenate([r["o_win"][n].reshape(8, 511, 4, 64), sk[4 + n]], 1) for n in range(2)]
    out = (y[None, :TP], y[TP:, None], shift[:1], pwkv, *pk, memk, memv, shift[1:], swkv, *sk[:4], *win)
    return tuple(np.ascontiguousarray(a) for a in out)
```
